# Optimizing a Trainium2 kernel written in Bass

```python
import math
import jax, jax.numpy as jnp
from jax import lax
import numpy as np

D_MODEL = 1024
BATCH = 1
SEQ = 256
DEPTH = 2

N_MIXERS = 2
N_RWKV_LAYERS = (DEPTH + 1) // 2
N_DSA_LAYERS = DEPTH // 2
N_META = 16
D_FF = 2816
NORM_EPS = 1e-6
HEAD_DIM = 64
ROPE_DIM = HEAD_DIM // 4
ROPE_THETA = 500000.0
RWKV_HEADS = D_MODEL // HEAD_DIM
D_DECAY_LORA = 64
D_AAA_LORA = 64
D_GATE_LORA = 160
RWKV_LN_EPS = 64e-5
ATT_HEADS = D_MODEL // HEAD_DIM
ATT_KV_HEADS = 4
ATT_GROUP = ATT_HEADS // ATT_KV_HEADS
IDX_HEADS = 8
IDX_DIM = 64
TOPK_MAX = 256
Q_BLOCK = 128
ATT_Q_W = ATT_HEADS * HEAD_DIM
ATT_KV_W = ATT_KV_HEADS * HEAD_DIM
IDX_Q_W = IDX_HEADS * IDX_DIM
ATT_SPLITS = (ATT_Q_W, ATT_Q_W + ATT_KV_W, ATT_Q_W + 2 * ATT_KV_W,
              ATT_Q_W + 2 * ATT_KV_W + IDX_Q_W, ATT_Q_W + 2 * ATT_KV_W + IDX_Q_W + IDX_DIM)
ATT_IN_W = ATT_Q_W + 2 * ATT_KV_W + IDX_Q_W + IDX_DIM + IDX_HEADS


def rms_norm(x, g, eps=NORM_EPS):
    xf = x.astype(jnp.float32)
    y = xf * lax.rsqrt(jnp.mean(xf * xf, axis=-1, keepdims=True) + eps)
    return y.astype(x.dtype) * g

def swiglu(h, w_in, w_out):
    gate, up = jnp.split(h @ w_in, 2, axis=-1)
    return (jax.nn.silu(gate) * up) @ w_out

def rope_tables(n_pos, dtype):
    inv = ROPE_THETA ** (-jnp.arange(0, ROPE_DIM, 2, dtype=jnp.float32) / ROPE_DIM)
    ang = jnp.arange(n_pos, dtype=jnp.float32)[:, None] * inv[None, :]
    return jnp.cos(ang).astype(dtype), jnp.sin(ang).astype(dtype)

def partial_rope(x, cos, sin):
    half = ROPE_DIM // 2
    x1 = x[..., :half]
    x2 = x[..., half:ROPE_DIM]
    c = cos[None, :, None, :]
    s = sin[None, :, None, :]
    return jnp.concatenate([x1 * c - x2 * s, x2 * c + x1 * s, x[..., ROPE_DIM:]], axis=-1)

def wkv7_scan(r, w, k, v, a, b):
    B, T, H, N = r.shape
    xs = tuple(jnp.moveaxis(t.astype(jnp.float32), 1, 0) for t in (r, w, k, v, a, b))

    def step(S, inp):
        r_t, w_t, k_t, v_t, a_t, b_t = inp
        sa = jnp.einsum("bhij,bhj->bhi", S, a_t)
        S = S * w_t[:, :, None, :] + sa[..., None] * b_t[:, :, None, :] + v_t[..., None] * k_t[:, :, None, :]
        y = jnp.einsum("bhij,bhj->bhi", S, r_t)
        return S, y

    S0 = jnp.zeros((B, H, N, N), jnp.float32)
    _, ys = lax.scan(step, S0, xs)
    return jnp.moveaxis(ys, 0, 1).astype(r.dtype)

def rwkv7_time_mix(h, mix, w_r, w_k, w_v, w_o, w0, w1, w2, a0, a1, a2, g1, g2,
                   k_k, k_a, r_k, lnx_g, lnx_b):
    B, T, D = h.shape
    H, N = RWKV_HEADS, HEAD_DIM
    xx = jnp.pad(h, ((0, 0), (1, 0), (0, 0)))[:, :-1] - h
    xm = h[None] + xx[None] * mix[:, None, None, :]
    xr, xw, xk, xv, xa, xg = xm[0], xm[1], xm[2], xm[3], xm[4], xm[5]
    r = xr @ w_r
    k = xk @ w_k
    v = xv @ w_v
    w_log = -jax.nn.softplus(-(w0 + jnp.tanh(xw @ w1) @ w2)) - 0.5
    a = jax.nn.sigmoid(a0 + (xa @ a1) @ a2)
    g = jax.nn.sigmoid(xg @ g1) @ g2
    kk = (k * k_k).reshape(B, T, H, N).astype(jnp.float32)
    kk = (kk / jnp.maximum(jnp.sqrt(jnp.sum(kk * kk, axis=-1, keepdims=True)), 1e-12)).astype(h.dtype)
    k = k * (1.0 + (a - 1.0) * k_a)
    decay = jnp.exp(-jnp.exp(w_log.astype(jnp.float32)))
    rh = r.reshape(B, T, H, N)
    kh = k.reshape(B, T, H, N)
    vh = v.reshape(B, T, H, N)
    ah = a.reshape(B, T, H, N)
    y = wkv7_scan(rh, decay.reshape(B, T, H, N), kh, vh, -kk, kk * ah)
    yf = y.astype(jnp.float32)
    mu = jnp.mean(yf, axis=-1, keepdims=True)
    var = jnp.mean((yf - mu) ** 2, axis=-1, keepdims=True)
    yn = ((yf - mu) * lax.rsqrt(var + RWKV_LN_EPS)).astype(h.dtype).reshape(B, T, D) * lnx_g + lnx_b
    bonus = (jnp.sum(rh * kh * r_k, axis=-1, keepdims=True) * vh).reshape(B, T, D)
    return ((yn + bonus) * g) @ w_o

def dsa_attention(h, w_in, q_g, k_g, w_o, cos, sin, topk):
    B, T, D = h.shape
    q, k, v, qi, ki, wi = jnp.split(h @ w_in, ATT_SPLITS, axis=-1)
    q = partial_rope(rms_norm(q.reshape(B, T, ATT_HEADS, HEAD_DIM), q_g), cos, sin)
    k = partial_rope(rms_norm(k.reshape(B, T, ATT_KV_HEADS, HEAD_DIM), k_g), cos, sin)
    v = v.reshape(B, T, ATT_KV_HEADS, HEAD_DIM)
    qi = partial_rope(qi.reshape(B, T, IDX_HEADS, IDX_DIM), cos, sin)
    ki = partial_rope(ki[:, :, None, :], cos, sin)[:, :, 0, :]
    wi = wi * (IDX_HEADS ** -0.5 * IDX_DIM ** -0.5)

    n_blk = -(-T // Q_BLOCK)
    pad = n_blk * Q_BLOCK - T

    def to_blocks(t):
        t = jnp.pad(t, [(0, 0), (0, pad)] + [(0, 0)] * (t.ndim - 2))
        return jnp.moveaxis(t.reshape((B, n_blk, Q_BLOCK) + t.shape[2:]), 1, 0)

    starts = jnp.arange(n_blk, dtype=jnp.int32) * Q_BLOCK
    kpos = jnp.arange(T, dtype=jnp.int32)
    scale = HEAD_DIM ** -0.5

    def block(args):
        qb, qib, wib, start = args
        qpos = start + jnp.arange(Q_BLOCK, dtype=jnp.int32)
        rel = jax.nn.relu(jnp.einsum("bqhd,bkd->bqhk", qib, ki))
        score = jnp.einsum("bqh,bqhk->bqk", wib, rel).astype(jnp.float32)
        causal = kpos[None, :] <= qpos[:, None]
        score = jnp.where(causal[None], score, -jnp.inf)
        _, idx = lax.top_k(score, topk)
        valid = idx <= qpos[None, :, None]
        kg = jax.vmap(lambda kb, ib: kb[ib])(k, idx)
        vg = jax.vmap(lambda vb, ib: vb[ib])(v, idx)
        qg = qb.reshape(B, Q_BLOCK, ATT_KV_HEADS, ATT_GROUP, HEAD_DIM)
        logits = jnp.einsum("bqgrd,bqkgd->bqgrk", qg, kg).astype(jnp.float32) * scale
        logits = jnp.where(valid[:, :, None, None, :], logits, -jnp.inf)
        p = jax.nn.softmax(logits, axis=-1).astype(v.dtype)
        o = jnp.einsum("bqgrk,bqkgd->bqgrd", p, vg)
        return o.reshape(B, Q_BLOCK, ATT_Q_W)

    out = lax.map(block, (to_blocks(q), to_blocks(qi), to_blocks(wi), starts))
    out = jnp.moveaxis(out, 0, 1).reshape(B, n_blk * Q_BLOCK, ATT_Q_W)[:, :T]
    return out @ w_o

def first_inputs(seed: int = 0) -> dict:
    key = jax.random.key(seed)
    ks = jax.random.split(key, 32)
    f32 = jnp.float32

    def nrm(k, shape, scale):
        return jax.random.normal(k, shape, f32) * scale

    D = D_MODEL
    A = N_RWKV_LAYERS
    S = N_DSA_LAYERS
    return {
        "x": nrm(ks[0], (BATCH, SEQ, D), 1.0),
        "meta": nrm(ks[1], (N_META, D), 1.0),
        "norm_g": 1.0 + nrm(ks[2], (DEPTH, 3, D), 0.02),
        "ffn_w_in": nrm(ks[3], (DEPTH, 2, D, 2 * D_FF), D ** -0.5),
        "ffn_w_out": nrm(ks[4], (DEPTH, 2, D_FF, D), D_FF ** -0.5),
        "rk_mix": jax.random.uniform(ks[5], (A, 6, D), f32),
        "rk_w_r": nrm(ks[6], (A, D, D), D ** -0.5),
        "rk_w_k": nrm(ks[7], (A, D, D), D ** -0.5),
        "rk_w_v": nrm(ks[8], (A, D, D), D ** -0.5),
        "rk_w_o": nrm(ks[9], (A, D, D), D ** -0.5),
        "rk_w0": -0.6 + nrm(ks[10], (A, D), 0.3),
        "rk_w1": nrm(ks[11], (A, D, D_DECAY_LORA), D ** -0.5),
        "rk_w2": nrm(ks[12], (A, D_DECAY_LORA, D), 0.1 * D_DECAY_LORA ** -0.5),
        "rk_a0": nrm(ks[13], (A, D), 0.1),
        "rk_a1": nrm(ks[14], (A, D, D_AAA_LORA), D ** -0.5),
        "rk_a2": nrm(ks[15], (A, D_AAA_LORA, D), 0.1 * D_AAA_LORA ** -0.5),
        "rk_g1": nrm(ks[16], (A, D, D_GATE_LORA), D ** -0.5),
        "rk_g2": nrm(ks[17], (A, D_GATE_LORA, D), D_GATE_LORA ** -0.5),
        "rk_k_k": 0.85 + nrm(ks[18], (A, D), 0.05),
        "rk_k_a": 1.0 + nrm(ks[19], (A, D), 0.05),
        "rk_r_k": nrm(ks[20], (A, RWKV_HEADS, HEAD_DIM), 0.1),
        "rk_lnx_g": 1.0 + nrm(ks[21], (A, D), 0.02),
        "rk_lnx_b": nrm(ks[22], (A, D), 0.02),
        "at_w_in": nrm(ks[23], (S, D, ATT_IN_W), D ** -0.5),
        "at_q_g": 1.0 + nrm(ks[24], (S, HEAD_DIM), 0.02),
        "at_k_g": 1.0 + nrm(ks[25], (S, HEAD_DIM), 0.02),
        "at_w_o": nrm(ks[26], (S, ATT_Q_W, D), ATT_Q_W ** -0.5),
    }

def first_block(x, meta, norm_g, ffn_w_in, ffn_w_out, rk_mix, rk_w_r, rk_w_k, rk_w_v, rk_w_o,
              rk_w0, rk_w1, rk_w2, rk_a0, rk_a1, rk_a2, rk_g1, rk_g2, rk_k_k, rk_k_a, rk_r_k,
              rk_lnx_g, rk_lnx_b, at_w_in, at_q_g, at_k_g, at_w_o):
    B, L, D = x.shape
    topk = min(TOPK_MAX, L // 4)
    h = jnp.concatenate([jnp.broadcast_to(meta.astype(x.dtype)[None], (B, N_META, D)), x], axis=1)
    T = h.shape[1]
    cos, sin = rope_tables(T, x.dtype)
    for i in range(DEPTH):
        g = norm_g[i]
        h = h + 0.5 * swiglu(rms_norm(h, g[0]), ffn_w_in[i, 0], ffn_w_out[i, 0])
        hn = rms_norm(h, g[1])
        j = i // N_MIXERS
        if i % N_MIXERS == 0:
            h = h + rwkv7_time_mix(hn, rk_mix[j], rk_w_r[j], rk_w_k[j], rk_w_v[j], rk_w_o[j],
                                   rk_w0[j], rk_w1[j], rk_w2[j], rk_a0[j], rk_a1[j], rk_a2[j],
                                   rk_g1[j], rk_g2[j], rk_k_k[j], rk_k_a[j], rk_r_k[j],
                                   rk_lnx_g[j], rk_lnx_b[j])
        else:
            h = h + dsa_attention(hn, at_w_in[j], at_q_g[j], at_k_g[j], at_w_o[j], cos, sin, topk)
        h = h + 0.5 * swiglu(rms_norm(h, g[2]), ffn_w_in[i, 1], ffn_w_out[i, 1])
    return h[:, N_META:]


DEPTH_2 = 1

HEAD_DIM_A = 64
N_HEADS_A = 8
WIDTH_A = N_HEADS_A * HEAD_DIM_A
DILATED_BRANCHES = ((128, 1), (512, 4), (2048, 16))

N_HEADS_B = 8
QK_NOPE_DIM = 64
QK_ROPE_DIM = 32
V_HEAD_DIM = 64
QK_HEAD_DIM_B = QK_NOPE_DIM + QK_ROPE_DIM
Q_LORA_RANK = 768
KV_LORA_RANK = 256
WIDTH_B = N_HEADS_B * V_HEAD_DIM
ROPE_THETA_2 = 10000.0

MIX_WIDTH = WIDTH_A + WIDTH_B
D_FF_2 = 4 * D_MODEL

REL_BUCKETS = 32
REL_MAX_DIST = 2048
EPS = 1e-6

IN_SPLITS = (WIDTH_A, WIDTH_A, WIDTH_A, Q_LORA_RANK, KV_LORA_RANK, QK_ROPE_DIM)
IN_WIDTH = sum(IN_SPLITS)


def rms_norm_2(x, g):
    xf = x.astype(jnp.float32)
    y = xf * lax.rsqrt(jnp.mean(xf * xf, axis=-1, keepdims=True) + EPS)
    return (y * g.astype(jnp.float32)).astype(x.dtype)

def t5_causal_bucket(dist):
    dist = np.asarray(dist, dtype=np.int64)
    max_exact = REL_BUCKETS // 2
    safe = np.maximum(dist, 1).astype(np.float32)
    large = max_exact + (np.log(safe / max_exact) / math.log(REL_MAX_DIST / max_exact)
                         * (REL_BUCKETS - max_exact)).astype(np.int64)
    large = np.minimum(large, REL_BUCKETS - 1)
    return np.where(dist < max_exact, dist, large).astype(np.int32)

def apply_rope(x, positions):
    r = x.shape[-1]
    inv_freq = 1.0 / (ROPE_THETA_2 ** (jnp.arange(0, r, 2, dtype=jnp.float32) / r))
    ang = positions.astype(jnp.float32)[..., None] * inv_freq
    cos = jnp.cos(ang)[:, :, None, :]
    sin = jnp.sin(ang)[:, :, None, :]
    xf = x.astype(jnp.float32)
    x1, x2 = xf[..., : r // 2], xf[..., r // 2:]
    out = jnp.concatenate([x1 * cos - x2 * sin, x2 * cos + x1 * sin], axis=-1)
    return out.astype(x.dtype)

def to_query_blocks(t):
    b, s = t.shape[:2]
    nblk = s // Q_BLOCK
    return jnp.moveaxis(t.reshape((b, nblk, Q_BLOCK) + t.shape[2:]), 1, 0)

def from_query_blocks(t):
    t = jnp.moveaxis(t, 0, 1)
    return t.reshape((t.shape[0], t.shape[1] * t.shape[2]) + t.shape[3:])

def dilated_attention(q, k, v, rel_bias):
    b, s, h, dh = q.shape
    scale = 1.0 / math.sqrt(dh)
    branches = []
    for window, dil in DILATED_BRANCHES:
        offs_np = dil * np.arange(window // dil + 1, dtype=np.int32)
        bias = rel_bias[jnp.asarray(t5_causal_bucket(offs_np))].T.astype(jnp.float32)
        branches.append((jnp.asarray(offs_np), bias))
    nblk = s // Q_BLOCK

    def block_fn(args):
        i, qi = args
        tq = i * Q_BLOCK + jnp.arange(Q_BLOCK, dtype=jnp.int32)
        ms, ss, os_ = [], [], []
        for offs, bias in branches:
            idx = tq[:, None] - offs[None, :]
            valid = idx >= 0
            idxc = jnp.maximum(idx, 0)
            kg = k[:, idxc]
            vg = v[:, idxc]
            logits = jnp.einsum('bqhd,bqkhd->bhqk', qi, kg).astype(jnp.float32) * scale
            logits = logits + bias[None, :, None, :]
            logits = jnp.where(valid[None, None], logits, -jnp.inf)
            m = jnp.max(logits, axis=-1, keepdims=True)
            p = jnp.exp(logits - m)
            den = jnp.sum(p, axis=-1, keepdims=True)
            o = jnp.einsum('bhqk,bqkhd->bhqd', p, vg.astype(jnp.float32)) / den
            ms.append(m); ss.append(den); os_.append(o)
        m_all = jnp.stack(ms)
        w = jnp.stack(ss) * jnp.exp(m_all - jnp.max(m_all, axis=0, keepdims=True))
        out = jnp.sum(w * jnp.stack(os_), axis=0) / jnp.sum(w, axis=0)
        return jnp.transpose(out, (0, 2, 1, 3)).astype(q.dtype)

    out = lax.map(block_fn, (jnp.arange(nblk, dtype=jnp.int32), to_query_blocks(q)))
    return from_query_blocks(out)

def causal_block_attention(q, k, v):
    b, s, h, dqk = q.shape
    scale = 1.0 / math.sqrt(dqk)
    kpos = jnp.arange(s, dtype=jnp.int32)
    nblk = s // Q_BLOCK

    def block_fn(args):
        i, qi = args
        tq = i * Q_BLOCK + jnp.arange(Q_BLOCK, dtype=jnp.int32)
        logits = jnp.einsum('bqhd,bkhd->bhqk', qi, k).astype(jnp.float32) * scale
        logits = jnp.where((kpos[None, :] <= tq[:, None])[None, None], logits, -jnp.inf)
        p = jax.nn.softmax(logits, axis=-1)
        out = jnp.einsum('bhqk,bkhd->bqhd', p, v.astype(jnp.float32))
        return out.astype(q.dtype)

    out = lax.map(block_fn, (jnp.arange(nblk, dtype=jnp.int32), to_query_blocks(q)))
    return from_query_blocks(out)

def second_inputs(seed: int = 0) -> dict:
    key = jax.random.key(seed)
    ks = jax.random.split(key, 20)
    f32 = jnp.float32

    def nrm(k, shape, fan_in):
        return jax.random.normal(k, shape, f32) * (fan_in ** -0.5)

    def gain(k, n):
        return 1.0 + 0.05 * jax.random.normal(k, (n,), f32)

    x = jax.random.normal(ks[0], (BATCH, SEQ, D_MODEL), f32)
    offset = jax.random.randint(ks[1], (BATCH, 1), 0, 1024, dtype=jnp.int32)
    positions = jnp.arange(SEQ, dtype=jnp.int32)[None, :] + offset
    return {
        "x": x,
        "positions": positions,
        "norm_mix_g": gain(ks[2], D_MODEL),
        "w_in": nrm(ks[3], (D_MODEL, IN_WIDTH), D_MODEL),
        "qnorm_a_g": gain(ks[4], HEAD_DIM_A),
        "knorm_a_g": gain(ks[5], HEAD_DIM_A),
        "rel_bias": 0.5 * jax.random.normal(ks[6], (REL_BUCKETS, N_HEADS_A), f32),
        "cq_norm_g": gain(ks[7], Q_LORA_RANK),
        "ckv_norm_g": gain(ks[8], KV_LORA_RANK),
        "w_uq": nrm(ks[9], (Q_LORA_RANK, N_HEADS_B * QK_HEAD_DIM_B), Q_LORA_RANK),
        "w_ukv": nrm(ks[10], (KV_LORA_RANK, N_HEADS_B * (QK_NOPE_DIM + V_HEAD_DIM)), KV_LORA_RANK),
        "qnorm_b_g": gain(ks[11], QK_HEAD_DIM_B),
        "knorm_b_g": gain(ks[12], QK_HEAD_DIM_B),
        "w_o": nrm(ks[13], (MIX_WIDTH, D_MODEL), MIX_WIDTH),
        "norm_ffn_g": gain(ks[14], D_MODEL),
        "w_ff1": nrm(ks[15], (D_MODEL, D_FF_2), D_MODEL),
        "w_ff2": nrm(ks[16], (D_FF_2, D_MODEL), D_FF_2),
    }

def second_block(x, positions, norm_mix_g, w_in, qnorm_a_g, knorm_a_g, rel_bias,
              cq_norm_g, ckv_norm_g, w_uq, w_ukv, qnorm_b_g, knorm_b_g, w_o,
              norm_ffn_g, w_ff1, w_ff2):
    b, s, _ = x.shape
    h = x
    for _layer in range(DEPTH_2):
        xn = rms_norm_2(h, norm_mix_g)
        proj = jnp.einsum('bsd,de->bse', xn, w_in)
        cuts = list(np.cumsum(IN_SPLITS)[:-1])
        qa, ka, va, c_q, c_kv, k_rope = jnp.split(proj, cuts, axis=-1)

        qa = rms_norm_2(qa.reshape(b, s, N_HEADS_A, HEAD_DIM_A), qnorm_a_g)
        ka = rms_norm_2(ka.reshape(b, s, N_HEADS_A, HEAD_DIM_A), knorm_a_g)
        va = va.reshape(b, s, N_HEADS_A, HEAD_DIM_A)
        out_a = dilated_attention(qa, ka, va, rel_bias).reshape(b, s, WIDTH_A)

        qb = jnp.einsum('bsr,re->bse', rms_norm_2(c_q, cq_norm_g), w_uq)
        qb = qb.reshape(b, s, N_HEADS_B, QK_HEAD_DIM_B)
        kv = jnp.einsum('bsr,re->bse', rms_norm_2(c_kv, ckv_norm_g), w_ukv)
        kv = kv.reshape(b, s, N_HEADS_B, QK_NOPE_DIM + V_HEAD_DIM)
        k_nope, vb = kv[..., :QK_NOPE_DIM], kv[..., QK_NOPE_DIM:]
        k_rope_h = jnp.broadcast_to(k_rope[:, :, None, :], (b, s, N_HEADS_B, QK_ROPE_DIM))
        kb = jnp.concatenate([k_nope, k_rope_h], axis=-1)
        qb = rms_norm_2(qb, qnorm_b_g)
        kb = rms_norm_2(kb, knorm_b_g)
        qb = jnp.concatenate([qb[..., :QK_NOPE_DIM],
                              apply_rope(qb[..., QK_NOPE_DIM:], positions)], axis=-1)
        kb = jnp.concatenate([kb[..., :QK_NOPE_DIM],
                              apply_rope(kb[..., QK_NOPE_DIM:], positions)], axis=-1)
        out_b = causal_block_attention(qb, kb, vb).reshape(b, s, WIDTH_B)

        mixed = jnp.concatenate([out_a, out_b], axis=-1)
        h = h + jnp.einsum('bse,ed->bsd', mixed, w_o)

        hn = rms_norm_2(h, norm_ffn_g)
        hid = jnp.square(jax.nn.relu(jnp.einsum('bsd,df->bsf', hn, w_ff1)))
        h = h + jnp.einsum('bsf,fd->bsd', hid, w_ff2)
    return h


def setup_inputs(seed=0):
    out = dict(first_inputs(seed))
    for name, value in second_inputs(seed + 1).items():
        if name != "x":
            out[name + "_2"] = value
    return out


def reference(
    x, meta, norm_g, ffn_w_in, ffn_w_out, rk_mix, rk_w_r, rk_w_k, rk_w_v, rk_w_o, rk_w0, rk_w1,
    rk_w2, rk_a0, rk_a1, rk_a2, rk_g1, rk_g2, rk_k_k, rk_k_a, rk_r_k, rk_lnx_g, rk_lnx_b,
    at_w_in, at_q_g, at_k_g, at_w_o, positions_2, norm_mix_g_2, w_in_2, qnorm_a_g_2,
    knorm_a_g_2, rel_bias_2, cq_norm_g_2, ckv_norm_g_2, w_uq_2, w_ukv_2, qnorm_b_g_2,
    knorm_b_g_2, w_o_2, norm_ffn_g_2, w_ff1_2, w_ff2_2,
):
    x = first_block(
        x, meta, norm_g, ffn_w_in, ffn_w_out, rk_mix, rk_w_r, rk_w_k, rk_w_v, rk_w_o, rk_w0,
        rk_w1, rk_w2, rk_a0, rk_a1, rk_a2, rk_g1, rk_g2, rk_k_k, rk_k_a, rk_r_k, rk_lnx_g,
        rk_lnx_b, at_w_in, at_q_g, at_k_g, at_w_o,
    )
    return second_block(
        x, positions_2, norm_mix_g_2, w_in_2, qnorm_a_g_2, knorm_a_g_2, rel_bias_2, cq_norm_g_2,
        ckv_norm_g_2, w_uq_2, w_ukv_2, qnorm_b_g_2, knorm_b_g_2, w_o_2, norm_ffn_g_2, w_ff1_2,
        w_ff2_2,
    )


_drawn_inputs = setup_inputs


def setup_inputs(seed=0):
    import zlib

    import numpy as np

    out = dict(_drawn_inputs(seed))
    spreads = {}
    factors = {'rk_w1': 3.436,
     'rk_w2': 3.603,
     'rk_k_k': 3.227,
     'rk_lnx_g': 2.735,
     'at_q_g': 8.0,
     'at_k_g': 8.0,
     'norm_mix_g_2': 3.861,
     'qnorm_a_g_2': 8.0,
     'knorm_a_g_2': 7.873,
     'cq_norm_g_2': 8.0,
     'ckv_norm_g_2': 7.044,
     'qnorm_b_g_2': 8.0,
     'knorm_b_g_2': 8.0,
     'norm_ffn_g_2': 4.856}
    for name, (base, spread) in spreads.items():
        noise = np.random.default_rng([zlib.crc32(name.encode()), seed]).standard_normal(out[name].shape)
        drawn = base * np.exp(spread * noise) if base else spread * noise
        out[name] = __import__('jax').numpy.asarray(drawn.astype(out[name].dtype))
    for name, factor in factors.items():
        out[name] = (out[name] * factor).astype(out[name].dtype)
    return out
```

```python
import math
from contextlib import ExitStack, contextmanager

import numpy as np

import concourse.bass as bass
from concourse import mybir

F32 = mybir.dt.float32
F32R = mybir.dt.float32r
I32 = mybir.dt.int32
ALU = mybir.AluOpType
ACT = mybir.ActivationFunctionType
AX = mybir.AxisListType

D = 1024
KC = D // 128
META = 16
SEQ = 256
T = META + SEQ
FF = 2816
FC = FF // 128
FF2 = 4096
HD = 64
EPS = 1e-6
LN_EPS = 64e-5
H_A = 16
TOPK = 64
BLK = 96
CH = 32
NCH = 9
NB = 3
TP = NB * BLK
NEG = -1.0e30
CAP = 3.0e38
TAKEN = -3.4e38

STAGES = [
    ("f0_in", 22, 22, 2048), ("f0_dn", 16, 8, 1408),
    ("rk_r", 4, 4, 2048), ("rk_k", 4, 4, 2048), ("rk_v", 4, 4, 2048),
    ("lora_wa", 1, 1, 1024), ("lora_g", 1, 1, 1280), ("wa2", 1, 8, 1024),
    ("g2", 1, 4, 2048), ("rk_o", 4, 4, 2048),
    ("f1_in", 22, 22, 2048), ("f1_dn", 16, 8, 1408),
    ("f2_in", 22, 22, 2048), ("f2_dn", 16, 8, 1408),
    ("at_q", 4, 4, 2048), ("at_k", 2, 2, 2048), ("at_qi", 2, 2, 2048), ("at_tail", 1, 1, 2048),
    ("at_v", 1, 1, 2048), ("at_o", 4, 4, 2048),
    ("f3_in", 22, 22, 2048), ("f3_dn", 16, 8, 1408),
    ("b_qa", 2, 2, 2048), ("b_ka", 2, 2, 2048), ("b_va", 2, 2, 2048), ("b_cq", 3, 3, 2048),
    ("b_ckv", 1, 1, 2048), ("b_tail", 1, 1, 1024), ("b_uq", 4, 4, 1152), ("b_ukv", 1, 3, 2048),
    ("b_o", 4, 4, 2048), ("b_ff1", 16, 16, 2048), ("b_ff2", 16, 8, 2048),
]
U0, G0, UN, GN, UW = {}, {}, {}, {}, {}
_u = _g = 0
for _name, _n, _m, _w in STAGES:
    U0[_name], G0[_name], UN[_name], GN[_name], UW[_name] = _u, _g, _n, _m, _w
    _u += _n
    _g += _m
UNITS = _u

RAW = 4
SPL = 2


def halves(w):
    cut = 1024 if w > 1024 else w // 2
    return (slice(0, cut), slice(cut, w))

VEC = {}
_c = 0
for _name, _n in [("norm_g", 48), ("rk_mix", 48), ("w0", 8), ("a0", 8), ("k_k", 8), ("k_a", 8),
                  ("r_k", 8), ("lnx_g", 8), ("lnx_b", 8), ("norm_mix", 8), ("norm_ffn", 8),
                  ("cq_g", 6), ("ckv_g", 2), ("q_g", 1), ("k_g", 1), ("qa_g", 1), ("ka_g", 1),
                  ("qb_g", 1), ("kb_g", 1)]:
    VEC[_name] = _c
    _c += _n
NVEC = _c

LEVELS = (2, 4, 8, 16)


def norm_col(layer, which):
    return VEC["norm_g"] + (layer * 3 + which) * KC


def shape_constants():
    c = {}
    c["ident"] = np.eye(128, dtype=np.float32)
    c["ones"] = np.ones((128, 128), np.float32)
    half = np.arange(128) // 64
    c["bo64"] = (half[:, None] == half[None, :]).astype(np.float32)
    s = np.arange(BLK)
    same = (s[:, None] // CH) == (s[None, :] // CH)
    strict_t = same & (s[:, None] < s[None, :])
    m = [strict_t, strict_t.T, same & (s[:, None] <= s[None, :])]
    lvl = []
    for size in (1,) + LEVELS:
        lo = (s[:, None] // (2 * size) == s[None, :] // (2 * size)) & \
             (s[:, None] // size % 2 == 1) & (s[None, :] // size % 2 == 0)
        lvl.append(lo)
    m += [lvl[0], lvl[0].T] + [x.T for x in lvl[1:]] + [np.eye(BLK, dtype=bool)]
    scan = np.stack([x.astype(np.float32) for x in m], 1)
    c["scan"] = np.zeros((128, 10 * BLK), np.float32)
    c["scan"][:BLK] = scan.reshape(BLK, -1)
    rot = np.zeros((128, 128), np.float32)
    for b in (0, 64):
        for i in range(8):
            rot[b + i + 8, b + i] = 1.0
            rot[b + i, b + i + 8] = 1.0
    c["rot_a"] = rot
    inv = (np.float32(500000.0) ** (-np.arange(0, 16, 2, dtype=np.float32) / np.float32(16))).astype(np.float32)
    ang = np.arange(T, dtype=np.float32)[:, None] * inv[None, :]
    cs, sn = np.cos(ang).astype(np.float32).T, np.sin(ang).astype(np.float32).T
    ct, st = np.ones((128, T), np.float32), np.zeros((128, T), np.float32)
    for b in (0, 64):
        ct[b:b + 8] = cs
        ct[b + 8:b + 16] = cs
        st[b:b + 8] = -sn
        st[b + 8:b + 16] = sn
    c["cs_a"] = np.concatenate([ct, st], 1)
    cap = np.full((128, 2, T), CAP, np.float32)
    for b in range(2):
        q = META + 128 * b + np.arange(128)
        cap[:, b][np.arange(T)[None, :] > q[:, None]] = -CAP
    c["cap"] = cap.reshape(128, 2 * T)
    rb = np.zeros((128, 96), np.float32)
    for i in range(16):
        rb[64 + i + 16, 64 + i] = 1.0
        rb[64 + i, 64 + i + 16] = 1.0
    c["rot_b"] = rb
    invb = (np.float32(1.0) / (np.float32(10000.0) ** (np.arange(0, 32, 2, dtype=np.float32) / np.float32(32)))).astype(np.float32)
    fr = np.zeros((128, 2), np.float32)
    fr[64:80, 0] = invb
    fr[80:96, 0] = invb
    fr[64:80, 1] = -1.0
    fr[80:96, 1] = 1.0
    c["freq"] = fr
    k = np.arange(256)[None, :] - 128 - np.arange(128)[:, None]
    c["causal"] = np.where(k > 0, np.float32(NEG), np.float32(0)).astype(np.float32)
    dist = 255 - np.arange(384)
    safe = np.maximum(np.maximum(dist, 0), 1).astype(np.float32)
    large = 16 + (np.log(safe / 16) / math.log(2048 / 16) * 16).astype(np.int64)
    large = np.minimum(large, 31)
    bucket = np.where(np.maximum(dist, 0) < 16, np.maximum(dist, 0), large)
    oh = np.zeros((33, 384), np.float32)
    oh[bucket, np.arange(384)] = 8.0
    times = (dist <= 128).astype(int) + (dist % 4 == 0) + (dist % 16 == 0)
    oh[32] = np.where((dist >= 0) & (times > 0), 8.0 * np.log(np.maximum(times, 1)), NEG)
    c["dist"] = oh
    return c


class Link:

    def __init__(self, eng, sem):
        self.eng, self.sem, self.n, self.i, self.per = eng, sem, 0, None, 0

    def value(self):
        return self.n if self.i is None else self.i * self.per + self.n

    def do(self, ins):
        ins.then_inc(self.sem, 1)
        self.n += 1

    def sync(self):
        self.eng.wait_ge(self.sem, self.value())

    def __call__(self, ins):
        self.do(ins)
        self.sync()

    @contextmanager
    def loop(self, times, per):
        first = self.n
        with self.eng.Fori(0, times) as i:
            self.i, self.per = i, per
            yield i
            assert self.n - first == per, f"steps {self.n - first}, not {per}"
        self.i = None
        self.n = first + per * times


def val(c, i, k):
    return c if i is None else i * k + c


def turns(link, n, per, steps, body, at_least=0):
    peel = n % per
    while peel < at_least:
        peel += per
    if peel:
        body(range(peel), None)
    if n - peel == per:
        body(range(peel, n), None)
    elif n > peel:
        with link.loop((n - peel) // per, steps) as i:
            body(range(peel, peel + per), i)



SPLITS = [("f0", 8), ("m0", 8), ("m1", 8), ("m2", 8), ("m3", 8), ("m4", 8), ("m5", 8), ("ro", 8),
          ("f1", 8), ("f2", 8), ("at", 8), ("f3", 8), ("b", 8), ("cq", 6), ("ckv", 2), ("ff", 8)]
X0, XM0 = {}, {}
_x = _m = 0
for _name, _n in SPLITS:
    X0[_name], XM0[_name] = _x, _m
    _x += _n
    _m += 0 if _name == "ro" else _n
NORMS = [("f0", 8), ("rk", 8), ("f1", 4), ("f2", 8), ("at", 8), ("f3", 4), ("b", 8), ("ff", 4)]
Q0, N0 = {}, {}
_q = 0
for _i, (_name, _n) in enumerate(NORMS):
    Q0[_name], N0[_name] = _q, _i
    _q += _n


def build(nc, t):
    ctx = ExitStack()
    with ctx:
        used = [0]

        class Region:

            def __init__(self, start):
                self.here = start

            def __call__(self, name, shape, dtype=F32):
                size = 4 * int(np.prod(shape[1:]))
                x = nc.alloc_sbuf_tensor_at(name, shape, dtype, offset=self.here)
                self.here += (size + 31) // 32 * 32
                used[0] = max(used[0], self.here)
                return x

        def sem(name):
            return ctx.enter_context(nc.semaphore(name))

        keep = Region((nc.sbuf_base + 63) // 32 * 32)
        raw = [keep(f"raw{i}", [128, 2048]) for i in range(RAW)]
        whi = [keep(f"whi{i}", [128, 2048], F32R) for i in range(SPL)]
        wlo = [keep(f"wlo{i}", [128, 2048], F32R) for i in range(SPL)]
        h = keep("h", [128, KC, T])
        ident = keep("ident", [128, 128])
        ones = keep("ones", [128, 128])
        bo64 = keep("bo64", [128, 128])
        vec = keep("vec", [128, NVEC])
        ss = keep("ss", [128, T])
        rstd = keep("rstd", [128, T])
        epsc = keep("epsc", [128, 2])

        arena = keep.here
        xr = Region(arena)
        xh, xl = [None, None], [None, None]
        xh[0] = xr("xh0", [128, KC, T], F32R)
        xl[0] = xr("xl0", [128, KC, T], F32R)
        after_x0 = xr.here
        xh[1] = xr("xh1", [128, KC, T], F32R)
        xl[1] = xr("xl1", [128, KC, T], F32R)
        after_x1 = xr.here

        ff = Region(after_x0)
        hid_h = ff("hid_h", [128, FC * T], F32R)
        hid_l = ff("hid_l", [128, FC * T], F32R)
        gate = ff("gate", [128, 2, T])
        upg = ff("upg", [128, 2, T])
        sig = ff("sig", [128, 2, T])
        hidf = ff("hidf", [128, 2, T])
        sq = ff("sq", [128, 2, 2, T])
        xg = ff("xg", [128, 2, 2, T])
        ff = Region(after_x0)
        hid2_h = ff("hid2_h", [128, 32 * SEQ], F32R)
        hid2_l = ff("hid2_l", [128, 32 * SEQ], F32R)
        act2 = ff("act2", [128, 2, 2, SEQ])
        hidf2 = ff("hidf2", [128, 2, 2, SEQ])
        outt = ff("outt", [128, KC, SEQ])

        rk = Region(after_x1)
        hn = rk("hn", [128, KC, T])
        xx = rk("xx", [128, KC, T])
        rk.here = after_x1 + 2 * 4 * KC * TP
        a_g = rk("a_g", [128, KC, T])
        head_end = rk.here
        lh = rk("lh", [128, T])
        lh_h = rk("lh_h", [128, T], F32R)
        lh_l = rk("lh_l", [128, T], F32R)
        gh = rk("gh", [80, 2, T])
        gh_h = rk("gh_h", [80, 2, T], F32R)
        gh_l = rk("gh_l", [80, 2, T], F32R)
        wend = rk("wend", [128, KC, NCH])
        first = rk("first", [128, KC, NCH])
        R_ = rk("R_", [128, KC, TP])
        K_ = rk("K_", [128, KC, TP])
        V_ = rk("V_", [128, KC, TP])
        A_ = rk("A_", [128, KC, TP])
        B_ = rk("B_", [128, KC, TP])
        w_at = rk.here
        W_ = rk("W_", [128, KC, TP])
        masks = rk("masks", [128, 10, BLK])
        r2 = Region(w_at)
        xmf = r2("xmf", [128, KC, T])
        bonus = Region(w_at)("bonus", [128, KC, T])
        r2 = Region(after_x1)
        wst = r2("wst", [128, KC, TP])
        Wc = r2("Wc", [128, KC, TP])
        ktmp = Region(after_x0)("ktmp", [128, KC, TP])
        kden = Region(arena)("kden", [128, KC, T])
        sc = Region(arena)
        U_ = sc("U_", [96, NB, 512])
        mrb = sc("mrb", [96, 8, TP])
        btok = sc("btok", [96, NB, 512])
        GV = sc("GV", [128, NCH, 256])
        L_ = [sc(f"L{e}", [96, TP]) for e in range(2)]
        LT = [sc(f"LT{e}", [96, TP]) for e in range(2)]
        LM = [sc(f"LM{e}", [96, TP]) for e in range(2)]
        XX = [sc(f"XX{e}", [96, TP]) for e in range(2)]
        XT = [sc(f"XT{e}", [96, TP]) for e in range(2)]
        QQ = [sc(f"QQ{e}", [96, TP]) for e in range(2)]
        lak = [sc(f"lak{e}", [96, TP]) for e in range(2)]
        mrk = [sc(f"mrk{e}", [96, TP]) for e in range(2)]
        atok = sc("atok", [96, NB, 128])
        ktok = sc("ktok", [96, NB, 128])
        vtok = sc("vtok", [96, NB, 128])
        p1 = sc("p1", [96, NB, 128])
        bh = sc("bh", [128, TP])
        kh = sc("kh", [128, TP])
        S_ = [sc(f"S{e}", [128, 256]) for e in range(2)]
        St = sc("St", [128, 256])
        assert sc.here <= head_end, (sc.here, head_end)

        ds_ = Region(after_x1)
        rawq = ds_("rawq", [128, 18, T])
        vt = ds_("vt", [96, NB, 256])
        rot_a = ds_("rot_a", [128, 128])
        cs_a = ds_("cs_a", [128, 2, T])
        cap = ds_("cap", [128, 2, T])
        wit = ds_("wit", [128, 2, 8])
        rel = ds_("rel", [128, 2, T])
        score = ds_("score", [128, 2, T])
        taken = [ds_(f"taken{i}", [128, 2, T]) for i in range(2)]
        m8 = ds_("m8", [128, 8])
        at_in = Region(after_x0)("at_in", [128, KC, T])
        b2 = Region(after_x1)
        b_in = Region(after_x0)("b_in", [128, KC, SEQ])
        qka = b2("qka", [128, 8, SEQ])
        vat = b2("vat", [128, 2, 512])
        craw = b2("craw", [128, 8, SEQ])
        krope = b2("krope", [128, SEQ])
        cxf_at = b2.here
        qkb = b2("qkb", [96, 16, SEQ])
        vbt = b2("vbt", [128, 2, 512])
        bias = b2("bias", [128, 8, 256])
        causal = b2("causal", [128, 256])
        rot_b = b2("rot_b", [128, 96])
        cs_b = b2("cs_b", [128, 2, SEQ])
        posi = b2("posi", [128, SEQ], I32)
        posf = b2("posf", [128, SEQ])
        ang = b2("ang", [128, SEQ])
        red = b2("red", [128, SEQ])
        freq = b2("freq", [128, 2])
        distt = b2("distt", [33, 384])
        relb = b2("relb", [33, 8, 128])
        bt = b2("bt", [128, 2, SEQ])
        cvr = b2("cvr", [128, 2, SEQ])
        csq = Region(cxf_at + 4 * 8 * SEQ)("csq", [128, 8, SEQ])
        cxf = Region(cxf_at)("cxf", [128, 8, SEQ])
        attn_at = max(ds_.here, b2.here)
        an = Region(attn_at)
        biasw = Region(attn_at)("biasw", [128, 8, 384])
        lg = an("lg", [128, 2, T])
        pr = an("pr", [128, 3, T])
        prn = an("prn", [128, 2, T])
        pts = an("pts", [128, 2, 3, 128])
        amx = an("amx", [128, 64])
        nmx = an("nmx", [128, 64])
        asum = an("asum", [128, 64])
        ainv = an("ainv", [128, 64])

        sqp = [an(f"sqp{i}", [128, 2, T]) for i in range(2)]
        hvr = [an(f"hvr{i}", [128, 2, T]) for i in range(2)]
        rtt = an("rtt", [128, 2, T])
        assert used[0] <= nc.sbuf_usable_end, (used[0], nc.sbuf_usable_end)

        PS = ctx.enter_context(nc.psum_tensor("PS", [128, 8, 512], F32))


        s_raw = [sem(f"raw_arrived{i}") for i in range(RAW)]
        s_hi = sem("hi_split")
        s_lo = sem("lo_split")
        s_unit = sem("unit_used")
        s_free = sem("group_drained")
        s_xm = sem("x_made")
        s_xh = sem("x_high")
        s_x = sem("x_low")
        s_sq = sem("squared")
        s_ssa = sem("squares_added")
        s_nmm = sem("norm_summed")
        s_var = sem("mean_square")
        s_std = sem("root")
        s_gate = sem("gate_scaled")
        s_sig = sem("gate_sigmoid")
        s_hid = sem("hidden_made")
        s_hhi = sem("hidden_high")
        s_hlo = sem("hidden_low")
        s_dve, s_act, s_pool = sem("dve_step"), sem("act_step"), sem("pool_step")
        s_h0 = sem("h_arrived")
        s_const = sem("constants_arrived")
        s_rkc = sem("scan_masks_arrived")
        s_dsc = sem("dsa_tables_arrived")
        s_bc = sem("last_block_tables_arrived")

        s_tanh, s_ghs = sem("tanh_done"), sem("gate_lora_sigmoid")
        s_lhd, s_lhh, s_lhl = sem("lora_drained"), sem("lora_high"), sem("lora_low")
        s_ghd, s_ghh, s_ghl = sem("gate_lora_drained"), sem("gate_lora_high"), sem("gate_lora_low")
        s_part = sem("part_of_unit")
        s_wa, s_dec = sem("decay_and_a_drained"), sem("decay_ready")
        s_kk, s_kksq, s_kkm, s_kkr = sem("kk_made"), sem("kk_squared"), sem("kk_summed"), sem("kk_root")
        s_rkr, s_bonm, s_bon = sem("bonus_products"), sem("bonus_summed"), sem("bonus_made")
        s_bk, s_tr = sem("pair_ready"), sem("transposed")
        s_tka, s_tkd = sem("tokens_major_act"), sem("tokens_major_dve")
        s_gm, s_gr = sem("gram_product"), sem("gram_masked")
        s_lm, s_q, s_qc, s_xt = sem("level_ready"), sem("level_q"), sem("level_q_copied"), sem("level_update")
        s_p1, s_p1c, s_um, s_ue = sem("lak_v"), sem("lak_v_copied"), sem("u_product"), sem("u_copied")
        s_ztm, s_zt, s_yvm, s_yv = sem("z_product"), sem("z_copied"), sem("yv_product"), sem("yv_copied")
        s_gvm, s_gv = sem("gamma_product"), sem("gamma_copied")
        s_sam, s_sau, s_dsm, s_s = sem("sa_product"), sem("sa_made"), sem("state_product"), sem("state_made")
        s_ysm, s_yse, s_ym, s_yc = sem("ys_product"), sem("ys_added"), sem("intra_product"), sem("y_added")
        s_mum, s_yc2, s_ysq, s_vm = sem("y_mean"), sem("y_centred"), sem("y_squared"), sem("y_var_sum")
        s_bv, s_bvr = sem("y_var"), sem("y_root")
        s_hsq, s_hsum, s_hvar, s_hroot = sem("head_squared"), sem("head_summed"), sem("head_var"), sem("head_root")
        s_hsc, s_hrot, s_hout = sem("head_scaled"), sem("head_rotated"), sem("head_ready")
        s_wtm, s_wt = sem("wi_transposed"), sem("wi_ready")
        s_rlm, s_rl, s_ra = sem("index_product"), sem("index_relu"), sem("index_added")
        s_sel = sem("selection_ready")
        s_lgm, s_lg, s_ex, s_prn = sem("logits"), sem("logits_max"), sem("exponentials"), sem("probabilities")
        s_ptm, s_pte, s_om, s_oh, s_ol = (sem("p_transposed"), sem("p_copied"), sem("head_product"),
                                          sem("head_high"), sem("head_low"))
        s_csq, s_css, s_cnm, s_cv, s_cst = (sem("latent_squared"), sem("latent_squares_added"),
                                            sem("latent_summed"), sem("latent_var"), sem("latent_root"))
        s_ang, s_sin = sem("angles"), sem("sines")
        s_bwm, s_bw, s_bst, s_bld = (sem("bias_rows_product"), sem("bias_rows"), sem("bias_stored"),
                                     sem("bias_loaded"))
        s_r2, s_hf2, s_hlo2 = sem("relu_scaled"), sem("relu_squared"), sem("hidden2_low")
        s_out = sem("result_stored")

        tok = {"f0": T, "f1": T, "f2": T, "f3": SEQ}
        after = {"f0": None, "f1": "f2", "f2": None, "f3": None}
        gain = {"f0": norm_col(0, 0), "f1": norm_col(0, 2), "f2": norm_col(1, 0), "f3": norm_col(1, 2)}

        def hv(n, a, b=None):
            b = a + 1 if b is None else b
            return h[:, a:b, T - n:T]

        def bank(G):
            return 2 * (G % 2)

        block = ctx.enter_context(nc.Block())

        @block.sync
        def _(sp):
            link = Link(sp, None)
            r_arrived, r_split = sp.alloc_register("arrived"), sp.alloc_register("split")
            sp.dma_start(h[:, :, :], t["h0"]).then_inc(s_h0, 16)
            for dst, name in ((ident, "ident"), (ones, "ones"), (bo64, "bo64"), (vec, "vec")):
                sp.dma_start(dst[:, :], t[name]).then_inc(s_const, 16)

            def load(name):
                src, w, u0 = t["w_" + name], UW[name], U0[name]

                def body(us, i):
                    for u in us:
                        U = u0 + u
                        arrived, split = val(16 * (U // RAW), i, 16), val(2 * (U - RAW + 1), i, 8)
                        s = src[u] if i is None else src[bass.ds(i * 4 + u, 1)].rearrange("o p w -> (o p) w")
                        if i is not None:
                            sp.reg_mov(r_arrived, arrived)
                            sp.reg_mov(r_split, split)
                            arrived, split = r_arrived, r_split
                        if U >= RAW:
                            sp.wait_ge(s_raw[U % RAW], arrived)
                            sp.wait_ge(s_lo, split)
                        sp.dma_start(raw[U % RAW][:, 0:w], s).then_inc(s_raw[U % RAW], 16)
                turns(link, UN[name], 4, 0, body, RAW - u0 if u0 < RAW else 0)

            for name, *_ in STAGES:
                load(name)
            sp.wait_ge(s_free, G0["b_ff2"] + 8)
            sp.dma_start(t["out"], outt[:, :, :]).then_inc(s_out, 16)
            sp.wait_ge(s_out, 16)

        @block.gpsimd
        def _(pool):
            link = Link(pool, None)
            for name, n, _m, w in STAGES:
                u0 = U0[name]

                def body(us, i):
                    for u in us:
                        U = u0 + u
                        for q, part in enumerate(halves(w)):
                            pool.wait_ge(s_hi, val(2 * U + q + 1, i, 8))
                            if U >= SPL:
                                pool.wait_ge(s_unit, val(2 * (U - SPL) + q + 1, i, 8))
                            nc.gpsimd.tensor_tensor(wlo[U % SPL][:, part], raw[U % RAW][:, part],
                                                    whi[U % SPL][:, part].bitcast(F32), ALU.subtract
                                                    ).then_inc(s_lo, 1)
                turns(link, n, 4, 0, body)
        HB = {f"f{i}": FC * i for i in range(4)}

        def dsa_jobs():
            out = []
            for hd in range(16):
                e, g = hd % 2, hd // 4
                for b in range(2):
                    nk = META + 128 * (b + 1)
                    rows = slice(64 * e, 64 * e + 64)
                    vb = [(vt[0:min(BLK, nk - BLK * j), j, g * 64:g * 64 + 64], BLK * j, min(BLK, nk - BLK * j))
                          for j in range(-(-nk // BLK))]
                    out.append(dict(q=rawq[rows, hd // 2, META + 128 * b:META + 128 * b + 128],
                                    k=rawq[rows, 8 + g, 0:nk], nk=nk, add=taken[0][:, b, 0:nk],
                                    scale=0.125, v=vb, head=hd, b=b))
            return out

        def last_jobs():
            out = []
            for hd in range(16):
                for b in range(2):
                    nk = 128 * (b + 1)
                    if hd < 8:
                        e = hd % 2
                        rows = slice(64 * e, 64 * e + 64)
                        q, k = qka[rows, hd // 2, 128 * b:128 * b + 128], qka[rows, 4 + hd // 2, 0:nk]
                        add, scale, val_ = bias[:, hd, 256 - nk:256], 0.125, vat
                    else:
                        q, k = qkb[0:96, hd - 8, 128 * b:128 * b + 128], qkb[0:96, hd, 0:nk]
                        add, scale, val_ = causal[:, 256 - nk:256], float(96 ** -0.5), vbt
                    vb = [(val_[:, j, (hd % 8) * 64:(hd % 8) * 64 + 64], 128 * j, 128) for j in range(b + 1)]
                    out.append(dict(q=q, k=k, nk=nk, add=add, scale=scale, v=vb, head=hd, b=b))
            return out

        JOBS = {"at": (dsa_jobs(), 0), "b": (last_jobs(), 32)}

        def two(x, j, n=2):
            return x[:, j:j + n, :]

        def head_tiles_at():
            out = []
            for j in range(0, 16, 2):
                gain_ = VEC["q_g"] if j < 8 else VEC["k_g"]
                out.append(dict(x=rawq[:, j:j + 2, :], rows=128, m=2, n=T, norm=j < 12, one=bo64[:, :],
                                inv=1 / 64, g=gain_, rot=rot_a[:, :], cos=cs_a[:, 0, :], sin=cs_a[:, 1, :]))
            out.append(dict(x=rawq[:, 16:17, :], rows=128, m=1, n=T, norm=False, rot=rot_a[:, :],
                            cos=cs_a[:, 0, :], sin=cs_a[:, 1, :]))
            return out

        def head_tiles_b():
            out = []
            for j in range(0, 8, 2):
                out.append(dict(x=qka[:, j:j + 2, :], rows=128, m=2, n=SEQ, norm=True, one=bo64[:, :],
                                inv=1 / 64, g=VEC["qa_g"] if j < 4 else VEC["ka_g"], rot=None))
            for j in range(0, 16, 2):
                out.append(dict(x=qkb[:, j:j + 2, :], rows=96, m=2, n=SEQ, norm=True,
                                one=ones[0:96, 0:96], inv=1 / 96, g=VEC["qb_g"] if j < 8 else VEC["kb_g"],
                                rot=rot_b[0:96, :], cos=cs_b[0:96, 0, :], sin=cs_b[0:96, 1, :]))
            return out

        TILES = {"at": head_tiles_at(), "b": head_tiles_b()}
        NT0 = {"at": 0, "b": sum(x["norm"] for x in TILES["at"])}
        RT0 = {"at": 0, "b": len(TILES["at"])}

        def counts(which, j):
            ts = TILES[which][:j + 1]
            return (NT0[which] + sum(x["norm"] for x in ts),
                    RT0[which] + sum(x["rot"] is not None for x in ts))

        @block.tensor
        def _(pe):
            link = Link(pe, None)
            mm = nc.tensor.matmul

            def products(out, w, x, start, stop, tokens=False):
                for n, (a, b) in enumerate(((w[0], x[0]), (w[0], x[1]), (w[1], x[0]))):
                    last = mm(out, b, a, start=start and n == 0, stop=stop and n == 2) if tokens else \
                        mm(out, a, b, start=start and n == 0, stop=stop and n == 2)
                return last

            def weights(U, rows, cols):
                return whi[U % SPL][rows, cols], wlo[U % SPL][rows, cols]

            ALLR = slice(0, 128)

            def norm_sum(name, n):
                pe.wait_ge(s_ssa, 8 * (N0[name] + 1))
                mm(PS[:, 6, 0:n], ones[:, :], ss[:, 0:n], start=True, stop=True).then_inc(s_nmm, 1)

            def project(name, n, b, x, norm=None, straight=0):
                def body(us, i):
                    for u in us:
                        U, G = U0[name] + u, G0[name] + u
                        for mi in range(2):
                            pe.wait_ge(s_lo, val(2 * U + mi + 1, i, 8))
                            if G >= 2 and mi == 0:
                                pe.wait_ge(s_free, val(G - 1, i, 4))
                            for k in range(KC):
                                if x and u == 0 and mi == 0:
                                    pe.wait_ge(s_x, X0[x] + k + 1)
                                c = mi * 1024 + k * 128
                                last = products(PS[:, bank(G) + mi, 0:n], weights(U, ALLR, slice(c, c + 128)),
                                                (xh[b][:, k, 0:n], xl[b][:, k, 0:n]), k == 0, k == KC - 1)
                            last.then_inc(s_unit, 1)
                            if u == 0 and mi == 0 and norm:
                                norm_sum(norm, n)
                if straight:
                    body(range(straight), None)
                    with link.loop((UN[name] - straight) // 4, 0) as i:
                        body(range(straight, straight + 4), i)
                else:
                    turns(link, UN[name], 4, 0, body)

            def project_down(name, n, hh, hl, stride, nk, ready):
                half = nk // 2

                def body(ms, i):
                    for m in ms:
                        G = G0[name] + m
                        for part in range(2):
                            U = U0[name] + 2 * m + part
                            if part == 0:
                                pe.wait_ge(s_free, val(G - 1, i, 4))
                            for k in range(half):
                                kk = part * half + k
                                if k in (0, 8):
                                    pe.wait_ge(s_lo, val(2 * U + k // 8 + 1, i, 16))
                                if m == 0:
                                    ready(kk)
                                last = products(PS[:, bank(G), 0:n], weights(U, ALLR, slice(k * 128, k * 128 + 128)),
                                                (hh[:, kk * stride:kk * stride + n], hl[:, kk * stride:kk * stride + n]),
                                                kk == 0, kk == nk - 1)
                                if k in (7, half - 1):
                                    last.then_inc(s_unit, 1)
                turns(link, 8, 4, 0, body)

            def swiglu(f):
                project(f + "_in", tok[f], 0, f, norm=f)
                project_down(f + "_dn", tok[f], hid_h, hid_l, T, FC,
                             lambda kk: pe.wait_ge(s_hlo, HB[f] + kk + 1))

            def head_norms(which):
                tiles = TILES[which]
                for j in range(len(tiles) + 2):
                    if j < len(tiles) and tiles[j]["norm"]:
                        x = tiles[j]
                        r, n = slice(0, x["rows"]), x["n"]
                        c, _r = counts(which, j)
                        pe.wait_ge(s_hsq, c)
                        if c - NT0[which] > 2:
                            pe.wait_ge(s_hvar, c - 2)
                        for q in range(2):
                            last = mm(PS[r, 2 * (c % 2) + q, 0:n], x["one"], sqp[c % 2][r, q, 0:n],
                                      start=True, stop=True)
                        last.then_inc(s_hsum, 1)
                    if j >= 2 and tiles[j - 2]["rot"] is not None:
                        x = tiles[j - 2]
                        r, n = slice(0, x["rows"]), x["n"]
                        c, cr = counts(which, j - 2)
                        pe.wait_ge(s_hsc, c)
                        if cr - RT0[which] > 2:
                            pe.wait_ge(s_hout, cr - 2)
                        for q in range(x["m"]):
                            last = mm(PS[r, 4 + 2 * (cr % 2) + q, 0:n], x["rot"], x["x"][r, q, :],
                                      start=True, stop=True)
                        last.then_inc(s_hrot, 1)

            def attention(which):
                jobs, j0 = JOBS[which]
                for j in range(len(jobs) + 3):
                    if j < len(jobs):
                        x, c = jobs[j], j0 + j
                        if j >= 2:
                            pe.wait_ge(s_lg, c - 1)
                        mm(PS[:, j % 2, 0:x["nk"]], x["q"], x["k"], start=True, stop=True).then_inc(s_lgm, 1)
                    if 0 <= j - 2 < len(jobs):
                        x, c = jobs[j - 2], j0 + j - 2
                        pe.wait_ge(s_prn, c + 1)
                        if j - 2 >= 2:
                            pe.wait_ge(s_pte, c - 1)
                        for n, (_v, k0, kn) in enumerate(x["v"]):
                            last = nc.tensor.transpose(PS[0:kn, 2 + c % 2, n * 128:n * 128 + 128],
                                                       prn[:, c % 2, k0:k0 + kn], ident[:, :])
                        last.then_inc(s_ptm, 1)
                    if 0 <= j - 3 < len(jobs):
                        x, c = jobs[j - 3], j0 + j - 3
                        pe.wait_ge(s_pte, c + 1)
                        if j - 3 >= 2:
                            pe.wait_ge(s_ol, c - 1)
                        r = 64 * (x["head"] % 2)
                        for n, (v, k0, kn) in enumerate(x["v"]):
                            last = mm(PS[r:r + 64, 4 + c % 2, 0:128], v, pts[0:kn, c % 2, n, :],
                                      start=n == 0, stop=n == len(x["v"]) - 1)
                        last.then_inc(s_om, 1)

            pe.wait_ge(s_const, 64)
            swiglu("f0")
            norm_sum("rk", T)
            project("rk_r", T, 0, "m0")
            project("rk_k", T, 1, "m1")
            project("rk_v", T, 0, "m2")
            U, G = U0["lora_wa"], G0["lora_wa"]
            pe.wait_ge(s_lo, 2 * U + 2)
            pe.wait_ge(s_free, G - 1)
            for mi in range(2):
                for k in range(KC):
                    pe.wait_ge(s_x, X0[f"m{3 + mi}"] + k + 1)
                    last = products(PS[:, bank(G) + mi, 0:T], weights(U, ALLR, slice(k * 128, k * 128 + 128)),
                                    (xh[1 - mi][:, k, :], xl[1 - mi][:, k, :]), k == 0, k == KC - 1)
            last.then_inc(s_unit, 2)
            U, G = U0["lora_g"], G0["lora_g"]
            pe.wait_ge(s_lo, 2 * U + 2)
            pe.wait_ge(s_free, G - 1)
            for mi in range(2):
                for k in range(KC):
                    pe.wait_ge(s_x, X0["m5"] + k + 1)
                    c = k * 160 + mi * 80
                    last = products(PS[0:80, bank(G) + mi, 0:T], weights(U, ALLR, slice(c, c + 80)),
                                    (xh[1][:, k, :], xl[1][:, k, :]), k == 0, k == KC - 1)
            last.then_inc(s_unit, 2)
            U = U0["wa2"]
            pe.wait_ge(s_lo, 2 * U + 2)
            pe.wait_ge(s_lhl, 1)
            for m in range(KC):
                G = G0["wa2"] + m
                pe.wait_ge(s_free, G - 1)
                for mi in range(2):
                    r = slice(64 * mi, 64 * mi + 64)
                    last = products(PS[:, bank(G) + mi, 0:T], weights(U, r, slice(m * 128, m * 128 + 128)),
                                    (lh_h[r, :], lh_l[r, :]), True, True)
                last.then_inc(*((s_part, 1) if m < KC - 1 else (s_unit, 2)))
            pe.wait_ge(s_kksq, 1)
            for c in range(KC):
                if c >= 2:
                    pe.wait_ge(s_kkr, c - 1)
                mm(PS[:, 4 + c % 2, 0:T], bo64[:, :], ktmp[:, c, 0:T], start=True, stop=True).then_inc(s_kkm, 1)
            for c in range(KC):
                pe.wait_ge(s_rkr, c + 1)
                if c >= 2:
                    pe.wait_ge(s_bon, c - 1)
                mm(PS[:, 4 + c % 2, 0:T], bo64[:, :], ktmp[:, c, 0:T], start=True, stop=True).then_inc(s_bonm, 1)

            for half in range(2):
                for p in range(4):
                    c = 4 * half + p
                    pe.wait_ge(s_bk, c + 1)
                    for n, src in enumerate((A_[:, c, :], bh[:, :], kh[:, :], V_[:, c, :])):
                        for b in range(NB):
                            last = nc.tensor.transpose(PS[0:BLK, n, b * 128:b * 128 + 128],
                                                       src[:, b * BLK:b * BLK + BLK], ident[:, :])
                        last.then_inc(s_tr, 1)
                    for n in range(10):
                        e, ty = n // 5, n % 5
                        r = slice(64 * e, 64 * e + 64)
                        if n == 4:
                            pe.wait_ge(s_tka, 2 * c + 2)
                            pe.wait_ge(s_tkd, 2 * c + 2)
                        if n >= 8:
                            pe.wait_ge(s_gr, 10 * c + n - 7)
                        left = (B_, A_, K_, B_, K_)[ty]
                        right = (A_, B_, A_, R_, R_)[ty]
                        for b in range(NB):
                            bl = slice(b * BLK, b * BLK + BLK)
                            last = mm(PS[0:BLK, (4 + n) % 8, bl], left[r, c, bl], right[r, c, bl],
                                      start=True, stop=True)
                        last.then_inc(s_gm, 1)
                    for lv in range(4):
                        for e in range(2):
                            pe.wait_ge(s_lm, (c * 5 + lv) * 2 + e + 1)
                            for b in range(NB):
                                bl = slice(b * BLK, b * BLK + BLK)
                                last = mm(PS[0:BLK, e, bl], LM[e][:, bl], XX[e][:, bl], start=True, stop=True)
                            last.then_inc(s_q, 1)
                        for e in range(2):
                            pe.wait_ge(s_qc, (c * 4 + lv) * 2 + e + 1)
                            for b in range(NB):
                                bl = slice(b * BLK, b * BLK + BLK)
                                if lv < 3:
                                    mm(PS[0:BLK, 2 + e, bl], XT[e][:, bl], QQ[e][:, bl], start=True, stop=True)
                            for b in range(NB):
                                bl = slice(b * BLK, b * BLK + BLK)
                                last = mm(PS[0:BLK, 4 + e, bl], QQ[e][:, bl], XT[e][:, bl], start=True, stop=True)
                            last.then_inc(s_xt, 1)
                    pe.wait_ge(s_lm, (c * 5 + 4) * 2 + 2)

                    def per_block(out, left, right):
                        for e in range(2):
                            for b in range(NB):
                                last = mm(out(e, b), left(e, b), right(e, b), start=True, stop=True)
                        return last

                    def bl(b):
                        return slice(b * BLK, b * BLK + BLK)

                    def tk(e):
                        return slice(64 * e, 64 * e + 64)
                    per_block(lambda e, b: PS[0:BLK, 6, b * 128 + 64 * e:b * 128 + 64 * e + 64],
                              lambda e, b: lak[e][:, bl(b)], lambda e, b: vtok[:, b, tk(e)]).then_inc(s_p1, 1)
                    per_block(lambda e, b: PS[tk(e), 0, bl(b)],
                              lambda e, b: atok[:, b, tk(e)], lambda e, b: XT[e][:, bl(b)]).then_inc(s_ztm, 1)
                    per_block(lambda e, b: PS[tk(e), 1, bl(b)],
                              lambda e, b: vtok[:, b, tk(e)], lambda e, b: mrk[e][:, bl(b)]).then_inc(s_yvm, 1)
                    for ch in range(NCH):
                        b, r = ch // 3, slice(CH * (ch % 3), CH * (ch % 3) + CH)
                        for e in range(2):
                            last = mm(PS[tk(e), 2 + ch % 3, b * 64:b * 64 + 64], ktok[r, b, tk(e)], vtok[r, b, tk(e)],
                                      start=True, stop=True)
                    last.then_inc(s_gvm, 1)
                    pe.wait_ge(s_p1c, c + 1)
                    per_block(lambda e, b: PS[0:BLK, 7, b * 128 + 64 * e:b * 128 + 64 * e + 64],
                              lambda e, b: XT[e][:, bl(b)], lambda e, b: p1[:, b, tk(e)]).then_inc(s_um, 1)

                heads = [(p, e) for p in range(4) for e in range(2)]
                pe.wait_ge(s_ue, 4 * half + 4)
                pe.wait_ge(s_zt, 4 * half + 4)
                for ch in range(NCH):
                    b, r0 = ch // 3, CH * (ch % 3)
                    r = slice(r0, r0 + CH)
                    if ch:
                        pe.wait_ge(s_s, 8 * half + ch)
                        for p, e in heads:
                            last = mm(PS[r, 3 + e, p * 64:p * 64 + 64],
                                      A_[64 * e:64 * e + 64, 4 * half + p, ch * CH:ch * CH + CH],
                                      S_[ch % 2][64 * e:64 * e + 64, p * 64:p * 64 + 64], start=True, stop=True)
                        last.then_inc(s_sam, 1)
                    if ch < NCH - 1:
                        if ch:
                            pe.wait_ge(s_sau, 8 * half + ch)
                        for p, e in heads:
                            last = mm(PS[64 * e:64 * e + 64, 5, p * 64:p * 64 + 64],
                                      btok[r, b, p * 128 + 64 * e:p * 128 + 64 * e + 64],
                                      U_[r, b, (2 * p + e) * 64:(2 * p + e) * 64 + 64], start=True, stop=True)
                        last.then_inc(s_dsm, 1)
                    if ch:
                        if ch > 2:
                            pe.wait_ge(s_yse, 8 * half + ch - 2)
                        for p, e in heads:
                            last = mm(PS[64 * e:64 * e + 64, 6 + ch % 2, p * CH:p * CH + CH],
                                      S_[ch % 2][64 * e:64 * e + 64, p * 64:p * 64 + 64],
                                      R_[64 * e:64 * e + 64, 4 * half + p, ch * CH:ch * CH + CH],
                                      start=True, stop=True)
                        last.then_inc(s_ysm, 1)
                pe.wait_ge(s_sau, 8 * half + 8)
                for p in range(4):
                    if p >= 2:
                        pe.wait_ge(s_yc, 4 * half + p - 1)
                    for e in range(2):
                        for b in range(NB):
                            last = mm(PS[64 * e:64 * e + 64, p % 2, b * BLK:b * BLK + BLK],
                                      U_[:, b, (2 * p + e) * 64:(2 * p + e) * 64 + 64],
                                      mrb[:, 2 * p + e, b * BLK:b * BLK + BLK], start=True, stop=True)
                    last.then_inc(s_ym, 1)

            for c in range(KC):
                if c == 0:
                    pe.wait_ge(s_yc, KC)
                if c >= 2:
                    pe.wait_ge(s_yc2, c - 1)
                mm(PS[:, 4 + c % 2, 0:T], bo64[:, :], K_[:, c, 0:T], start=True, stop=True).then_inc(s_mum, 1)
            for c in range(KC):
                pe.wait_ge(s_ysq, c + 1)
                if c >= 2:
                    pe.wait_ge(s_bv, c - 1)
                mm(PS[:, 6 + c % 2, 0:T], bo64[:, :], A_[:, c, 0:T], start=True, stop=True).then_inc(s_vm, 1)
            U = U0["g2"]
            pe.wait_ge(s_lo, 2 * U + 2)
            pe.wait_ge(s_ghl, 1)
            for g in range(4):
                G = G0["g2"] + g
                pe.wait_ge(s_free, G - 1)
                for mi in range(2):
                    for k in range(2):
                        c = k * D + (2 * g + mi) * 128
                        last = products(PS[:, bank(G) + mi, 0:T], weights(U, slice(0, 80), slice(c, c + 128)),
                                        (gh_h[:, k, :], gh_l[:, k, :]), k == 0, k == 1)
                last.then_inc(*((s_part, 1) if g < 3 else (s_unit, 2)))
            project("rk_o", T, 1, "ro")
            swiglu("f1")

            swiglu("f2")
            norm_sum("at", T)
            project("at_q", T, 0, "at")
            project("at_k", T, 0, "at")
            project("at_qi", T, 0, "at")
            project("at_tail", T, 0, "at")
            U, G = U0["at_v"], G0["at_v"]
            pe.wait_ge(s_lo, 2 * U + 2)
            pe.wait_ge(s_free, G - 1)
            for j in range(NB):
                kn = min(BLK, T - BLK * j)
                for k in range(KC):
                    last = products(PS[0:kn, bank(G) + j // 2, (j % 2) * 256:(j % 2) * 256 + 256],
                                    weights(U, ALLR, slice(k * 256, k * 256 + 256)),
                                    (xh[0][:, k, j * BLK:j * BLK + kn], xl[0][:, k, j * BLK:j * BLK + kn]),
                                    k == 0, k == KC - 1, tokens=True)
            last.then_inc(s_unit, 2)
            pe.wait_ge(s_free, G + 1)
            pe.wait_ge(s_dsc, 48)
            head_norms("at")
            pe.wait_ge(s_hout, RT0["b"])
            for b in range(2):
                last = nc.tensor.transpose(PS[:, 0, b * 8:b * 8 + 8], rawq[0:8, 17, META + 128 * b:META + 128 * b + 128],
                                           ident[0:8, 0:8])
            last.then_inc(s_wtm, 1)
            pe.wait_ge(s_wt, 1)
            for b in range(2):
                nk = META + 128 * (b + 1)
                for hd in range(8):
                    n = b * 8 + hd
                    r = slice(64 * (hd % 2), 64 * (hd % 2) + 64)
                    if n >= 2:
                        pe.wait_ge(s_rl, n - 1)
                    mm(PS[:, 2 + n % 2, 0:nk], rawq[r, 12 + hd // 2, META + 128 * b:META + 128 * b + 128],
                       rawq[r, 16, 0:nk], start=True, stop=True).then_inc(s_rlm, 1)
            pe.wait_ge(s_rl, 16)
            attention("at")
            pe.wait_ge(s_ol, 32)
            project("at_o", SEQ, 1, None)
            swiglu("f3")

            norm_sum("b", SEQ)
            project("b_qa", SEQ, 0, "b")
            project("b_ka", SEQ, 0, "b")
            for u in range(2):
                U, G = U0["b_va"] + u, G0["b_va"] + u
                pe.wait_ge(s_lo, 2 * U + 2)
                pe.wait_ge(s_free, G - 1)
                for j in range(2):
                    for k in range(KC):
                        last = products(PS[:, bank(G) + j, 0:256], weights(U, ALLR, slice(k * 256, k * 256 + 256)),
                                        (xh[0][:, k, j * 128:j * 128 + 128], xl[0][:, k, j * 128:j * 128 + 128]),
                                        k == 0, k == KC - 1, tokens=True)
                last.then_inc(s_unit, 2)
            project("b_cq", SEQ, 0, "b")
            project("b_ckv", SEQ, 0, "b")
            U, G = U0["b_tail"], G0["b_tail"]
            pe.wait_ge(s_lo, 2 * U + 2)
            pe.wait_ge(s_free, G - 1)
            for k in range(KC):
                last = products(PS[:, bank(G), 0:SEQ], weights(U, ALLR, slice(k * 128, k * 128 + 128)),
                                (xh[0][:, k, 0:SEQ], xl[0][:, k, 0:SEQ]), k == 0, k == KC - 1)
            last.then_inc(s_unit, 2)
            pe.wait_ge(s_bc, 96)
            for hd in range(8):
                if hd >= 2:
                    pe.wait_ge(s_bw, hd - 1)
                mm(PS[:, 4 + hd % 2, 0:384], relb[:, hd, :], distt[:, :], start=True, stop=True).then_inc(s_bwm, 1)
            for n, need in enumerate((6, 8)):
                pe.wait_ge(s_css, need)
                mm(PS[:, 6 + n, 0:SEQ], ones[:, :], bt[:, n, :], start=True, stop=True).then_inc(s_cnm, 1)
            for u in range(4):
                U, G = U0["b_uq"] + u, G0["b_uq"] + u
                pe.wait_ge(s_lo, 2 * U + 2)
                pe.wait_ge(s_free, G - 1)
                for mi in range(2):
                    for k in range(6):
                        if u == 0:
                            pe.wait_ge(s_x, X0["cq"] + k + 1)
                        c = k * 192 + mi * 96
                        last = products(PS[0:96, bank(G) + mi, 0:SEQ], weights(U, ALLR, slice(c, c + 96)),
                                        (xh[1][:, k, 0:SEQ], xl[1][:, k, 0:SEQ]), k == 0, k == 5)
                last.then_inc(s_unit, 2)
            U = U0["b_ukv"]
            pe.wait_ge(s_lo, 2 * U + 2)
            pe.wait_ge(s_x, X0["ckv"] + 2)
            for g in range(3):
                G = G0["b_ukv"] + g
                pe.wait_ge(s_free, G - 1)
                for mi in range(2):
                    for k in range(2):
                        if g < 2:
                            c = k * 1024 + (2 * g + mi) * 128
                            last = products(PS[:, bank(G) + mi, 0:SEQ], weights(U, ALLR, slice(c, c + 128)),
                                            (xh[1][:, 6 + k, 0:SEQ], xl[1][:, 6 + k, 0:SEQ]), k == 0, k == 1)
                        else:
                            c = k * 1024 + 512
                            tb = slice(mi * 128, mi * 128 + 128)
                            last = products(PS[:, bank(G) + mi, 0:512], weights(U, ALLR, slice(c, c + 512)),
                                            (xh[1][:, 6 + k, tb], xl[1][:, 6 + k, tb]), k == 0, k == 1, tokens=True)
                last.then_inc(*((s_part, 1) if g < 2 else (s_unit, 2)))
            pe.wait_ge(s_free, G0["b_ukv"] + 3)
            head_norms("b")
            pe.wait_ge(s_hout, RT0["b"] + 8)
            pe.wait_ge(s_hsc, NT0["b"] + 12)
            attention("b")
            pe.wait_ge(s_ol, 64)
            project("b_o", SEQ, 1, None)
            project("b_ff1", SEQ, 0, "ff", norm="ff", straight=4)
            project_down("b_ff2", SEQ, hid2_h, hid2_l, SEQ, 32,
                         lambda kk: pe.wait_ge(s_hlo2, kk // 2 + 1))

        C1 = 6.28125
        C2 = float(np.float32(np.float16(2 * math.pi - C1)))
        C3 = float(2 * math.pi - C1 - C2)
        MAGIC = float(1.5 * 2 ** 23)
        PI = 3.1415925

        @block.vector
        def _(dve):
            v = nc.vector
            step = Link(dve, s_dve)

            def col(c, rows=slice(0, 128)):
                return vec[rows, c:c + 1]

            def low(dst, src, high, signal):
                v.tensor_tensor(dst, src, high.bitcast(F32), ALU.subtract).then_inc(signal, 1)

            def rms(name, n):
                dve.wait_ge(s_nmm, N0[name] + 1)
                v.tensor_scalar(rstd[:, 0:n], PS[:, 6, 0:n], 1 / D, EPS, ALU.mult, ALU.add).then_inc(s_var, 1)
                dve.wait_ge(s_std, N0[name] + 1)
                step(v.reciprocal(rstd[:, 0:n], rstd[:, 0:n]))

            def start_sum():
                step(v.memset(ss[:, :], 0.0))

            def add_squares(name, tile, src, n, i=None):
                v.tensor_tensor(ss[:, 0:n], ss[:, 0:n], src, ALU.add).then_inc(s_ssa, 1)
                dve.wait_ge(s_ssa, val(8 * N0[name] + tile + 1, i, 4))

            def swiglu(f):
                n, name, hb = tok[f], f + "_in", HB[f]

                def first(u, i):
                    U, G = U0[name] + u, G0[name] + u
                    dve.wait_ge(s_unit, val(2 * U + 1, i, 8))
                    v.tensor_tensor(gate[:, u % 2, 0:n], PS[:, bank(G), 0:n], rstd[:, 0:n], ALU.mult).then_inc(s_gate, 1)
                    dve.wait_ge(s_unit, val(2 * U + 2, i, 8))
                    v.tensor_tensor(upg[:, u % 2, 0:n], PS[:, bank(G) + 1, 0:n], rstd[:, 0:n], ALU.mult).then_inc(s_free, 1)
                    dve.wait_ge(s_free, val(G + 1, i, 4))
                    step(v.tensor_tensor(upg[:, u % 2, 0:n], upg[:, u % 2, 0:n], gate[:, u % 2, 0:n], ALU.mult))

                def second(u, i):
                    if u >= 2:
                        dve.wait_ge(s_hlo, val(hb + u - 1, i, 4))
                    dve.wait_ge(s_sig, val(hb + u + 1, i, 4))
                    v.tensor_tensor(hidf[:, u % 2, 0:n], upg[:, u % 2, 0:n], sig[:, u % 2, 0:n], ALU.mult).then_inc(s_hid, 1)
                    dve.wait_ge(s_hid, val(hb + u + 1, i, 4))

                def third(u, i):
                    dve.wait_ge(s_hhi, val(hb + u + 1, i, 4))
                    o = slice(u * T, u * T + n) if i is None else bass.ds(i * (4 * T) + u * T, n)
                    low(hid_l[:, o], hidf[:, u % 2, 0:n], hid_h[:, o], s_hlo)

                def body(us, i):
                    us = list(us)
                    for k, u in enumerate(us):
                        if u == 0:
                            rms(f, n)
                        first(u, i)
                        if k >= 1:
                            second(u - 1, i)
                        if k >= 2:
                            third(u - 2, i)
                    second(us[-1], i)
                    if len(us) > 1:
                        third(us[-2], i)
                    third(us[-1], i)
                turns(step, FC, 4, 4, body)

            def residual(name, n, w, units, factor, norm, g, split):
                groups = 8 // w

                def add(j, i):
                    U, G = U0[name] + units * (j + 1) - 1, G0[name] + j
                    dve.wait_ge(s_unit, val(2 * (U + 1), i, 8 * units))
                    if i is None:
                        x = hv(n, j * w, j * w + w)
                    else:
                        x = h[:, bass.ds(i * 4 + j, 1), T - n:T]
                    v.scalar_tensor_tensor(x, PS[:, bank(G):bank(G) + w, 0:n], factor, x,
                                           ALU.mult, ALU.add).then_inc(s_free, 1)
                    if g is None:
                        return
                    dve.wait_ge(s_free, val(G + 1, i, 4))
                    for q in range(w):
                        m = j * w + q
                        if i is None:
                            v.tensor_scalar(xg[:, j % 2, q, 0:n], hv(n, m)[:, 0, :], col(g + m), None, ALU.mult).then_inc(s_xm, 1)
                        else:
                            v.tensor_scalar(xg[:, j % 2, q, 0:n], h[:, bass.ds(i * 4 + m, 1), T - n:T].rearrange("p o n -> p (o n)"),
                                            vec[:, bass.ds(i * 4 + (g + m), 1)], None, ALU.mult).then_inc(s_xm, 1)

                def after_act(j, i):
                    dve.wait_ge(s_sq, val(Q0[norm] + j + 1, i, 4))
                    for q in range(w):
                        add_squares(norm, j * w + q, sq[:, j % 2, q, 0:n], n, i)
                    if g is None:
                        return
                    for q in range(w):
                        m = j * w + q
                        dve.wait_ge(s_xh, val(X0[split] + m + 1, i, 4))
                        o = slice(m, m + 1) if i is None else bass.ds(i * 4 + m, 1)
                        low(xl[0][:, o, 0:n].rearrange("p o n -> p (o n)"), xg[:, j % 2, q, 0:n],
                            xh[0][:, o, 0:n].rearrange("p o n -> p (o n)"), s_x)

                def body(js, i):
                    js = list(js)
                    for k, j in enumerate(js):
                        add(j, i)
                        if k >= 1:
                            after_act(j - 1, i)
                    after_act(js[-1], i)
                start_sum()
                turns(step, groups, 4, 0, body)

            def split_input(name, b, made, n, chunks=range(KC), at0=0):
                for k in chunks:
                    dve.wait_ge(s_xh, X0[name] + k - at0 + 1)
                    low(xl[b][:, k, 0:n], made(k), xh[b][:, k, 0:n], s_x)

            def head_norms(which):
                tiles = TILES[which]
                for j in range(len(tiles) + 2):
                    if j < len(tiles) and tiles[j]["norm"]:
                        x = tiles[j]
                        r, n = slice(0, x["rows"]), x["n"]
                        c, _r = counts(which, j)
                        if c > 2:
                            dve.wait_ge(s_hsc, c - 2)
                        dve.wait_ge(s_hsum, c)
                        v.tensor_scalar(hvr[c % 2][r, :, 0:n], PS[r, 2 * (c % 2):2 * (c % 2) + 2, 0:n],
                                        x["inv"], EPS, ALU.mult, ALU.add).then_inc(s_hvar, 1)
                    if 0 <= j - 1 < len(tiles) and tiles[j - 1]["norm"]:
                        x = tiles[j - 1]
                        r, n = slice(0, x["rows"]), x["n"]
                        c, _r = counts(which, j - 1)
                        dve.wait_ge(s_hroot, c)
                        step(v.reciprocal(hvr[c % 2][r, :, 0:n], hvr[c % 2][r, :, 0:n]))
                        v.scalar_tensor_tensor(x["x"], x["x"], col(x["g"], r), hvr[c % 2][r, :, 0:n],
                                               ALU.mult, ALU.mult).then_inc(s_hsc, 1)
                    if j >= 2 and tiles[j - 2]["rot"] is not None:
                        x = tiles[j - 2]
                        r, n, m = slice(0, x["rows"]), x["n"], x["m"]
                        c, cr = counts(which, j - 2)
                        dve.wait_ge(s_hrot, cr)
                        b0 = 4 + 2 * (cr % 2)
                        step(v.tensor_tensor(rtt[r, 0:m, 0:n], PS[r, b0:b0 + m, 0:n],
                                             x["sin"].unsqueeze(1).broadcast_to([x["rows"], m, n]), ALU.mult))
                        step(v.tensor_tensor(x["x"], x["x"],
                                             x["cos"].unsqueeze(1).broadcast_to([x["rows"], m, n]), ALU.mult))
                        v.tensor_tensor(x["x"], x["x"], rtt[r, 0:m, 0:n], ALU.add).then_inc(s_hout, 1)
                        dve.wait_ge(s_hout, cr)

            def attention(which):
                jobs, j0 = JOBS[which]
                for j in range(len(jobs) + 4):
                    if j < len(jobs):
                        x, c = jobs[j], j0 + j
                        nk = x["nk"]
                        dve.wait_ge(s_lgm, c + 1)
                        if j >= 2:
                            dve.wait_ge(s_ex, c - 1)
                        step(v.tensor_tensor_reduce(lg[:, c % 2, 0:nk], PS[:, j % 2, 0:nk], x["add"], x["scale"],
                                                    NEG * 100, ALU.add, ALU.max, amx[:, c:c + 1]))
                        v.tensor_scalar(nmx[:, c:c + 1], amx[:, c:c + 1], -1.0, None, ALU.mult).then_inc(s_lg, 1)
                    if 0 <= j - 1 < len(jobs):
                        x, c = jobs[j - 1], j0 + j - 1
                        nk = x["nk"]
                        dve.wait_ge(s_ex, c + 1)
                        step(v.reciprocal(ainv[:, c:c + 1], asum[:, c:c + 1]))
                        if j - 1 >= 2:
                            dve.wait_ge(s_ptm, c - 1)
                        v.tensor_scalar(prn[:, c % 2, 0:nk], pr[:, c % 2, 0:nk], ainv[:, c:c + 1], None,
                                        ALU.mult).then_inc(s_prn, 1)
                    if 0 <= j - 4 < len(jobs):
                        x, c = jobs[j - 4], j0 + j - 4
                        r = slice(64 * (x["head"] % 2), 64 * (x["head"] % 2) + 64)
                        o = slice(128 * x["b"], 128 * x["b"] + 128)
                        dve.wait_ge(s_oh, c + 1)
                        low(xl[1][r, x["head"] // 2, o], PS[r, 4 + c % 2, 0:128], xh[1][r, x["head"] // 2, o], s_ol)

            def drain2(name, u, dst, rows=slice(0, 128), n=T):
                U, G = U0[name] + u, G0[name] + u
                dve.wait_ge(s_unit, 2 * (U + 1))
                v.tensor_copy(dst, PS[rows, bank(G):bank(G) + 2, 0:n]).then_inc(s_free, 1)

            step(v.memset(epsc[:, :], 0.0))
            start_sum()
            dve.wait_ge(s_const, 64)
            dve.wait_ge(s_h0, 16)
            for j in range(4):
                for q in range(2):
                    m = 2 * j + q
                    if j >= 2:
                        dve.wait_ge(s_xh, m - 3)
                    v.tensor_scalar(xg[:, j % 2, q, :], h[:, m, :], col(gain["f0"] + m), None, ALU.mult).then_inc(s_xm, 1)
                    dve.wait_ge(s_sq, m + 1)
                    add_squares("f0", m, sq[:, m % 2, 0, :], T)
                    dve.wait_ge(s_xh, m + 1)
                    low(xl[0][:, m, :], xg[:, j % 2, q, :], xh[0][:, m, :], s_x)
            swiglu("f0")
            residual("f0_dn", T, 1, 2, 0.5, "rk", None, None)

            dve.wait_ge(s_ssa, 8 * N0["rk"] + 8)
            rms("rk", T)
            for c in range(KC):
                step.do(v.scalar_tensor_tensor(hn[:, c, :], h[:, c, :], col(norm_col(0, 1) + c), rstd[:, :],
                                               ALU.mult, ALU.mult))
            step.sync()
            step.do(v.tensor_tensor(xx[:, :, 1:T], hn[:, :, 0:T - 1], hn[:, :, 1:T], ALU.subtract))
            step(v.tensor_scalar(xx[:, :, 0:1], hn[:, :, 0:1], -1.0, None, ALU.mult))

            def mix(s, which):
                if s:
                    dve.wait_ge(s_x, X0[f"m{s}"])
                for c in range(KC):
                    v.scalar_tensor_tensor(xmf[:, c, :], xx[:, c, :], col(VEC["rk_mix"] + 8 * which + c), hn[:, c, :],
                                           ALU.mult, ALU.add).then_inc(s_xm, 1)
                if s >= 2:
                    dve.wait_ge(s_unit, 2 * U0[("rk_k", "rk_v", "lora_wa", "lora_g")[s - 2]])
                split_input(f"m{s}", s % 2, lambda k: xmf[:, k, :], T)

            for x in (R_, K_, V_, A_, B_):
                step.do(v.memset(x[:, :, T:TP], 0.0))
            step.sync()
            mix(0, 0)
            mix(1, 2)
            for u in range(4):
                drain2("rk_r", u, R_[:, 2 * u:2 * u + 2, 0:T])
            mix(2, 3)
            for u in range(4):
                drain2("rk_k", u, K_[:, 2 * u:2 * u + 2, 0:T])
            mix(3, 1)
            for u in range(4):
                drain2("rk_v", u, V_[:, 2 * u:2 * u + 2, 0:T])
            mix(4, 4)
            U, G = U0["lora_wa"], G0["lora_wa"]
            dve.wait_ge(s_unit, 2 * (U + 1))
            v.tensor_copy(lh[0:64, :], PS[0:64, bank(G), 0:T]).then_inc(s_lhd, 1)
            v.tensor_copy(lh[64:128, :], PS[64:128, bank(G) + 1, 0:T]).then_inc(s_free, 1)
            mix(5, 5)
            dve.wait_ge(s_lhh, 1)
            low(lh_l[:, :], lh[:, :], lh_h[:, :], s_lhl)
            U, G = U0["lora_g"], G0["lora_g"]
            dve.wait_ge(s_unit, 2 * (U + 1))
            v.tensor_copy(gh[:, :, :], PS[0:80, bank(G):bank(G) + 2, 0:T]).then_inc(s_free, 1)
            dve.wait_ge(s_ghh, 1)
            low(gh_l[:, :, :], gh[:, :, :], gh_h[:, :, :], s_ghl)
            step(v.memset(W_[:, :, T:TP], 1.0))
            for m in range(KC):
                G = G0["wa2"] + m
                if m < KC - 1:
                    dve.wait_ge(s_part, m + 1)
                else:
                    dve.wait_ge(s_unit, 2 * (U0["wa2"] + 1))
                v.tensor_scalar(W_[:, m, 0:T], PS[:, bank(G), 0:T], col(VEC["w0"] + m), None, ALU.add).then_inc(s_wa, 1)
                v.tensor_scalar(a_g[:, m, :], PS[:, bank(G) + 1, 0:T], col(VEC["a0"] + m), None, ALU.add).then_inc(s_free, 1)
            for c in range(KC):
                v.tensor_scalar(A_[:, c, 0:T], K_[:, c, 0:T], col(VEC["k_k"] + c), None, ALU.mult).then_inc(s_kk, 1)
            dve.wait_ge(s_dec, 1)
            step(v.memset(wst[:, :, :], 0.0))
            step(v.tensor_copy(wst[:, :, 0:TP:CH], W_[:, :, 0:TP:CH]))
            step(v.memset(W_[:, :, 0:TP:CH], 0.0))
            step(v.tensor_tensor_scan(Wc[:, :, :].rearrange("p c t -> p (c t)"), W_[:, :, :].rearrange("p c t -> p (c t)"),
                                      wst[:, :, :].rearrange("p c t -> p (c t)"), 0.0, ALU.mult, ALU.add))
            step(v.tensor_copy(wend[:, :, :], Wc[:, :, CH - 1:TP:CH]))
            dve.wait_ge(s_kkr, KC)
            step(v.tensor_scalar(kden[:, :, :], kden[:, :, :], 1e-12, None, ALU.max))
            step(v.reciprocal(kden[:, :, :], kden[:, :, :]))
            step(v.tensor_tensor(A_[:, :, 0:T], A_[:, :, 0:T], kden[:, :, :], ALU.mult))
            step(v.tensor_tensor(B_[:, :, 0:T], A_[:, :, 0:T], a_g[:, :, :], ALU.mult))
            for c in range(KC):
                step.do(v.tensor_scalar(a_g[:, c, :], a_g[:, c, :], 1.0, col(VEC["k_a"] + c), ALU.subtract, ALU.mult))
            step.sync()
            step(v.scalar_tensor_tensor(K_[:, :, 0:T], a_g[:, :, :], 1.0, K_[:, :, 0:T], ALU.add, ALU.mult))
            for c in range(KC):
                v.scalar_tensor_tensor(ktmp[:, c, 0:T], R_[:, c, 0:T], col(VEC["r_k"] + c), K_[:, c, 0:T],
                                       ALU.mult, ALU.mult).then_inc(s_rkr, 1)
            step(v.tensor_scalar(first[:, :, :], A_[:, :, 0:TP:CH], -1.0, None, ALU.mult))
            step(v.scalar_tensor_tensor(A_[:, :, 1:TP], A_[:, :, 1:TP], -1.0, Wc[:, :, 0:TP - 1], ALU.mult, ALU.mult))
            step(v.tensor_copy(A_[:, :, 0:TP:CH], first[:, :, :]))
            step(v.tensor_tensor(R_[:, :, :], R_[:, :, :], Wc[:, :, :], ALU.mult))
            step(v.reciprocal(Wc[:, :, :], Wc[:, :, :]))
            step(v.tensor_tensor(B_[:, :, :], B_[:, :, :], Wc[:, :, :], ALU.mult))
            step(v.tensor_tensor(K_[:, :, :], K_[:, :, :], Wc[:, :, :], ALU.mult))
            for c in range(KC):
                dve.wait_ge(s_bonm, c + 1)
                v.tensor_tensor(bonus[:, c, :], PS[:, 4 + c % 2, 0:T], V_[:, c, 0:T], ALU.mult).then_inc(s_bon, 1)
            dve.wait_ge(s_bon, KC)

            dve.wait_ge(s_rkc, 16)

            def mask(k):
                return masks[0:BLK, k, :].unsqueeze(1).broadcast_to([BLK, NB, BLK])

            def blocks(x):
                return x.rearrange("p (b t) -> p b t", b=NB)

            for half in range(2):
                for p in range(4):
                    c = 4 * half + p
                    if c:
                        dve.wait_ge(s_zt, c)
                        dve.wait_ge(s_gv, c)
                        dve.wait_ge(s_yv, c)
                        dve.wait_ge(s_ue, c)
                    for n, (dst, src) in enumerate(((bh, B_), (kh, K_))):
                        ins = v.tensor_tensor(dst[:, :].rearrange("p (n t) -> p n t", t=CH),
                                              src[:, c, :].rearrange("p (n t) -> p n t", t=CH),
                                              wend[:, c, :].unsqueeze(2).broadcast_to([128, NCH, CH]), ALU.mult)
                        if n:
                            ins.then_inc(s_bk, 1)
                        else:
                            step(ins)
                    for n, dst in enumerate((ktok, vtok)):
                        dve.wait_ge(s_tr, 4 * c + 3 + n)
                        v.tensor_copy(dst[:, :, :], PS[0:BLK, 2 + n, 0:384].rearrange("p (b f) -> p b f", b=NB)).then_inc(s_tkd, 1)
                    for n in range(10):
                        e, ty = n // 5, n % 5
                        dst = (LT[e][:, :], L_[e][:, :], lak[e][:, :], mrb[:, 2 * p + e, :], mrk[e][:, :])[ty]
                        dve.wait_ge(s_gm, 10 * c + n + 1)
                        v.tensor_tensor(blocks(dst), blocks(PS[0:BLK, (4 + n) % 8, 0:TP]), mask((0, 1, 0, 2, 2)[ty]),
                                        ALU.mult).then_inc(s_gr, 1)
                    dve.wait_ge(s_gr, 10 * c + 10)
                    for e in range(2):
                        for dst, src, mk in ((XX, L_, 3), (XT, LT, 4)):
                            step(v.tensor_tensor(blocks(dst[e][:, :]), blocks(src[e][:, :]), mask(mk), ALU.mult))
                            step(v.tensor_tensor(blocks(dst[e][:, :]), blocks(dst[e][:, :]), mask(9), ALU.add))
                        v.tensor_tensor(blocks(LM[e][:, :]), blocks(LT[e][:, :]), mask(5), ALU.mult).then_inc(s_lm, 1)
                    for lv in range(4):
                        for e in range(2):
                            dve.wait_ge(s_xt, (c * 4 + lv) * 2 + e + 1)
                            if lv < 3:
                                step(v.tensor_tensor(XX[e][:, :], XX[e][:, :], PS[0:BLK, 2 + e, 0:TP], ALU.add))
                                step(v.tensor_tensor(XT[e][:, :], XT[e][:, :], PS[0:BLK, 4 + e, 0:TP], ALU.add))
                                v.tensor_tensor(blocks(LM[e][:, :]), blocks(LT[e][:, :]), mask(6 + lv), ALU.mult).then_inc(s_lm, 1)
                            else:
                                v.tensor_tensor(XT[e][:, :], XT[e][:, :], PS[0:BLK, 4 + e, 0:TP], ALU.add).then_inc(s_lm, 1)
                    dve.wait_ge(s_yvm, c + 1)
                    v.tensor_copy(K_[:, c, :], PS[:, 1, 0:TP]).then_inc(s_yv, 1)
                    dve.wait_ge(s_um, c + 1)
                    v.tensor_copy(U_[:, :, p * 128:p * 128 + 128],
                                  PS[0:BLK, 7, 0:384].rearrange("p (b f) -> p b f", b=NB)).then_inc(s_ue, 1)

                q4 = slice(4 * half, 4 * half + 4)
                dve.wait_ge(s_gv, 4 * half + 4)
                dve.wait_ge(s_ue, 4 * half + 4)
                dve.wait_ge(s_yv, 4 * half + 4)
                for ch in range(NCH):
                    b, r = ch // 3, slice(CH * (ch % 3), CH * (ch % 3) + CH)
                    if ch:
                        dve.wait_ge(s_sam, 8 * half + ch)
                        us = U_[r, b, :].rearrange("s (p e i) -> s e p i", e=2, i=64)
                        v.tensor_tensor(us, us, PS[r, 3:5, 0:256].rearrange("s e (p i) -> s e p i", i=64),
                                        ALU.add).then_inc(s_sau, 1)
                    if ch < NCH - 1:
                        new = S_[(ch + 1) % 2]
                        add = GV[:, ch, :]
                        if ch:
                            step(v.tensor_tensor(St[:, :].rearrange("p (q i) -> p q i", q=4),
                                                 S_[ch % 2][:, :].rearrange("p (q i) -> p q i", q=4),
                                                 wend[:, q4, ch:ch + 1].broadcast_to([128, 4, 64]), ALU.mult))
                            step(v.tensor_tensor(St[:, :], St[:, :], GV[:, ch, :], ALU.add))
                            add = St[:, :]
                        dve.wait_ge(s_dsm, 8 * half + ch + 1)
                        v.tensor_tensor(new[:, :], add, PS[:, 5, 0:256], ALU.add).then_inc(s_s, 1)
                        dve.wait_ge(s_s, 8 * half + ch + 1)
                    if ch:
                        dve.wait_ge(s_ysm, 8 * half + ch)
                        ks = K_[:, q4, ch * CH:ch * CH + CH]
                        v.tensor_tensor(ks, ks, PS[:, 6 + ch % 2, 0:4 * CH].rearrange("p (q t) -> p q t", q=4),
                                        ALU.add).then_inc(s_yse, 1)
                dve.wait_ge(s_yse, 8 * half + 8)
                for p in range(4):
                    dve.wait_ge(s_ym, 4 * half + p + 1)
                    c = 4 * half + p
                    v.tensor_tensor(K_[:, c, :], K_[:, c, :], PS[:, p % 2, 0:TP], ALU.add).then_inc(s_yc, 1)

            dve.wait_ge(s_yc, KC)
            for c in range(KC):
                dve.wait_ge(s_mum, c + 1)
                v.scalar_tensor_tensor(R_[:, c, 0:T], PS[:, 4 + c % 2, 0:T], -1 / HD, K_[:, c, 0:T],
                                       ALU.mult, ALU.add).then_inc(s_yc2, 1)
            for c in range(KC):
                dve.wait_ge(s_vm, c + 1)
                v.tensor_scalar(B_[:, c, 0:T], PS[:, 6 + c % 2, 0:T], 1 / HD, LN_EPS, ALU.mult, ALU.add).then_inc(s_bv, 1)
            dve.wait_ge(s_bvr, 1)
            step(v.reciprocal(B_[:, :, 0:T], B_[:, :, 0:T]))
            for c in range(KC):
                step.do(v.scalar_tensor_tensor(R_[:, c, 0:T], R_[:, c, 0:T], col(VEC["lnx_g"] + c), B_[:, c, 0:T],
                                               ALU.mult, ALU.mult))
            step.sync()
            for c in range(KC):
                step.do(v.scalar_tensor_tensor(R_[:, c, 0:T], R_[:, c, 0:T], col(VEC["lnx_b"] + c), bonus[:, c, :],
                                               ALU.add, ALU.add))
            step.sync()
            for g in range(4):
                G = G0["g2"] + g
                if g < 3:
                    dve.wait_ge(s_part, 7 + g + 1)
                else:
                    dve.wait_ge(s_unit, 2 * (U0["g2"] + 1))
                v.tensor_tensor(V_[:, 2 * g:2 * g + 2, 0:T], PS[:, bank(G):bank(G) + 2, 0:T],
                                R_[:, 2 * g:2 * g + 2, 0:T], ALU.mult).then_inc(s_free, 1)
            dve.wait_ge(s_free, G0["g2"] + 4)
            split_input("ro", 1, lambda k: V_[:, k, 0:T], T)
            residual("rk_o", T, 2, 1, 1.0, "f1", gain["f1"], "f1")
            swiglu("f1")

            residual("f1_dn", T, 1, 2, 0.5, "f2", gain["f2"], "f2")
            swiglu("f2")
            residual("f2_dn", T, 1, 2, 0.5, "at", None, None)
            rms("at", T)
            for c in range(KC):
                v.scalar_tensor_tensor(at_in[:, c, :], h[:, c, :], col(norm_col(1, 1) + c), rstd[:, :],
                                       ALU.mult, ALU.mult).then_inc(s_xm, 1)
            split_input("at", 0, lambda k: at_in[:, k, :], T)
            for name, c0 in (("at_q", 0), ("at_k", 8), ("at_qi", 12), ("at_tail", 16)):
                for u in range(UN[name]):
                    drain2(name, u, rawq[:, c0 + 2 * u:c0 + 2 * u + 2, :])
            U, G = U0["at_v"], G0["at_v"]
            dve.wait_ge(s_unit, 2 * (U + 1))
            step.do(v.tensor_copy(vt[:, 0:2, :], PS[0:BLK, bank(G), 0:512].rearrange("p (b f) -> p b f", b=2)))
            v.tensor_copy(vt[0:T - 2 * BLK, 2, :], PS[0:T - 2 * BLK, bank(G) + 1, 0:256]).then_inc(s_free, 1)
            dve.wait_ge(s_free, G + 1)
            dve.wait_ge(s_dsc, 48)
            head_norms("at")
            dve.wait_ge(s_wtm, 1)
            v.tensor_scalar(wit[:, :, :], PS[:, 0, 0:16].rearrange("p (b f) -> p b f", b=2),
                            float(8 ** -0.5 * 64 ** -0.5), None, ALU.mult).then_inc(s_wt, 1)
            dve.wait_ge(s_wt, 1)
            for b in range(2):
                nk = META + 128 * (b + 1)
                for hd in range(8):
                    n = b * 8 + hd
                    dve.wait_ge(s_rl, n + 1)
                    if hd == 0:
                        ins = v.tensor_scalar(score[:, b, 0:nk], rel[:, n % 2, 0:nk], wit[:, b, 0:1], None, ALU.mult)
                    else:
                        ins = v.scalar_tensor_tensor(score[:, b, 0:nk], rel[:, n % 2, 0:nk], wit[:, b, hd:hd + 1],
                                                     score[:, b, 0:nk], ALU.mult, ALU.add)
                    ins.then_inc(s_ra, 1)
                    dve.wait_ge(s_ra, n + 1)
            for b in range(2):
                nk = META + 128 * (b + 1)
                step(v.tensor_tensor(taken[0][:, b, 0:nk], score[:, b, 0:nk], cap[:, b, 0:nk], ALU.min))
                for rnd in range(TOPK // 8):
                    src, dst = taken[rnd % 2][:, b, 0:nk], taken[(rnd + 1) % 2][:, b, 0:nk]
                    step(v.max(m8[:, :], src))
                    step(v.match_replace(dst, m8[:, :], src, TAKEN))
                step(v.tensor_scalar(taken[0][:, b, 0:nk], taken[0][:, b, 0:nk], TAKEN, 1.0, ALU.is_equal, ALU.subtract))
                step(v.scalar_tensor_tensor(taken[0][:, b, 0:nk], taken[0][:, b, 0:nk], -NEG, cap[:, b, 0:nk],
                                            ALU.mult, ALU.min))
            attention("at")
            dve.wait_ge(s_ol, 32)
            residual("at_o", SEQ, 2, 1, 1.0, "f3", gain["f3"], "f3")
            swiglu("f3")

            residual("f3_dn", SEQ, 1, 2, 0.5, "b", None, None)
            rms("b", SEQ)
            for c in range(KC):
                v.scalar_tensor_tensor(b_in[:, c, :], hv(SEQ, c)[:, 0, :], col(VEC["norm_mix"] + c), rstd[:, 0:SEQ],
                                       ALU.mult, ALU.mult).then_inc(s_xm, 1)
            split_input("b", 0, lambda k: b_in[:, k, :], SEQ)
            dve.wait_ge(s_bc, 96)
            step(v.tensor_copy(posf[:, :], posi[:, :]))
            step(v.tensor_scalar(ang[:, :], posf[:, :], freq[:, 0:1], None, ALU.mult))
            for n, (turn, shift) in enumerate(((0.25, math.pi / 2), (0.0, 0.0))):
                step(v.tensor_scalar(posf[:, :], ang[:, :], 1 / (2 * math.pi), turn, ALU.mult, ALU.add))
                step(v.tensor_scalar(posf[:, :], posf[:, :], MAGIC, None, ALU.add))
                step(v.tensor_scalar(posf[:, :], posf[:, :], MAGIC, None, ALU.subtract))
                step(v.scalar_tensor_tensor(red[:, :], posf[:, :], -C1, ang[:, :], ALU.mult, ALU.add))
                for part in (C2, C3):
                    step(v.scalar_tensor_tensor(red[:, :], posf[:, :], -part, red[:, :], ALU.mult, ALU.add))
                step(v.tensor_scalar(red[:, :], red[:, :], shift, PI, ALU.add, ALU.min))
                v.tensor_scalar(cs_b[:, n, :], red[:, :], -PI, None, ALU.max).then_inc(s_ang, 1)
            dve.wait_ge(s_sin, 2)
            step(v.tensor_scalar(cs_b[:, 1, :], cs_b[:, 1, :], freq[:, 1:2], None, ALU.mult))
            for name, c0 in (("b_qa", 0), ("b_ka", 4)):
                for u in range(2):
                    drain2(name, u, qka[:, c0 + 2 * u:c0 + 2 * u + 2, :], n=SEQ)
            for u in range(2):
                drain2("b_va", u, vat[:, :, u * 256:u * 256 + 256], n=256)
            for u in range(3):
                drain2("b_cq", u, craw[:, 2 * u:2 * u + 2, :], n=SEQ)
            drain2("b_ckv", 0, craw[:, 6:8, :], n=SEQ)
            U, G = U0["b_tail"], G0["b_tail"]
            dve.wait_ge(s_unit, 2 * (U + 1))
            v.tensor_copy(krope[64:96, :], PS[64:96, bank(G), 0:SEQ]).then_inc(s_free, 1)
            dve.wait_ge(s_free, G + 1)
            for hd in range(8):
                dve.wait_ge(s_bwm, hd + 1)
                v.tensor_copy(biasw[:, hd, :], PS[:, 4 + hd % 2, 0:384]).then_inc(s_bw, 1)
            for k in range(8):
                dve.wait_ge(s_csq, k + 1)
                n = 0 if k < 6 else 1
                if k in (0, 6):
                    ins = v.tensor_copy(bt[:, n, :], csq[:, k, :])
                else:
                    ins = v.tensor_tensor(bt[:, n, :], bt[:, n, :], csq[:, k, :], ALU.add)
                ins.then_inc(s_css, 1)
                dve.wait_ge(s_css, k + 1)
            for n, width in enumerate((768, 256)):
                dve.wait_ge(s_cnm, n + 1)
                v.tensor_scalar(cvr[:, n, :], PS[:, 6 + n, 0:SEQ], 1 / width, EPS, ALU.mult, ALU.add).then_inc(s_cv, 1)
            dve.wait_ge(s_cst, 2)
            step(v.reciprocal(cvr[:, :, :], cvr[:, :, :]))
            for k in range(8):
                g = VEC["cq_g"] + k if k < 6 else VEC["ckv_g"] + k - 6
                v.scalar_tensor_tensor(cxf[:, k, :], craw[:, k, :], col(g), cvr[:, 0 if k < 6 else 1, :],
                                       ALU.mult, ALU.mult).then_inc(s_xm, 1)
            split_input("cq", 1, lambda k: cxf[:, k, :], SEQ, range(8))
            for u in range(4):
                drain2("b_uq", u, qkb[:, 2 * u:2 * u + 2, :], slice(0, 96), SEQ)
            for hd in range(8):
                step.do(v.tensor_copy(qkb[64:96, 8 + hd, :], krope[64:96, :]))
            for g in range(2):
                G = G0["b_ukv"] + g
                dve.wait_ge(s_part, 10 + g + 1)
                pair = qkb[0:64, 8 + 4 * g:12 + 4 * g, :].rearrange("p (a e) t -> p a e t", e=2)
                step.do(v.tensor_copy(pair[:, :, 0, :], PS[0:64, bank(G):bank(G) + 2, 0:SEQ]))
                v.tensor_copy(pair[:, :, 1, :], PS[64:128, bank(G):bank(G) + 2, 0:SEQ]).then_inc(s_free, 1)
            U, G = U0["b_ukv"], G0["b_ukv"] + 2
            dve.wait_ge(s_unit, 2 * (U + 1))
            v.tensor_copy(vbt[:, :, :], PS[:, bank(G):bank(G) + 2, 0:512]).then_inc(s_free, 1)
            dve.wait_ge(s_free, G + 1)
            head_norms("b")
            dve.wait_ge(s_hsc, NT0["b"] + 12)
            dve.wait_ge(s_bld, 128)
            attention("b")
            dve.wait_ge(s_ol, 64)
            residual("b_o", SEQ, 2, 1, 1.0, "ff", VEC["norm_ffn"], "ff")

            def ff1(us, i):
                us = list(us)

                def tail(u):
                    dve.wait_ge(s_hf2, val(u + 1, i, 4))
                    o = slice(2 * u * SEQ, 2 * u * SEQ + 2 * SEQ) if i is None else bass.ds(i * (8 * SEQ) + 2 * u * SEQ, 2 * SEQ)
                    low(hid2_l[:, o], hidf2[:, u % 2, :, :].rearrange("p m n -> p (m n)"), hid2_h[:, o], s_hlo2)
                for k, u in enumerate(us):
                    U, G = U0["b_ff1"] + u, G0["b_ff1"] + u
                    dve.wait_ge(s_unit, val(2 * (U + 1), i, 8))
                    if u == 0:
                        rms("ff", SEQ)
                    v.scalar_tensor_tensor(act2[:, u % 2, :, :], PS[:, bank(G):bank(G) + 2, 0:SEQ], 0.0,
                                           rstd[:, 0:SEQ].unsqueeze(1).broadcast_to([128, 2, SEQ]),
                                           ALU.max, ALU.mult).then_inc(s_free, 1)
                    if k:
                        tail(u - 1)
                tail(us[-1])
            ff1(range(4), None)
            with step.loop(3, 0) as i:
                ff1(range(4, 8), i)
            for m in range(KC):
                U, G = U0["b_ff2"] + 2 * m + 1, G0["b_ff2"] + m
                dve.wait_ge(s_unit, 2 * (U + 1))
                v.tensor_tensor(outt[:, m, :], PS[:, bank(G), 0:SEQ], hv(SEQ, m)[:, 0, :], ALU.add).then_inc(s_free, 1)

        @block.scalar
        def _(act):
            a = nc.scalar
            step = Link(act, s_act)
            widths = [w for _n, n, _m, w in STAGES for _ in range(n)]

            def f(out, in_, func, **kw):
                return a.activation(out, in_, func, **kw)

            def hi(U, i=None, k=4, w=None):
                if U >= UNITS:
                    return
                w = widths[U] if w is None else w
                act.wait_ge(s_raw[U % RAW], val(16 * (U // RAW + 1), i, 4 * k))
                for q, part in enumerate(halves(w)):
                    if U >= SPL:
                        act.wait_ge(s_unit, val(2 * (U - SPL) + q + 1, i, 2 * k))
                    f(whi[U % SPL][:, part], raw[U % RAW][:, part], ACT.Copy).then_inc(s_hi, 1)

            def ahead(name):
                for u in range(UN[name]):
                    hi(U0[name] + u + 1)

            def last_width(name, u):
                return max(UW[name], widths[U0[name] + UN[name]])

            def root(name, n):
                act.wait_ge(s_var, N0[name] + 1)
                f(rstd[:, 0:n], rstd[:, 0:n], ACT.Sqrt).then_inc(s_std, 1)

            def swiglu_in(fn):
                n, name, hb = tok[fn], fn + "_in", HB[fn]

                def high(u, i):
                    act.wait_ge(s_hid, val(hb + u + 1, i, 4))
                    o = slice(u * T, u * T + n) if i is None else bass.ds(i * (4 * T) + u * T, n)
                    f(hid_h[:, o], hidf[:, u % 2, 0:n], ACT.Copy).then_inc(s_hhi, 1)

                def body(us, i):
                    us = list(us)
                    for k, u in enumerate(us):
                        w = last_width(name, u) if u == us[-1] else UW[name]
                        hi(U0[name] + u + 1, i, 4, w)
                        if u == 0:
                            root(fn, n)
                        act.wait_ge(s_gate, val(hb + u + 1, i, 4))
                        f(sig[:, u % 2, 0:n], gate[:, u % 2, 0:n], ACT.Sigmoid).then_inc(s_sig, 1)
                        if k >= 1:
                            high(u - 1, i)
                    high(us[-1], i)
                turns(step, FC, 4, 0, body)

            def residual(name, n, w, units, norm, split):
                def body(js, i):
                    for j in js:
                        for k in range(units):
                            u = units * j + k + 1
                            ww = UW[name]
                            if i is not None and j == list(js)[-1] and k == units - 1:
                                ww = last_width(name, u)
                            hi(U0[name] + u, i, 4 * units, ww if i is not None else None)
                        G = G0[name] + j
                        act.wait_ge(s_free, val(G + 1, i, 4))
                        if j >= 2 or norm != "f0":
                            pass
                        x = hv(n, j * w, j * w + w) if i is None else h[:, bass.ds(i * 4 + j, 1), T - n:T]
                        f(sq[:, j % 2, 0:w, 0:n], x, ACT.Square).then_inc(s_sq, 1)
                        for q in range(w if split else 0):
                            m = j * w + q
                            act.wait_ge(s_xm, val(XM0[split] + m + 1, i, 4))
                            o = slice(m, m + 1) if i is None else bass.ds(i * 4 + m, 1)
                            f(xh[0][:, o, 0:n].rearrange("p o n -> p (o n)"), xg[:, j % 2, q, 0:n], ACT.Copy).then_inc(s_xh, 1)
                turns(step, 8 // w, 4, 0, body)

            def split_input(name, b, made, n, chunks=range(KC)):
                for k in chunks:
                    act.wait_ge(s_xm, XM0[name] + k + 1)
                    f(xh[b][:, k, 0:n], made(k), ACT.Copy).then_inc(s_xh, 1)

            def head_norms(which):
                tiles = [x for x in TILES[which] if x["norm"]]
                c0 = NT0[which]
                for j in range(len(tiles) + 1):
                    if j < len(tiles):
                        x, c = tiles[j], c0 + j + 1
                        r, n = slice(0, x["rows"]), x["n"]
                        if j >= 2:
                            act.wait_ge(s_hsum, c - 2)
                        f(sqp[c % 2][r, :, 0:n], x["x"], ACT.Square).then_inc(s_hsq, 1)
                    if j >= 1:
                        x, c = tiles[j - 1], c0 + j
                        r, n = slice(0, x["rows"]), x["n"]
                        act.wait_ge(s_hvar, c)
                        f(hvr[c % 2][r, :, 0:n], hvr[c % 2][r, :, 0:n], ACT.Sqrt).then_inc(s_hroot, 1)

            def attention(which):
                jobs, j0 = JOBS[which]
                for j in range(len(jobs) + 4):
                    if j < len(jobs):
                        x, c = jobs[j], j0 + j
                        nk = x["nk"]
                        act.wait_ge(s_lg, c + 1)
                        if j >= 2:
                            act.wait_ge(s_prn, c - 1)
                        f(pr[:, c % 2, 0:nk], lg[:, c % 2, 0:nk], ACT.Exp, bias=nmx[:, c:c + 1],
                          accum_out=asum[:, c:c + 1]).then_inc(s_ex, 1)
                    if 0 <= j - 2 < len(jobs):
                        x, c = jobs[j - 2], j0 + j - 2
                        act.wait_ge(s_ptm, c + 1)
                        if j - 2 >= 2:
                            act.wait_ge(s_om, c - 1)
                        nv = len(x["v"])
                        if which == "at":
                            short = x["v"][-1][2]
                            f(pts[0:BLK, c % 2, 0:nv - 1, :], PS[0:BLK, 2 + c % 2, 0:(nv - 1) * 128].rearrange(
                                "p (n q) -> p n q", q=128), ACT.Copy).then_inc(s_act, 1)
                            step.n += 1
                            f(pts[0:short, c % 2, nv - 1, :], PS[0:short, 2 + c % 2, (nv - 1) * 128:nv * 128],
                              ACT.Copy).then_inc(s_pte, 1)
                        else:
                            f(pts[:, c % 2, 0:nv, :], PS[:, 2 + c % 2, 0:nv * 128].rearrange("p (n q) -> p n q", q=128),
                              ACT.Copy).then_inc(s_pte, 1)
                    if 0 <= j - 3 < len(jobs):
                        x, c = jobs[j - 3], j0 + j - 3
                        r = slice(64 * (x["head"] % 2), 64 * (x["head"] % 2) + 64)
                        act.wait_ge(s_om, c + 1)
                        f(xh[1][r, x["head"] // 2, 128 * x["b"]:128 * x["b"] + 128], PS[r, 4 + c % 2, 0:128],
                          ACT.Copy).then_inc(s_oh, 1)

            act.dma_start(masks[:, :, :], t["scan"].rearrange("p (k s) -> p k s", s=BLK)).then_inc(s_rkc, 16)
            hi(0)
            act.wait_ge(s_h0, 16)
            for m in range(KC):
                if m >= 2:
                    act.wait_ge(s_ssa, m - 1)
                f(sq[:, m % 2, 0, :], h[:, m, :], ACT.Square).then_inc(s_sq, 1)
                act.wait_ge(s_xm, m + 1)
                f(xh[0][:, m, :], xg[:, (m // 2) % 2, m % 2, :], ACT.Copy).then_inc(s_xh, 1)
            swiglu_in("f0")
            residual("f0_dn", T, 1, 2, "rk", None)

            root("rk", T)

            def mixed(s):
                if s >= 2:
                    act.wait_ge(s_unit, 2 * U0[("rk_k", "rk_v", "lora_wa", "lora_g")[s - 2]])
                split_input(f"m{s}", s % 2, lambda k: xmf[:, k, :], T)
            mixed(0)
            mixed(1)
            ahead("rk_r")
            mixed(2)
            ahead("rk_k")
            mixed(3)
            ahead("rk_v")
            mixed(4)
            hi(U0["lora_wa"] + 1)
            act.wait_ge(s_lhd, 1)
            step(f(lh[0:64, :], lh[0:64, :], ACT.Tanh))
            act.wait_ge(s_free, G0["lora_wa"] + 1)
            f(lh_h[:, :], lh[:, :], ACT.Copy).then_inc(s_lhh, 1)
            mixed(5)
            hi(U0["lora_g"] + 1)
            act.wait_ge(s_free, G0["lora_g"] + 1)
            step(f(gh[:, :, :], gh[:, :, :], ACT.Sigmoid))
            f(gh_h[:, :, :], gh[:, :, :], ACT.Copy).then_inc(s_ghh, 1)
            hi(U0["wa2"] + 1)
            act.wait_ge(s_wa, KC)
            step(f(W_[:, :, 0:T], W_[:, :, 0:T], ACT.Sigmoid))
            act.wait_ge(s_free, G0["wa2"] + KC)
            step(f(a_g[:, :, :], a_g[:, :, :], ACT.Sigmoid))
            f(W_[:, :, 0:T], W_[:, :, 0:T], ACT.Exp, scale=-math.exp(-0.5)).then_inc(s_dec, 1)
            act.wait_ge(s_kk, KC)
            f(ktmp[:, :, 0:T], A_[:, :, 0:T], ACT.Square).then_inc(s_kksq, 1)
            for c in range(KC):
                act.wait_ge(s_kkm, c + 1)
                f(kden[:, c, :], PS[:, 4 + c % 2, 0:T], ACT.Sqrt).then_inc(s_kkr, 1)
            for half in range(2):
                for p in range(4):
                    c = 4 * half + p
                    for n, dst in enumerate((atok[:, :, :], btok[:, :, p * 128:p * 128 + 128])):
                        act.wait_ge(s_tr, 4 * c + n + 1)
                        f(dst, PS[0:BLK, n, 0:384].rearrange("p (b f) -> p b f", b=NB), ACT.Copy).then_inc(s_tka, 1)
                    for lv in range(4):
                        for e in range(2):
                            act.wait_ge(s_q, (c * 4 + lv) * 2 + e + 1)
                            f(QQ[e][:, :], PS[0:BLK, e, 0:TP], ACT.Copy).then_inc(s_qc, 1)
                    act.wait_ge(s_p1, c + 1)
                    f(p1[:, :, :], PS[0:BLK, 6, 0:384].rearrange("p (b f) -> p b f", b=NB), ACT.Copy).then_inc(s_p1c, 1)
                    act.wait_ge(s_ztm, c + 1)
                    f(A_[:, c, :], PS[:, 0, 0:TP], ACT.Copy).then_inc(s_zt, 1)
                    act.wait_ge(s_gvm, c + 1)
                    f(GV[:, :, p * 64:p * 64 + 64].rearrange("q (b j) i -> q j b i", j=3),
                      PS[:, 2:5, 0:192].rearrange("q j (b i) -> q j b i", i=64),
                      ACT.Copy).then_inc(s_gv, 1)
            for c in range(KC):
                act.wait_ge(s_yc2, c + 1)
                f(A_[:, c, 0:T], R_[:, c, 0:T], ACT.Square).then_inc(s_ysq, 1)
            act.wait_ge(s_bv, KC)
            f(B_[:, :, 0:T], B_[:, :, 0:T], ACT.Sqrt).then_inc(s_bvr, 1)
            hi(U0["g2"] + 1)
            for k in range(KC):
                act.wait_ge(s_free, G0["g2"] + k // 2 + 1)
                f(xh[1][:, k, :], V_[:, k, 0:T], ACT.Copy).then_inc(s_xh, 1)
            residual("rk_o", T, 2, 1, "f1", "f1")
            swiglu_in("f1")

            residual("f1_dn", T, 1, 2, "f2", "f2")
            swiglu_in("f2")
            residual("f2_dn", T, 1, 2, "at", None)
            for dst, name in ((rot_a[:, :], "rot_a"), (cs_a[:, :, :], "cs_a"), (cap[:, :, :], "cap")):
                src = t[name] if name == "rot_a" else t[name].rearrange("p (c n) -> p c n", c=2)
                act.dma_start(dst, src).then_inc(s_dsc, 16)
            root("at", T)
            split_input("at", 0, lambda k: at_in[:, k, :], T)
            for name in ("at_q", "at_k", "at_qi", "at_tail", "at_v"):
                ahead(name)
            act.wait_ge(s_free, G0["at_v"] + 1)
            head_norms("at")
            for n in range(16):
                nk = META + 128 * (n // 8 + 1)
                act.wait_ge(s_rlm, n + 1)
                if n >= 2:
                    act.wait_ge(s_ra, n - 1)
                f(rel[:, n % 2, 0:nk], PS[:, 2 + n % 2, 0:nk], ACT.Relu).then_inc(s_rl, 1)
            attention("at")
            residual("at_o", SEQ, 2, 1, "f3", "f3")
            swiglu_in("f3")

            residual("f3_dn", SEQ, 1, 2, "b", None)
            for dst, name in ((causal, "causal"), (rot_b, "rot_b"), (freq, "freq"), (distt, "dist")):
                act.dma_start(dst[:, :], t[name]).then_inc(s_bc, 16)
            act.dma_start(relb[:, :, :], t["relb"]).then_inc(s_bc, 16)
            act.dma_start(posi[:, :], t["pos"].broadcast_to([128, SEQ])).then_inc(s_bc, 16)
            root("b", SEQ)
            split_input("b", 0, lambda k: b_in[:, k, :], SEQ)
            for n in range(2):
                act.wait_ge(s_ang, n + 1)
                f(cs_b[:, n, :], cs_b[:, n, :], ACT.Sin).then_inc(s_sin, 1)
            for name in ("b_qa", "b_ka", "b_va", "b_cq", "b_ckv", "b_tail"):
                ahead(name)
            for k in range(8):
                if k == 0:
                    act.wait_ge(s_free, G0["b_tail"] + 1)
                f(csq[:, k, :], craw[:, k, :], ACT.Square).then_inc(s_csq, 1)
            for n in range(2):
                act.wait_ge(s_cv, n + 1)
                f(cvr[:, n, :], cvr[:, n, :], ACT.Sqrt).then_inc(s_cst, 1)
            split_input("cq", 1, lambda k: cxf[:, k, :], SEQ, range(8))
            act.wait_ge(s_bw, 8)
            act.dma_start(t["rows"].rearrange("(p w) -> p w", p=128), biasw[:, :, :].rearrange("p h x -> p (h x)")
                          ).then_inc(s_bst, 16)
            for name in ("b_uq", "b_ukv"):
                ahead(name)
            act.wait_ge(s_bst, 16)
            pitch = 8 * 384 - 1
            skewed = t["rows"][127:127 + 128 * pitch].rearrange("(p w) -> p w", w=pitch)
            for hd in range(8):
                act.dma_start(bias[:, hd, :], skewed[:, hd * 384:hd * 384 + 256]).then_inc(s_bld, 16)
            act.wait_ge(s_free, G0["b_ukv"] + 3)
            head_norms("b")
            attention("b")
            residual("b_o", SEQ, 2, 1, "ff", "ff")

            def ff1(us, i):
                for u in us:
                    hi(U0["b_ff1"] + u + 1, i, 4, 2048)
                    if u == 0:
                        root("ff", SEQ)
                    act.wait_ge(s_free, val(G0["b_ff1"] + u + 1, i, 4))
                    step.do(f(hidf2[:, u % 2, :, :], act2[:, u % 2, :, :], ACT.Square))
                    o = slice(2 * u * SEQ, 2 * u * SEQ + 2 * SEQ) if i is None else bass.ds(i * (8 * SEQ) + 2 * u * SEQ, 2 * SEQ)
                    f(hid2_h[:, o], act2[:, u % 2, :, :].rearrange("p m n -> p (m n)"), ACT.Square).then_inc(s_hf2, 1)
            ff1(range(4), None)
            with step.loop(3, 4) as i:
                ff1(range(4, 8), i)
            for u in range(16):
                hi(U0["b_ff2"] + u + 1)


def tiles(w, cols):
    k, n = w.shape[0] // 128, w.shape[1] // cols
    return np.ascontiguousarray(w.reshape(k, 128, n, cols).transpose(2, 1, 0, 3)).reshape(n, 128, k * cols)


def pairs(w):
    n = w.shape[1] // 256
    x = w.reshape(KC, 128, n, 2, 128).transpose(2, 1, 3, 0, 4)
    return np.ascontiguousarray(x).reshape(n, 128, 2048)


def down_units(w, parts):
    k = w.shape[0] // 128 // parts
    x = w.reshape(parts, k, 128, 8, 128).transpose(3, 0, 2, 1, 4)
    return np.ascontiguousarray(x).reshape(8 * parts, 128, k * 128)


def columns(x):
    return x.reshape(-1, 128).T


def layout(inp):
    f = {k: np.asarray(v) for k, v in inp.items()}
    out = {}
    x = np.concatenate([f["meta"], f["x"][0]], 0)
    out["h0"] = np.ascontiguousarray(x.T.reshape(KC, 128, T).transpose(1, 0, 2))
    for i in range(4):
        w = f["ffn_w_in"][i // 2, i % 2]
        w = w.reshape(D, 2, FC, 128).transpose(0, 2, 1, 3).reshape(D, 2 * FF)
        out[f"w_f{i}_in"] = pairs(w)
        out[f"w_f{i}_dn"] = down_units(f["ffn_w_out"][i // 2, i % 2], 2)
    for name in "rkvo":
        out["w_rk_" + name] = pairs(f["rk_w_" + name][0])
    out["w_lora_wa"] = tiles(np.concatenate([f["rk_w1"][0], f["rk_a1"][0]], 1), 128)
    out["w_lora_g"] = tiles(f["rk_g1"][0], 160)
    out["w_wa2"] = np.concatenate([f["rk_w2"][0], f["rk_a2"][0]], 0)[None]
    g2 = np.zeros((1, 128, 2, D), np.float32)
    g2[0, 0:80] = f["rk_g2"][0].reshape(2, 80, D).transpose(1, 0, 2)
    out["w_g2"] = g2.reshape(1, 128, 2 * D)
    w = f["at_w_in"][0]
    out["w_at_q"] = pairs(w[:, 0:1024])
    k = w[:, 1024:1280].reshape(D, 4, 1, 64)
    out["w_at_k"] = pairs(np.concatenate([k, k], 2).reshape(D, 512))
    out["w_at_v"] = tiles(w[:, 1280:1536], 256)
    out["w_at_qi"] = pairs(w[:, 1536:2048])
    ki, wi = w[:, 2048:2112], w[:, 2112:2120]
    out["w_at_tail"] = pairs(np.concatenate([ki, ki, wi, np.zeros((D, 120), np.float32)], 1))
    out["w_at_o"] = pairs(f["at_w_o"][0])
    w = f["w_in_2"]
    out["w_b_qa"], out["w_b_ka"] = pairs(w[:, 0:512]), pairs(w[:, 512:1024])
    out["w_b_va"], out["w_b_cq"] = tiles(w[:, 1024:1536], 256), pairs(w[:, 1536:2304])
    out["w_b_ckv"] = pairs(w[:, 2304:2560])
    z = np.zeros((D, 64), np.float32)
    out["w_b_tail"] = tiles(np.concatenate([z, w[:, 2560:2592], z[:, 0:32]], 1), 128)
    out["w_b_uq"] = tiles(f["w_uq_2"], 192)
    kv = f["w_ukv_2"].reshape(256, 8, 128)
    out["w_b_ukv"] = tiles(np.concatenate([kv[:, :, 0:64].reshape(256, 512), kv[:, :, 64:].reshape(256, 512)], 1), 1024)
    out["w_b_o"] = pairs(f["w_o_2"])
    out["w_b_ff1"] = pairs(f["w_ff1_2"])
    out["w_b_ff2"] = down_units(f["w_ff2_2"], 2)
    vecs = [f["norm_g"], f["rk_mix"], f["rk_w0"], f["rk_a0"], f["rk_k_k"], f["rk_k_a"], f["rk_r_k"],
            f["rk_lnx_g"], f["rk_lnx_b"], f["norm_mix_g_2"], f["norm_ffn_g_2"], f["cq_norm_g_2"], f["ckv_norm_g_2"]]
    vecs += [np.concatenate([f[n].reshape(-1)] * 2) for n in ("at_q_g", "at_k_g", "qnorm_a_g_2", "knorm_a_g_2")]
    vecs += [np.concatenate([f[n], np.zeros(32, np.float32)]) for n in ("qnorm_b_g_2", "knorm_b_g_2")]
    out["vec"] = np.ascontiguousarray(np.concatenate([columns(x) for x in vecs], 1))
    rb = np.concatenate([f["rel_bias_2"], np.ones((1, 8), np.float32)], 0)
    out["relb"] = np.ascontiguousarray(np.repeat(rb[:, :, None], 128, 2))
    out["pos"] = f["positions_2"].reshape(1, SEQ)
    out.update(shape_constants())
    return {k: np.ascontiguousarray(x) for k, x in out.items()}


def kernel(**inputs):
    import concourse.bacc as bacc
    from concourse.bass_utils import run_bass_kernel_spmd

    nc = bacc.Bacc("TRN2", target_bir_lowering=False, num_devices=1)
    arrays = layout(inputs)
    t = {}
    for name, x in arrays.items():
        t[name] = nc.dram_tensor(name + "_in", x.shape, mybir.dt.from_np(x.dtype), kind="ExternalInput").ap()
    t["out"] = nc.dram_tensor("result", [128, KC, SEQ], F32, kind="ExternalOutput").ap()
    t["rows"] = nc.dram_tensor("bias_rows_scratch", [128 * 8 * 384], F32, kind="Internal").ap()
    build(nc, t)
    r = run_bass_kernel_spmd(nc, [{n + "_in": x for n, x in arrays.items()}], core_ids=[0])
    y = r.results[0]["result"]
    return y.transpose(2, 1, 0).reshape(1, SEQ, D)
```

```python
import math
from contextlib import ExitStack, contextmanager

import numpy as np

import concourse.bass as bass
from concourse import mybir

F32 = mybir.dt.float32
F32R = mybir.dt.float32r
I32 = mybir.dt.int32
ALU = mybir.AluOpType
ACT = mybir.ActivationFunctionType
AX = mybir.AxisListType

D = 1024
KC = D // 128
META = 16
SEQ = 256
T = META + SEQ
FF = 2816
FC = FF // 128
FF2 = 4096
HD = 64
EPS = 1e-6
LN_EPS = 64e-5
H_A = 16
TOPK = 64
BLK = 96
CH = 32
NCH = 9
NB = 3
TP = NB * BLK
NEG = -1.0e30
CAP = 3.0e38
TAKEN = -3.4e38

STAGES = [
    ("f0_in", 22, 22, 2048), ("f0_dn", 16, 8, 1408),
    ("rk_r", 4, 4, 2048), ("rk_k", 4, 4, 2048), ("rk_v", 4, 4, 2048),
    ("lora_wa", 1, 1, 1024), ("lora_g", 1, 1, 1280), ("wa2", 1, 8, 1024),
    ("g2", 1, 4, 2048), ("rk_o", 4, 4, 2048),
    ("f1_in", 22, 22, 2048), ("f1_dn", 16, 8, 1408),
    ("f2_in", 22, 22, 2048), ("f2_dn", 16, 8, 1408),
    ("at_q", 4, 4, 2048), ("at_k", 2, 2, 2048), ("at_qi", 2, 2, 2048), ("at_tail", 1, 1, 2048),
    ("at_v", 1, 1, 2048), ("at_o", 4, 4, 2048),
    ("f3_in", 22, 22, 2048), ("f3_dn", 16, 8, 1408),
    ("b_qa", 2, 2, 2048), ("b_ka", 2, 2, 2048), ("b_va", 2, 2, 2048), ("b_cq", 3, 3, 2048),
    ("b_ckv", 1, 1, 2048), ("b_tail", 1, 1, 1024), ("b_uq", 4, 4, 1152), ("b_ukv", 1, 3, 2048),
    ("b_o", 4, 4, 2048), ("b_ff1", 16, 16, 2048), ("b_ff2", 16, 8, 2048),
]
U0, G0, UN, GN, UW = {}, {}, {}, {}, {}
_u = _g = 0
for _name, _n, _m, _w in STAGES:
    U0[_name], G0[_name], UN[_name], GN[_name], UW[_name] = _u, _g, _n, _m, _w
    _u += _n
    _g += _m
UNITS = _u

RAW = 4
SPL = 2


def halves(w):
    cut = 1024 if w > 1024 else w // 2
    return (slice(0, cut), slice(cut, w))

VEC = {}
_c = 0
for _name, _n in [("norm_g", 48), ("rk_mix", 48), ("w0", 8), ("a0", 8), ("k_k", 8), ("k_a", 8),
                  ("r_k", 8), ("lnx_g", 8), ("lnx_b", 8), ("norm_mix", 8), ("norm_ffn", 8),
                  ("cq_g", 6), ("ckv_g", 2), ("q_g", 1), ("k_g", 1), ("qa_g", 1), ("ka_g", 1),
                  ("qb_g", 1), ("kb_g", 1)]:
    VEC[_name] = _c
    _c += _n
NVEC = _c

LEVELS = (2, 4, 8, 16)


def norm_col(layer, which):
    return VEC["norm_g"] + (layer * 3 + which) * KC


def shape_constants():
    c = {}
    c["ident"] = np.eye(128, dtype=np.float32)
    c["ones"] = np.ones((128, 128), np.float32)
    half = np.arange(128) // 64
    c["bo64"] = (half[:, None] == half[None, :]).astype(np.float32)
    c["sel"] = np.zeros((128, 88), np.float32)
    c["sel"][np.arange(128), 30 + half] = 1.0
    c["sel"][:96, 56 + 15] = 1.0
    s = np.arange(BLK)
    same = (s[:, None] // CH) == (s[None, :] // CH)
    strict_t = same & (s[:, None] < s[None, :])
    m = [strict_t, strict_t.T, same & (s[:, None] <= s[None, :])]
    lvl = []
    for size in (1,) + LEVELS:
        lo = (s[:, None] // (2 * size) == s[None, :] // (2 * size)) & \
             (s[:, None] // size % 2 == 1) & (s[None, :] // size % 2 == 0)
        lvl.append(lo)
    m += [lvl[0], lvl[0].T] + [x.T for x in lvl[1:]] + [np.eye(BLK, dtype=bool)]
    scan = np.stack([x.astype(np.float32) for x in m], 1)
    c["scan"] = np.zeros((128, 10 * BLK), np.float32)
    c["scan"][:BLK] = scan.reshape(BLK, -1)
    rot = np.zeros((128, 128), np.float32)
    for b in (0, 64):
        for i in range(8):
            rot[b + i + 8, b + i] = 1.0
            rot[b + i, b + i + 8] = 1.0
    c["rot_a"] = rot
    inv = (np.float32(500000.0) ** (-np.arange(0, 16, 2, dtype=np.float32) / np.float32(16))).astype(np.float32)
    ang = np.arange(T, dtype=np.float32)[:, None] * inv[None, :]
    cs, sn = np.cos(ang).astype(np.float32).T, np.sin(ang).astype(np.float32).T
    ct, st = np.ones((128, T), np.float32), np.zeros((128, T), np.float32)
    for b in (0, 64):
        ct[b:b + 8] = cs
        ct[b + 8:b + 16] = cs
        st[b:b + 8] = -sn
        st[b + 8:b + 16] = sn
    c["cs_a"] = np.concatenate([ct, st], 1)
    cap = np.full((128, 2, T), CAP, np.float32)
    for b in range(2):
        q = META + 128 * b + np.arange(128)
        cap[:, b][np.arange(T)[None, :] > q[:, None]] = -CAP
    c["cap"] = cap.reshape(128, 2 * T)
    rb = np.zeros((128, 96), np.float32)
    for i in range(16):
        rb[64 + i + 16, 64 + i] = 1.0
        rb[64 + i, 64 + i + 16] = 1.0
    c["rot_b"] = rb
    invb = (np.float32(1.0) / (np.float32(10000.0) ** (np.arange(0, 32, 2, dtype=np.float32) / np.float32(32)))).astype(np.float32)
    fr = np.zeros((128, 2), np.float32)
    fr[64:80, 0] = invb
    fr[80:96, 0] = invb
    fr[64:80, 1] = -1.0
    fr[80:96, 1] = 1.0
    c["freq"] = fr
    k = np.arange(256)[None, :] - 128 - np.arange(128)[:, None]
    c["causal"] = np.where(k > 0, np.float32(NEG), np.float32(0)).astype(np.float32)
    dist = 255 - np.arange(384)
    safe = np.maximum(np.maximum(dist, 0), 1).astype(np.float32)
    large = 16 + (np.log(safe / 16) / math.log(2048 / 16) * 16).astype(np.int64)
    large = np.minimum(large, 31)
    bucket = np.where(np.maximum(dist, 0) < 16, np.maximum(dist, 0), large)
    oh = np.zeros((33, 384), np.float32)
    oh[bucket, np.arange(384)] = 8.0
    times = (dist <= 128).astype(int) + (dist % 4 == 0) + (dist % 16 == 0)
    oh[32] = np.where((dist >= 0) & (times > 0), 8.0 * np.log(np.maximum(times, 1)), NEG)
    c["dist"] = oh
    return c


class Link:

    def __init__(self, eng, sem):
        self.eng, self.sem, self.n, self.i, self.per = eng, sem, 0, None, 0

    def value(self):
        return self.n if self.i is None else self.i * self.per + self.n

    def do(self, ins):
        ins.then_inc(self.sem, 1)
        self.n += 1

    def sync(self):
        self.eng.wait_ge(self.sem, self.value())

    def __call__(self, ins):
        self.do(ins)
        self.sync()

    @contextmanager
    def loop(self, times, per):
        first = self.n
        with self.eng.Fori(0, times) as i:
            self.i, self.per = i, per
            yield i
            assert self.n - first == per, f"steps {self.n - first}, not {per}"
        self.i = None
        self.n = first + per * times


def val(c, i, k):
    return c if i is None else i * k + c


def turns(link, n, per, steps, body, at_least=0):
    peel = n % per
    while peel < at_least:
        peel += per
    if peel:
        body(range(peel), None)
    if n - peel == per:
        body(range(peel, n), None)
    elif n > peel:
        with link.loop((n - peel) // per, steps) as i:
            body(range(peel, peel + per), i)



SPLITS = [("f0", 8), ("m0", 8), ("m1", 8), ("m2", 8), ("m3", 8), ("m4", 8), ("m5", 8), ("ro", 8),
          ("f1", 8), ("f2", 8), ("at", 8), ("f3", 8), ("b", 8), ("cq", 6), ("ckv", 2), ("ff", 8)]
X0, XM0 = {}, {}
_x = _m = 0
for _name, _n in SPLITS:
    X0[_name], XM0[_name] = _x, _m
    _x += _n
    _m += 0 if _name == "ro" else _n
NORMS = [("f0", 8), ("rk", 8), ("f1", 4), ("f2", 8), ("at", 8), ("f3", 4), ("b", 8), ("ff", 4)]
Q0, N0 = {}, {}
_q = 0
for _i, (_name, _n) in enumerate(NORMS):
    Q0[_name], N0[_name] = _q, _i
    _q += _n


def build(nc, t):
    ctx = ExitStack()
    with ctx:
        used = [0]

        class Region:

            def __init__(self, start):
                self.here = start

            def __call__(self, name, shape, dtype=F32):
                size = 4 * int(np.prod(shape[1:]))
                x = nc.alloc_sbuf_tensor_at(name, shape, dtype, offset=self.here)
                self.here += (size + 31) // 32 * 32
                used[0] = max(used[0], self.here)
                return x

        def sem(name):
            return ctx.enter_context(nc.semaphore(name))

        keep = Region((nc.sbuf_base + 63) // 32 * 32)
        keep_at = keep.here
        raw = [keep(f"raw{i}", [128, 2048]) for i in range(RAW)]
        whi = [keep(f"whi{i}", [128, 2048], F32R) for i in range(SPL)]
        wlo = [keep(f"wlo{i}", [128, 2048], F32R) for i in range(SPL)]
        h = keep("h", [128, KC, T])
        ident = keep("ident", [128, 128])
        ones = keep("ones", [128, 128])
        bo64 = keep("bo64", [128, 128])
        sel = keep("sel", [128, 88])
        vec = keep("vec", [128, NVEC])
        ss = keep("ss", [128, T])
        rstd = keep("rstd", [128, T])
        epsc = keep("epsc", [128, 2])

        arena = keep.here
        xr = Region(arena)
        xh, xl = [None, None], [None, None]
        xh[0] = xr("xh0", [128, KC, T], F32R)
        xl[0] = xr("xl0", [128, KC, T], F32R)
        after_x0 = xr.here
        xh[1] = xr("xh1", [128, KC, T], F32R)
        xl[1] = xr("xl1", [128, KC, T], F32R)
        after_x1 = xr.here

        ff = Region(after_x0)
        hid_h = ff("hid_h", [128, FC * T], F32R)
        hid_l = ff("hid_l", [128, FC * T], F32R)
        gate = ff("gate", [128, 2, T])
        upg = ff("upg", [128, 2, T])
        sig = ff("sig", [128, 2, T])
        hidf = ff("hidf", [128, 2, T])
        sq = ff("sq", [128, 2, 2, T])
        xg = ff("xg", [128, 2, 2, T])
        ff = Region(after_x0)
        hid2_h = ff("hid2_h", [128, 32 * SEQ], F32R)
        hid2_l = ff("hid2_l", [128, 32 * SEQ], F32R)
        act2 = ff("act2", [128, 2, 2, SEQ])
        hidf2 = ff("hidf2", [128, 2, 2, SEQ])
        outt = ff("outt", [128, KC, SEQ])

        rk = Region(after_x1)
        hn = rk("hn", [128, KC, T])
        xx = rk("xx", [128, KC, T])
        rk.here = after_x1 + 2 * 4 * KC * TP
        a_g = rk("a_g", [128, KC, T])
        head_end = rk.here
        lh_at = rk.here
        lh = rk("lh", [128, T])
        lh_h = rk("lh_h", [128, T], F32R)
        lh_l = rk("lh_l", [128, T], F32R)
        gh = rk("gh", [80, 2, T])
        gh_h = rk("gh_h", [80, 2, T], F32R)
        gh_l = rk("gh_l", [80, 2, T], F32R)
        wend = rk("wend", [128, KC, NCH])
        first = rk("first", [128, KC, NCH])
        R_ = rk("R_", [128, KC, TP])
        K_ = rk("K_", [128, KC, TP])
        V_ = rk("V_", [128, KC, TP])
        A_ = rk("A_", [128, KC, TP])
        B_ = rk("B_", [128, KC, TP])
        w_at = rk.here
        W_ = rk("W_", [128, KC, TP])
        masks = rk("masks", [128, 10, BLK])
        r2 = Region(w_at)
        xmf = r2("xmf", [128, KC, T])
        bonus = Region(w_at)("bonus", [128, KC, T])
        r2 = Region(after_x1)
        wst = r2("wst", [128, KC, TP])
        Wc = r2("Wc", [128, KC, TP])
        ktmp = Region(after_x0)("ktmp", [128, KC, TP])
        kden = Region(arena)("kden", [16, T])
        sc = Region(arena)
        U_ = sc("U_", [96, NB, 512])
        mrb = sc("mrb", [96, 8, TP])
        btok = sc("btok", [96, NB, 512])
        GV = sc("GV", [128, NCH, 256])
        L_ = QQ = [sc(f"L{e}", [96, TP]) for e in range(4)]
        LT = [sc(f"LT{e}", [96, TP]) for e in range(4)]
        xx_at = sc.here
        XX = [sc(f"XX{e}", [96, TP]) for e in range(4)]
        lm_at = sc.here
        LM = [sc(f"LM{e}", [96, TP]) for e in range(4)]
        XT = [sc(f"XT{e}", [96, TP]) for e in range(4)]
        lak = [sc(f"lak{e}", [96, TP]) for e in range(2)]
        in_raw = Region(keep_at + (U0["rk_o"] + 3) % RAW * 8192)
        mrk_at = in_raw.here
        mrk = [in_raw(f"mrk{e}", [96, TP]) for e in range(4)]
        lak += [in_raw(f"lak{e}", [96, TP]) for e in range(2, 4)]
        atok = [sc(f"atok{e}", [96, NB, 128]) for e in range(2)]
        ktok = [sc("ktok0", [96, NB, 128]), Region(rk.here)("ktok1", [96, NB, 128])]
        in_lh = Region(lh_at)
        vtok = [in_lh(f"vtok{e}", [96, NB, 128]) for e in range(2)]
        in_lm, in_mrk, in_xx = Region(lm_at), Region(mrk_at), Region(xx_at)
        p1 = [in_lm(f"p1{e}", [96, NB, 128]) for e in range(2)]
        bh = [in_mrk(f"bh{e}", [128, TP]) for e in range(2)]
        kh = [in_mrk(f"kh{e}", [128, TP]) for e in range(2)]
        S_ = [in_xx(f"S{e}", [128, 256]) for e in range(2)]
        St = in_xx("St", [128, 256])
        assert sc.here <= head_end, (sc.here, head_end)

        ds_ = Region(after_x1)
        rawq = ds_("rawq", [128, 18, T])
        vt = ds_("vt", [96, NB, 256])
        rot_a = ds_("rot_a", [128, 128])
        cs_a = ds_("cs_a", [128, 2, T])
        cap = ds_("cap", [128, 2, T])
        wit = ds_("wit", [128, 2, 8])
        rel = ds_("rel", [128, 2, T])
        score = ds_("score", [128, 2, T])
        taken = [ds_(f"taken{i}", [128, 2, T]) for i in range(2)]
        m8 = ds_("m8", [128, 8])
        rcol_a = ds_("rcol_a", [128, NB, 4])
        b2 = Region(after_x1)
        qka = b2("qka", [128, 8, SEQ])
        vat = b2("vat", [128, 2, 512])
        craw = b2("craw", [128, 8, SEQ])
        krope = b2("krope", [128, SEQ])
        cxf_at = b2.here
        qkb = b2("qkb", [96, 16, SEQ])
        vbt = b2("vbt", [128, 2, 512])
        bias = b2("bias", [128, 8, 256])
        causal = b2("causal", [128, 256])
        rot_b = b2("rot_b", [128, 96])
        cs_b = b2("cs_b", [128, 2, SEQ])
        rcol_b = b2("rcol_b", [128, 2, 4])
        posi = b2("posi", [128, SEQ], I32)
        posf = b2("posf", [128, SEQ])
        ang = b2("ang", [128, SEQ])
        red = b2("red", [128, SEQ])
        freq = b2("freq", [128, 2])
        distt = b2("distt", [33, 384])
        relb = b2("relb", [33, 8, 128])
        bt = b2("bt", [128, 2, SEQ])
        cvr = b2("cvr", [128, 2, SEQ])
        csq = Region(cxf_at + 4 * 8 * SEQ)("csq", [128, 8, SEQ])
        cxf = Region(cxf_at)("cxf", [128, 8, SEQ])
        attn_at = max(ds_.here, b2.here)
        an = Region(attn_at)
        biasw = Region(attn_at)("biasw", [128, 8, 384])
        lg = an("lg", [128, 2, T])
        pr = an("pr", [128, 3, T])
        prn = an("prn", [128, 2, T])
        pts = an("pts", [128, 2, 3, 128])
        amx = an("amx", [128, 64])
        nmx = an("nmx", [128, 64])
        asum = an("asum", [128, 64])
        ainv = an("ainv", [128, 64])

        sqp = [an(f"sqp{i}", [128, 2, T]) for i in range(2)]
        hinv = [an(f"hinv{i}", [32, T]) for i in range(2)]
        rtt = an("rtt", [128, 2, T])
        assert used[0] <= nc.sbuf_usable_end, (used[0], nc.sbuf_usable_end)

        PS = ctx.enter_context(nc.psum_tensor("PS", [128, 8, 512], F32))


        def by_head(tile, rows=16):
            return sel[:, 30 - 2 * tile:30 - 2 * tile + rows]

        def row(r, rows, m):
            return ident[0:rows, r:r + 1].broadcast_to([rows, m])

        s_raw = [sem(f"raw_arrived{i}") for i in range(RAW)]
        s_hi = sem("hi_split")
        s_lo = sem("lo_split")
        s_unit = sem("unit_used")
        s_free = sem("group_drained")
        s_xm = sem("x_made")
        s_xh = sem("x_high")
        s_x = sem("x_low")
        s_sq = sem("squared")
        s_ssa = sem("squares_added")
        s_nmm = sem("norm_summed")
        s_var = sem("mean_square")
        s_std = sem("root")
        s_gate = sem("gate_scaled")
        s_sig = sem("gate_sigmoid")
        s_hid = sem("hidden_made")
        s_hhi = sem("hidden_high")
        s_hlo = sem("hidden_low")
        s_rcm = sem("token_rms_in_rows")
        s_dve, s_act, s_pool = sem("dve_step"), sem("act_step"), sem("pool_step")
        s_h0 = sem("h_arrived")
        s_const = sem("constants_arrived")
        s_rkc = sem("scan_masks_arrived")
        s_dsc = sem("dsa_tables_arrived")
        s_bc = sem("last_block_tables_arrived")

        s_tanh, s_ghs = sem("tanh_done"), sem("gate_lora_sigmoid")
        s_lhd, s_lhh, s_lhl = sem("lora_drained"), sem("lora_high"), sem("lora_low")
        s_ghd, s_ghh, s_ghl = sem("gate_lora_drained"), sem("gate_lora_high"), sem("gate_lora_low")
        s_part = sem("part_of_unit")
        s_wa, s_dec = sem("decay_and_a_drained"), sem("decay_sigmoid")
        s_cum, s_dk = sem("decays_added"), sem("decays_multiplied")
        s_kk, s_kksq, s_kkm, s_kkr = sem("kk_made"), sem("kk_squared"), sem("kk_summed"), sem("kk_root")
        s_rkr, s_bonm, s_bon = sem("bonus_products"), sem("bonus_summed"), sem("bonus_made")
        s_kki, s_kkb, s_kkd = sem("kk_inverse"), sem("kk_spread"), sem("kk_divided")
        s_gni, s_gnb, s_gnd = sem("y_inverse"), sem("y_spread"), sem("y_divided")
        s_hi_, s_hb = sem("head_inverse"), sem("head_spread")
        s_bk, s_tr = sem("pair_ready"), sem("transposed")
        s_tka, s_tkd = sem("tokens_major_act"), sem("tokens_major_dve")
        s_gm, s_gr = sem("gram_product"), sem("gram_masked")
        s_lm, s_q, s_qc, s_xt = sem("level_mask"), sem("level_q"), sem("level_q_copied"), sem("level_update")
        s_xd, s_xi = sem("level_added"), sem("inverse_begun")
        s_p1, s_p1c, s_um, s_ue = sem("lak_v"), sem("lak_v_copied"), sem("u_product"), sem("u_copied")
        s_ztm, s_zt, s_yvm, s_yv = sem("z_product"), sem("z_copied"), sem("yv_product"), sem("yv_copied")
        s_gvm, s_gv = sem("gamma_product"), sem("gamma_copied")
        s_sam, s_sau, s_dsm, s_s = sem("sa_product"), sem("sa_made"), sem("state_product"), sem("state_made")
        s_ysm, s_yse, s_ym, s_yc = sem("ys_product"), sem("ys_added"), sem("intra_product"), sem("y_added")
        s_mum, s_yc2, s_ysq, s_vm = sem("y_mean"), sem("y_centred"), sem("y_squared"), sem("y_var_sum")
        s_bv, s_bvr = sem("y_var"), sem("y_root")
        s_hsq, s_hsum, s_hvar, s_hroot = sem("head_squared"), sem("head_summed"), sem("head_var"), sem("head_root")
        s_hsc, s_hrot, s_hout = sem("head_scaled"), sem("head_rotated"), sem("head_ready")
        s_wtm, s_wt = sem("wi_transposed"), sem("wi_ready")
        s_rlm, s_rl, s_ra = sem("index_product"), sem("index_relu"), sem("index_added")
        s_sel = sem("selection_ready")
        s_lgm, s_lg, s_ex, s_prn = sem("logits"), sem("logits_max"), sem("exponentials"), sem("probabilities")
        s_ptm, s_pte, s_om, s_oh, s_ol = (sem("p_transposed"), sem("p_copied"), sem("head_product"),
                                          sem("head_high"), sem("head_low"))
        s_csq, s_css, s_cnm, s_cv, s_cst = (sem("latent_squared"), sem("latent_squares_added"),
                                            sem("latent_summed"), sem("latent_var"), sem("latent_root"))
        s_ang, s_sin = sem("angles"), sem("sines")
        s_bwm, s_bw, s_bst, s_bld = (sem("bias_rows_product"), sem("bias_rows"), sem("bias_stored"),
                                     sem("bias_loaded"))
        s_r2, s_hf2, s_hlo2 = sem("relu_scaled"), sem("relu_squared"), sem("hidden2_low")
        s_out = sem("result_stored")

        tok = {"f0": T, "f1": T, "f2": T, "f3": SEQ}
        after = {"f0": None, "f1": "f2", "f2": None, "f3": None}
        gain = {"f0": norm_col(0, 0), "f1": norm_col(0, 2), "f2": norm_col(1, 0), "f3": norm_col(1, 2)}

        def hv(n, a, b=None):
            b = a + 1 if b is None else b
            return h[:, a:b, T - n:T]

        def bank(G):
            return 2 * (G % 2)

        def mask(k):
            return masks[0:BLK, k, :].unsqueeze(1).broadcast_to([BLK, NB, BLK])

        def blocks(x):
            return x.rearrange("p (b t) -> p b t", b=NB)

        block = ctx.enter_context(nc.Block())

        @block.sync
        def _(sp):
            link = Link(sp, None)
            r_arrived, r_split = sp.alloc_register("arrived"), sp.alloc_register("split")
            sp.dma_start(h[:, :, :], t["h0"]).then_inc(s_h0, 16)
            for dst, name in ((ident, "ident"), (ones, "ones"), (bo64, "bo64"), (sel, "sel"), (vec, "vec")):
                sp.dma_start(dst[:, :], t[name]).then_inc(s_const, 16)

            def load(name):
                src, w, u0 = t["w_" + name], UW[name], U0[name]

                def body(us, i):
                    for u in us:
                        U = u0 + u
                        arrived, split = val(16 * (U // RAW), i, 16), val(2 * (U - RAW + 1), i, 8)
                        s = src[u] if i is None else src[bass.ds(i * 4 + u, 1)].rearrange("o p w -> (o p) w")
                        if i is not None:
                            sp.reg_mov(r_arrived, arrived)
                            sp.reg_mov(r_split, split)
                            arrived, split = r_arrived, r_split
                        if name == "rk_o" and u == 3:
                            sp.wait_ge(s_yc, KC)
                        if U >= RAW:
                            sp.wait_ge(s_raw[U % RAW], arrived)
                            sp.wait_ge(s_lo, split)
                        sp.dma_start(raw[U % RAW][:, 0:w], s).then_inc(s_raw[U % RAW], 16)
                turns(link, UN[name], 4, 0, body, RAW - u0 if u0 < RAW else 0)

            for name, *_ in STAGES:
                load(name)
            sp.wait_ge(s_free, G0["b_ff2"] + 8)
            sp.dma_start(t["out"], outt[:, :, :]).then_inc(s_out, 16)
            sp.wait_ge(s_out, 16)

        @block.gpsimd
        def _(pool):
            link = Link(pool, None)

            def scan_part():
                tt = nc.gpsimd.tensor_tensor
                pool.wait_ge(s_lo, 2 * (U0["g2"] + 1))
                pool.wait_ge(s_rkc, 16)
                pool.wait_ge(s_bon, KC)
                for q in range(4):
                    for pp in range(2):
                        if q and pp == 0:
                            pool.wait_ge(s_yvm, 2 * q)
                        for n, (dst, src) in enumerate(((bh[pp], B_), (kh[pp], K_))):
                            ins = tt(dst[:, :].rearrange("p (n t) -> p n t", t=CH),
                                     src[:, 2 * q + pp, :].rearrange("p (n t) -> p n t", t=CH),
                                     wend[:, 2 * q + pp, :].unsqueeze(2).broadcast_to([128, NCH, CH]), ALU.mult)
                            ins.then_inc(s_bk, 1)
                    for e in range(4):
                        pool.wait_ge(s_gr, 20 * q + 5 * e + 1)
                        tt(blocks(LM[e][:, :]), blocks(LT[e][:, :]), mask(5), ALU.mult).then_inc(s_lm, 1)
                    for lv in range(1, 4):
                        for e in range(4):
                            pool.wait_ge(s_q, 16 * q + 4 * (lv - 1) + e + 1)
                            tt(blocks(LM[e][:, :]), blocks(LT[e][:, :]), mask(5 + lv), ALU.mult).then_inc(s_lm, 1)

            for name, n, _m, w in STAGES:
                u0 = U0[name]

                def body(us, i):
                    for u in us:
                        U = u0 + u
                        for q, part in enumerate(halves(w)):
                            pool.wait_ge(s_hi, val(2 * U + q + 1, i, 8))
                            if U >= SPL:
                                pool.wait_ge(s_unit, val(2 * (U - SPL) + q + 1, i, 8))
                            nc.gpsimd.tensor_tensor(wlo[U % SPL][:, part], raw[U % RAW][:, part],
                                                    whi[U % SPL][:, part].bitcast(F32), ALU.subtract
                                                    ).then_inc(s_lo, 1)
                turns(link, n, 4, 0, body)
                if name == "g2":
                    scan_part()
        HB = {f"f{i}": FC * i for i in range(4)}

        def dsa_jobs():
            out = []
            for hd in range(16):
                e, g = hd % 2, hd // 4
                for b in range(2):
                    nk = META + 128 * (b + 1)
                    rows = slice(64 * e, 64 * e + 64)
                    vb = [(vt[0:min(BLK, nk - BLK * j), j, g * 64:g * 64 + 64], BLK * j, min(BLK, nk - BLK * j))
                          for j in range(-(-nk // BLK))]
                    out.append(dict(q=rawq[rows, hd // 2, META + 128 * b:META + 128 * b + 128],
                                    k=rawq[rows, 8 + g, 0:nk], nk=nk, add=taken[0][:, b, 0:nk],
                                    scale=0.125, v=vb, head=hd, b=b))
            return out

        def last_jobs():
            out = []
            for hd in range(16):
                for b in range(2):
                    nk = 128 * (b + 1)
                    if hd < 8:
                        e = hd % 2
                        rows = slice(64 * e, 64 * e + 64)
                        q, k = qka[rows, hd // 2, 128 * b:128 * b + 128], qka[rows, 4 + hd // 2, 0:nk]
                        add, scale, val_ = bias[:, hd, 256 - nk:256], 0.125, vat
                    else:
                        q, k = qkb[0:96, hd - 8, 128 * b:128 * b + 128], qkb[0:96, hd, 0:nk]
                        add, scale, val_ = causal[:, 256 - nk:256], float(96 ** -0.5), vbt
                    vb = [(val_[:, j, (hd % 8) * 64:(hd % 8) * 64 + 64], 128 * j, 128) for j in range(b + 1)]
                    out.append(dict(q=q, k=k, nk=nk, add=add, scale=scale, v=vb, head=hd, b=b))
            return out

        JOBS = {"at": (dsa_jobs(), 0), "b": (last_jobs(), 32)}

        def two(x, j, n=2):
            return x[:, j:j + n, :]

        def head_tiles_at():
            out = []
            for j in range(0, 16, 2):
                gain_ = VEC["q_g"] if j < 8 else VEC["k_g"]
                out.append(dict(x=rawq[:, j:j + 2, :], rows=128, m=2, n=T, norm=j < 12, one=bo64[:, :],
                                inv=1 / 64, g=gain_, rot=rot_a[:, :], cos=cs_a[:, 0, :], sin=cs_a[:, 1, :]))
            out.append(dict(x=rawq[:, 16:17, :], rows=128, m=1, n=T, norm=False, rot=rot_a[:, :],
                            cos=cs_a[:, 0, :], sin=cs_a[:, 1, :]))
            return out

        def head_tiles_b():
            out = []
            for j in range(0, 8, 2):
                out.append(dict(x=qka[:, j:j + 2, :], rows=128, m=2, n=SEQ, norm=True, one=bo64[:, :],
                                inv=1 / 64, g=VEC["qa_g"] if j < 4 else VEC["ka_g"], rot=None))
            for j in range(0, 16, 2):
                out.append(dict(x=qkb[:, j:j + 2, :], rows=96, m=2, n=SEQ, norm=True,
                                one=ones[0:96, 0:96], inv=1 / 96, g=VEC["qb_g"] if j < 8 else VEC["kb_g"],
                                rot=rot_b[0:96, :], cos=cs_b[0:96, 0, :], sin=cs_b[0:96, 1, :]))
            return out

        TILES = {"at": head_tiles_at(), "b": head_tiles_b()}
        NT0 = {"at": 0, "b": sum(x["norm"] for x in TILES["at"])}
        RT0 = {"at": 0, "b": len(TILES["at"])}

        def counts(which, j):
            ts = TILES[which][:j + 1]
            return (NT0[which] + sum(x["norm"] for x in ts),
                    RT0[which] + sum(x["rot"] is not None for x in ts))

        GROUPS = [("at", 0, 6, 24, 0), ("b", 0, 4, 16, 1), ("b", 4, 12, 16, 2)]

        def groups(which):
            return [g[1:] for g in GROUPS if g[0] == which]

        def head_sum(x, j, q, g):
            a, _b, rows, _n = g
            t_ = 2 * (j - a) + q
            return by_head(t_, rows) if x["rows"] == 128 else sel[0:96, 71 - t_:71 - t_ + rows]

        @block.tensor
        def _(pe):
            link = Link(pe, None)
            mm = nc.tensor.matmul

            def products(out, w, x, start, stop, tokens=False):
                for n, (a, b) in enumerate(((w[0], x[0]), (w[0], x[1]), (w[1], x[0]))):
                    last = mm(out, b, a, start=start and n == 0, stop=stop and n == 2) if tokens else \
                        mm(out, a, b, start=start and n == 0, stop=stop and n == 2)
                return last

            def weights(U, rows, cols):
                return whi[U % SPL][rows, cols], wlo[U % SPL][rows, cols]

            ALLR = slice(0, 128)

            def norm_sum(name, n):
                pe.wait_ge(s_ssa, 8 * (N0[name] + 1))
                mm(PS[:, 6, 0:n], ones[:, :], ss[:, 0:n], start=True, stop=True).then_inc(s_nmm, 1)

            def project(name, n, b, x, norm=None, straight=0):
                def body(us, i):
                    for u in us:
                        U, G = U0[name] + u, G0[name] + u
                        for mi in range(2):
                            pe.wait_ge(s_lo, val(2 * U + mi + 1, i, 8))
                            if G >= 2 and mi == 0:
                                pe.wait_ge(s_free, val(G - 1, i, 4))
                            for k in range(KC):
                                if x and u == 0 and mi == 0:
                                    pe.wait_ge(s_x, X0[x] + k + 1)
                                c = mi * 1024 + k * 128
                                last = products(PS[:, bank(G) + mi, 0:n], weights(U, ALLR, slice(c, c + 128)),
                                                (xh[b][:, k, 0:n], xl[b][:, k, 0:n]), k == 0, k == KC - 1)
                            last.then_inc(s_unit, 1)
                            if u == 0 and mi == 0 and norm:
                                norm_sum(norm, n)
                if straight:
                    body(range(straight), None)
                    with link.loop((UN[name] - straight) // 4, 0) as i:
                        body(range(straight, straight + 4), i)
                else:
                    turns(link, UN[name], 4, 0, body)

            def project_down(name, n, hh, hl, stride, nk, ready):
                half = nk // 2

                def body(ms, i):
                    for m in ms:
                        G = G0[name] + m
                        for part in range(2):
                            U = U0[name] + 2 * m + part
                            if part == 0:
                                pe.wait_ge(s_free, val(G - 1, i, 4))
                            for k in range(half):
                                kk = part * half + k
                                if k in (0, 8):
                                    pe.wait_ge(s_lo, val(2 * U + k // 8 + 1, i, 16))
                                if m == 0:
                                    ready(kk)
                                last = products(PS[:, bank(G), 0:n], weights(U, ALLR, slice(k * 128, k * 128 + 128)),
                                                (hh[:, kk * stride:kk * stride + n], hl[:, kk * stride:kk * stride + n]),
                                                kk == 0, kk == nk - 1)
                                if k in (7, half - 1):
                                    last.then_inc(s_unit, 1)
                turns(link, 8, 4, 0, body)

            def swiglu(f):
                project(f + "_in", tok[f], 0, f, norm=f)
                project_down(f + "_dn", tok[f], hid_h, hid_l, T, FC,
                             lambda kk: pe.wait_ge(s_hlo, HB[f] + kk + 1))

            def head_norms(which):
                tiles = TILES[which]
                for g in groups(which):
                    for j in range(g[0], g[1]):
                        x = tiles[j]
                        c, _r = counts(which, j)
                        pe.wait_ge(s_hsq, c)
                        for q in range(2):
                            last = mm(PS[0:g[2], 6 + g[3] % 2, 0:x["n"]], head_sum(x, j, q, g),
                                      sqp[c % 2][0:x["rows"], q, 0:x["n"]], start=j == g[0] and q == 0,
                                      stop=j == g[1] - 1 and q == 1)
                        last.then_inc(s_hsum, 1)
                for j in range(len(tiles) + 2):
                    if j < len(tiles) and tiles[j]["norm"]:
                        x = tiles[j]
                        g = [g for g in groups(which) if g[0] <= j < g[1]][0]
                        c, _r = counts(which, j)
                        if j == g[0]:
                            pe.wait_ge(s_hi_, g[3] + 1)
                        if c - NT0[which] > 2:
                            pe.wait_ge(s_hsc, c - 2)
                        for q in range(2):
                            o, t_, inv = 2 * (c % 2) + q, 2 * (j - g[0]) + q, hinv[g[3] % 2][0:g[2], 0:x["n"]]
                            if x["rows"] == 96:
                                last = mm(PS[0:96, o, 0:x["n"]], row(t_, g[2], 96), inv, start=True, stop=True)
                            for e in range(2 if x["rows"] == 128 else 0):
                                last = mm(PS[64 * e:64 * e + 64, o, 0:x["n"]], row(2 * t_ + e, g[2], 64), inv,
                                          start=True, stop=True)
                        last.then_inc(s_hb, 1)
                    if j >= 2 and tiles[j - 2]["rot"] is not None:
                        x = tiles[j - 2]
                        r, n = slice(0, x["rows"]), x["n"]
                        c, cr = counts(which, j - 2)
                        pe.wait_ge(s_hsc, c)
                        if cr - RT0[which] > 2:
                            pe.wait_ge(s_hout, cr - 2)
                        for q in range(x["m"]):
                            last = mm(PS[r, 4 + 2 * (cr % 2) + q, 0:n], x["rot"], x["x"][r, q, :],
                                      start=True, stop=True)
                        last.then_inc(s_hrot, 1)

            def attention(which):
                jobs, j0 = JOBS[which]
                for j in range(len(jobs) + 3):
                    if j < len(jobs):
                        x, c = jobs[j], j0 + j
                        if j >= 2:
                            pe.wait_ge(s_lg, c - 1)
                        mm(PS[:, j % 2, 0:x["nk"]], x["q"], x["k"], start=True, stop=True).then_inc(s_lgm, 1)
                    if 0 <= j - 2 < len(jobs):
                        x, c = jobs[j - 2], j0 + j - 2
                        pe.wait_ge(s_prn, c + 1)
                        if j - 2 >= 2:
                            pe.wait_ge(s_pte, c - 1)
                        for n, (_v, k0, kn) in enumerate(x["v"]):
                            last = nc.tensor.transpose(PS[0:kn, 2 + c % 2, n * 128:n * 128 + 128],
                                                       prn[:, c % 2, k0:k0 + kn], ident[:, :])
                        last.then_inc(s_ptm, 1)
                    if 0 <= j - 3 < len(jobs):
                        x, c = jobs[j - 3], j0 + j - 3
                        pe.wait_ge(s_pte, c + 1)
                        if j - 3 >= 2:
                            pe.wait_ge(s_ol, c - 1)
                        r = 64 * (x["head"] % 2)
                        for n, (v, k0, kn) in enumerate(x["v"]):
                            last = mm(PS[r:r + 64, 4 + c % 2, 0:128], v, pts[0:kn, c % 2, n, :],
                                      start=n == 0, stop=n == len(x["v"]) - 1)
                        last.then_inc(s_om, 1)

            pe.wait_ge(s_const, 80)
            swiglu("f0")
            norm_sum("rk", T)
            project("rk_r", T, 0, "m0")
            project("rk_k", T, 1, "m1")
            project("rk_v", T, 0, "m2")
            U, G = U0["lora_wa"], G0["lora_wa"]
            pe.wait_ge(s_lo, 2 * U + 2)
            pe.wait_ge(s_free, G - 1)
            for mi in range(2):
                for k in range(KC):
                    pe.wait_ge(s_x, X0[f"m{3 + mi}"] + k + 1)
                    last = products(PS[:, bank(G) + mi, 0:T], weights(U, ALLR, slice(k * 128, k * 128 + 128)),
                                    (xh[1 - mi][:, k, :], xl[1 - mi][:, k, :]), k == 0, k == KC - 1)
            last.then_inc(s_unit, 2)
            U, G = U0["lora_g"], G0["lora_g"]
            pe.wait_ge(s_lo, 2 * U + 2)
            pe.wait_ge(s_free, G - 1)
            for mi in range(2):
                for k in range(KC):
                    pe.wait_ge(s_x, X0["m5"] + k + 1)
                    c = k * 160 + mi * 80
                    last = products(PS[0:80, bank(G) + mi, 0:T], weights(U, ALLR, slice(c, c + 80)),
                                    (xh[1][:, k, :], xl[1][:, k, :]), k == 0, k == KC - 1)
            last.then_inc(s_unit, 2)
            U = U0["wa2"]
            pe.wait_ge(s_lo, 2 * U + 2)
            pe.wait_ge(s_lhl, 1)
            for m in range(KC):
                G = G0["wa2"] + m
                pe.wait_ge(s_free, G - 1)
                for mi in range(2):
                    r = slice(64 * mi, 64 * mi + 64)
                    last = products(PS[:, bank(G) + mi, 0:T], weights(U, r, slice(m * 128, m * 128 + 128)),
                                    (lh_h[r, :], lh_l[r, :]), True, True)
                last.then_inc(*((s_part, 1) if m < KC - 1 else (s_unit, 2)))
            pe.wait_ge(s_kksq, 1)
            for c in range(KC):
                last = mm(PS[0:16, 4, 0:T], by_head(c), ktmp[:, c, 0:T], start=c == 0, stop=c == KC - 1)
            last.then_inc(s_kkm, 1)
            pe.wait_ge(s_kki, 1)
            for m in range(4):
                if m >= 2:
                    pe.wait_ge(s_kkd, m - 1)
                for n in range(2):
                    for e in range(2):
                        last = mm(PS[64 * e:64 * e + 64, 4 + 2 * (m % 2) + n, 0:T], row(4 * m + 2 * n + e, 16, 64),
                                  kden[:, :], start=True, stop=True)
                last.then_inc(s_kkb, 1)
            for c in range(KC):
                pe.wait_ge(s_rkr, c + 1)
                if c >= 2:
                    pe.wait_ge(s_bon, c - 1)
                mm(PS[:, 4 + c % 2, 0:T], bo64[:, :], ktmp[:, c, 0:T], start=True, stop=True).then_inc(s_bonm, 1)

            def bl(b):
                return slice(b * BLK, b * BLK + BLK)

            def tk(e):
                return slice(64 * e, 64 * e + 64)

            def per_block(out, left, right):
                for e in range(2):
                    for b in range(NB):
                        last = mm(out(e, b), left(e, b), right(e, b), start=True, stop=True)
                return last

            for half in range(2):
                for q in (2 * half, 2 * half + 1):
                    c0 = 2 * q
                    if q:
                        for s in (s_zt, s_gv, s_yv, s_ue):
                            pe.wait_ge(s, c0)
                        if q == 2:
                            pe.wait_ge(s_yc, 4)
                    for pp in range(2):
                        c = c0 + pp
                        pe.wait_ge(s_bk, 2 * c + 2)
                        for n, src in enumerate((A_[:, c, :], bh[pp][:, :], kh[pp][:, :], V_[:, c, :])):
                            for b in range(NB):
                                last = nc.tensor.transpose(PS[0:BLK, 4 * pp + n, b * 128:b * 128 + 128],
                                                           src[:, bl(b)], ident[:, :])
                            last.then_inc(s_tr, 1)
                    for n in range(20):
                        c, e, ty = c0 + n // 10, n // 5 % 2, n % 5
                        if n in (0, 4):
                            pe.wait_ge(s_tka, 2 * (c0 + n // 4) + 2)
                            pe.wait_ge(s_tkd, 2 * (c0 + n // 4) + 2)
                        if n >= 8:
                            pe.wait_ge(s_gr, 20 * q + n - 7)
                        left = (B_, A_, K_, B_, K_)[ty]
                        right = (A_, B_, A_, R_, R_)[ty]
                        for b in range(NB):
                            last = mm(PS[0:BLK, n % 8, bl(b)], left[tk(e), c, bl(b)], right[tk(e), c, bl(b)],
                                      start=True, stop=True)
                        last.then_inc(s_gm, 1)
                    pe.wait_ge(s_gr, 20 * q + 20)
                    pe.wait_ge(s_xi, 4 * q + 4)
                    for lv in range(4):
                        for e in range(4):
                            pe.wait_ge(s_lm, 16 * q + 4 * lv + e + 1)
                            if lv:
                                pe.wait_ge(s_xd, 16 * q + 4 * (lv - 1) + e + 1)
                            for b in range(NB):
                                last = mm(PS[0:BLK, e, bl(b)], LM[e][:, bl(b)], XX[e][:, bl(b)], start=True, stop=True)
                            last.then_inc(s_q, 1)
                        for e in range(4):
                            pe.wait_ge(s_qc, 16 * q + 4 * lv + e + 1)
                            if lv < 3:
                                for b in range(NB):
                                    mm(PS[0:BLK, 4 + e, bl(b)], XT[e][:, bl(b)], QQ[e][:, bl(b)], start=True, stop=True)
                            for b in range(NB):
                                last = mm(PS[0:BLK, e, bl(b)], QQ[e][:, bl(b)], XT[e][:, bl(b)], start=True, stop=True)
                            last.then_inc(s_xt, 1)
                    pe.wait_ge(s_xd, 16 * q + 16)
                    for pp in range(2):
                        per_block(lambda e, b: PS[0:BLK, pp, b * 128 + 64 * e:b * 128 + 64 * e + 64],
                                  lambda e, b: lak[2 * pp + e][:, bl(b)], lambda e, b: vtok[pp][:, b, tk(e)]).then_inc(s_p1, 1)
                    for pp in range(2):
                        per_block(lambda e, b: PS[tk(e), 2 + pp, bl(b)],
                                  lambda e, b: atok[pp][:, b, tk(e)], lambda e, b: XT[2 * pp + e][:, bl(b)]).then_inc(s_ztm, 1)
                    for pp in range(2):
                        per_block(lambda e, b: PS[tk(e), 4 + pp, bl(b)],
                                  lambda e, b: vtok[pp][:, b, tk(e)], lambda e, b: mrk[2 * pp + e][:, bl(b)]).then_inc(s_yvm, 1)
                    for pp in range(2):
                        pe.wait_ge(s_p1c, c0 + pp + 1)
                        per_block(lambda e, b: PS[0:BLK, 6 + pp, b * 128 + 64 * e:b * 128 + 64 * e + 64],
                                  lambda e, b: XT[2 * pp + e][:, bl(b)], lambda e, b: p1[pp][:, b, tk(e)]).then_inc(s_um, 1)
                    for pp in range(2):
                        pe.wait_ge(s_zt, c0 + pp + 1)
                        if pp:
                            pe.wait_ge(s_yv, c0 + 2)
                        for ch in range(NCH):
                            b, r = ch // 3, slice(CH * (ch % 3), CH * (ch % 3) + CH)
                            for e in range(2):
                                last = mm(PS[tk(e), 3 * pp + ch % 3, b * 64:b * 64 + 64], ktok[pp][r, b, tk(e)],
                                          vtok[pp][r, b, tk(e)], start=True, stop=True)
                        last.then_inc(s_gvm, 1)

                heads = [(p, e) for p in range(4) for e in range(2)]
                pe.wait_ge(s_ue, 4 * half + 4)
                pe.wait_ge(s_zt, 4 * half + 4)
                pe.wait_ge(s_gv, 4 * half + 4)
                for ch in range(NCH):
                    b, r0 = ch // 3, CH * (ch % 3)
                    r = slice(r0, r0 + CH)
                    if ch:
                        pe.wait_ge(s_s, 8 * half + ch)
                        for p, e in heads:
                            last = mm(PS[r, 3 + e, p * 64:p * 64 + 64],
                                      A_[64 * e:64 * e + 64, 4 * half + p, ch * CH:ch * CH + CH],
                                      S_[ch % 2][64 * e:64 * e + 64, p * 64:p * 64 + 64], start=True, stop=True)
                        last.then_inc(s_sam, 1)
                    if ch < NCH - 1:
                        if ch:
                            pe.wait_ge(s_sau, 8 * half + ch)
                        for p, e in heads:
                            last = mm(PS[64 * e:64 * e + 64, 5, p * 64:p * 64 + 64],
                                      btok[r, b, p * 128 + 64 * e:p * 128 + 64 * e + 64],
                                      U_[r, b, (2 * p + e) * 64:(2 * p + e) * 64 + 64], start=True, stop=True)
                        last.then_inc(s_dsm, 1)
                    if ch:
                        if ch > 2:
                            pe.wait_ge(s_yse, 8 * half + ch - 2)
                        for p, e in heads:
                            last = mm(PS[64 * e:64 * e + 64, 6 + ch % 2, p * CH:p * CH + CH],
                                      S_[ch % 2][64 * e:64 * e + 64, p * 64:p * 64 + 64],
                                      R_[64 * e:64 * e + 64, 4 * half + p, ch * CH:ch * CH + CH],
                                      start=True, stop=True)
                        last.then_inc(s_ysm, 1)
                pe.wait_ge(s_sau, 8 * half + 8)
                for p in range(4):
                    if p >= 2:
                        pe.wait_ge(s_yc, 4 * half + p - 1)
                    for e in range(2):
                        for b in range(NB):
                            last = mm(PS[64 * e:64 * e + 64, p % 2, b * BLK:b * BLK + BLK],
                                      U_[:, b, (2 * p + e) * 64:(2 * p + e) * 64 + 64],
                                      mrb[:, 2 * p + e, b * BLK:b * BLK + BLK], start=True, stop=True)
                    last.then_inc(s_ym, 1)

            for c in range(KC):
                if c == 0:
                    pe.wait_ge(s_yc, KC)
                if c >= 2:
                    pe.wait_ge(s_yc2, c - 1)
                mm(PS[:, 4 + c % 2, 0:T], bo64[:, :], K_[:, c, 0:T], start=True, stop=True).then_inc(s_mum, 1)
            for c in range(KC):
                pe.wait_ge(s_ysq, c + 1)
                last = mm(PS[0:16, 6, 0:T], by_head(c), A_[:, c, 0:T], start=c == 0, stop=c == KC - 1)
            last.then_inc(s_vm, 1)
            pe.wait_ge(s_gni, 1)
            for m in range(4):
                if m >= 2:
                    pe.wait_ge(s_gnd, m - 1)
                for n in range(2):
                    for e in range(2):
                        last = mm(PS[64 * e:64 * e + 64, 4 + 2 * (m % 2) + n, 0:T], row(4 * m + 2 * n + e, 16, 64),
                                  kden[:, :], start=True, stop=True)
                last.then_inc(s_gnb, 1)
            U = U0["g2"]
            pe.wait_ge(s_lo, 2 * U + 2)
            pe.wait_ge(s_ghl, 1)
            for g in range(4):
                G = G0["g2"] + g
                pe.wait_ge(s_free, G - 1)
                for mi in range(2):
                    for k in range(2):
                        c = k * D + (2 * g + mi) * 128
                        last = products(PS[:, bank(G) + mi, 0:T], weights(U, slice(0, 80), slice(c, c + 128)),
                                        (gh_h[:, k, :], gh_l[:, k, :]), k == 0, k == 1)
                last.then_inc(*((s_part, 1) if g < 3 else (s_unit, 2)))
            project("rk_o", T, 1, "ro")
            swiglu("f1")

            swiglu("f2")
            project("at_q", T, 0, "at", norm="at")
            project("at_k", T, 0, "at")
            project("at_qi", T, 0, "at")
            project("at_tail", T, 0, "at")
            pe.wait_ge(s_free, G0["at_q"] + 1)
            for j in range(NB):
                kn = min(BLK, T - BLK * j)
                last = mm(PS[0:kn, 6, 4 * j:4 * j + 4], rstd[:, j * BLK:j * BLK + kn], ident[:, 0:4],
                          start=True, stop=True)
            last.then_inc(s_rcm, 1)
            U, G = U0["at_v"], G0["at_v"]
            pe.wait_ge(s_lo, 2 * U + 2)
            pe.wait_ge(s_free, G - 1)
            for j in range(NB):
                kn = min(BLK, T - BLK * j)
                for k in range(KC):
                    last = products(PS[0:kn, bank(G) + j // 2, (j % 2) * 256:(j % 2) * 256 + 256],
                                    weights(U, ALLR, slice(k * 256, k * 256 + 256)),
                                    (xh[0][:, k, j * BLK:j * BLK + kn], xl[0][:, k, j * BLK:j * BLK + kn]),
                                    k == 0, k == KC - 1, tokens=True)
            last.then_inc(s_unit, 2)
            pe.wait_ge(s_free, G + 1)
            pe.wait_ge(s_dsc, 48)
            head_norms("at")
            pe.wait_ge(s_hout, RT0["b"])
            for b in range(2):
                last = nc.tensor.transpose(PS[:, 0, b * 8:b * 8 + 8], rawq[0:8, 17, META + 128 * b:META + 128 * b + 128],
                                           ident[0:8, 0:8])
            last.then_inc(s_wtm, 1)
            pe.wait_ge(s_wt, 1)
            for b in range(2):
                nk = META + 128 * (b + 1)
                for hd in range(8):
                    n = b * 8 + hd
                    r = slice(64 * (hd % 2), 64 * (hd % 2) + 64)
                    if n >= 2:
                        pe.wait_ge(s_rl, n - 1)
                    mm(PS[:, 2 + n % 2, 0:nk], rawq[r, 12 + hd // 2, META + 128 * b:META + 128 * b + 128],
                       rawq[r, 16, 0:nk], start=True, stop=True).then_inc(s_rlm, 1)
            pe.wait_ge(s_rl, 16)
            attention("at")
            pe.wait_ge(s_ol, 32)
            project("at_o", SEQ, 1, None)
            swiglu("f3")

            project("b_qa", SEQ, 0, "b", norm="b")
            project("b_ka", SEQ, 0, "b")
            pe.wait_ge(s_free, G0["b_qa"] + 1)
            for j in range(2):
                last = mm(PS[:, 6, 4 * j:4 * j + 4], rstd[:, j * 128:j * 128 + 128], ident[:, 0:4],
                          start=True, stop=True)
            last.then_inc(s_rcm, 1)
            for u in range(2):
                U, G = U0["b_va"] + u, G0["b_va"] + u
                pe.wait_ge(s_lo, 2 * U + 2)
                pe.wait_ge(s_free, G - 1)
                for j in range(2):
                    for k in range(KC):
                        last = products(PS[:, bank(G) + j, 0:256], weights(U, ALLR, slice(k * 256, k * 256 + 256)),
                                        (xh[0][:, k, j * 128:j * 128 + 128], xl[0][:, k, j * 128:j * 128 + 128]),
                                        k == 0, k == KC - 1, tokens=True)
                last.then_inc(s_unit, 2)
            project("b_cq", SEQ, 0, "b")
            project("b_ckv", SEQ, 0, "b")
            U, G = U0["b_tail"], G0["b_tail"]
            pe.wait_ge(s_lo, 2 * U + 2)
            pe.wait_ge(s_free, G - 1)
            for k in range(KC):
                last = products(PS[:, bank(G), 0:SEQ], weights(U, ALLR, slice(k * 128, k * 128 + 128)),
                                (xh[0][:, k, 0:SEQ], xl[0][:, k, 0:SEQ]), k == 0, k == KC - 1)
            last.then_inc(s_unit, 2)
            pe.wait_ge(s_bc, 96)
            for hd in range(8):
                if hd >= 2:
                    pe.wait_ge(s_bw, hd - 1)
                mm(PS[:, 4 + hd % 2, 0:384], relb[:, hd, :], distt[:, :], start=True, stop=True).then_inc(s_bwm, 1)
            for n, need in enumerate((6, 8)):
                pe.wait_ge(s_css, need)
                mm(PS[:, 6 + n, 0:SEQ], ones[:, :], bt[:, n, :], start=True, stop=True).then_inc(s_cnm, 1)
            for u in range(4):
                U, G = U0["b_uq"] + u, G0["b_uq"] + u
                pe.wait_ge(s_lo, 2 * U + 2)
                pe.wait_ge(s_free, G - 1)
                for mi in range(2):
                    for k in range(6):
                        if u == 0:
                            pe.wait_ge(s_x, X0["cq"] + k + 1)
                        c = k * 192 + mi * 96
                        last = products(PS[0:96, bank(G) + mi, 0:SEQ], weights(U, ALLR, slice(c, c + 96)),
                                        (xh[1][:, k, 0:SEQ], xl[1][:, k, 0:SEQ]), k == 0, k == 5)
                last.then_inc(s_unit, 2)
            U = U0["b_ukv"]
            pe.wait_ge(s_lo, 2 * U + 2)
            pe.wait_ge(s_x, X0["ckv"] + 2)
            for g in range(3):
                G = G0["b_ukv"] + g
                pe.wait_ge(s_free, G - 1)
                for mi in range(2):
                    for k in range(2):
                        if g < 2:
                            c = k * 1024 + (2 * g + mi) * 128
                            last = products(PS[:, bank(G) + mi, 0:SEQ], weights(U, ALLR, slice(c, c + 128)),
                                            (xh[1][:, 6 + k, 0:SEQ], xl[1][:, 6 + k, 0:SEQ]), k == 0, k == 1)
                        else:
                            c = k * 1024 + 512
                            tb = slice(mi * 128, mi * 128 + 128)
                            last = products(PS[:, bank(G) + mi, 0:512], weights(U, ALLR, slice(c, c + 512)),
                                            (xh[1][:, 6 + k, tb], xl[1][:, 6 + k, tb]), k == 0, k == 1, tokens=True)
                last.then_inc(*((s_part, 1) if g < 2 else (s_unit, 2)))
            pe.wait_ge(s_free, G0["b_ukv"] + 3)
            head_norms("b")
            pe.wait_ge(s_hout, RT0["b"] + 8)
            pe.wait_ge(s_hsc, NT0["b"] + 12)
            attention("b")
            pe.wait_ge(s_ol, 64)
            project("b_o", SEQ, 1, None)
            project("b_ff1", SEQ, 0, "ff", norm="ff", straight=4)
            project_down("b_ff2", SEQ, hid2_h, hid2_l, SEQ, 32,
                         lambda kk: pe.wait_ge(s_hlo2, kk // 2 + 1))

        C1 = 6.28125
        C2 = float(np.float32(np.float16(2 * math.pi - C1)))
        C3 = float(2 * math.pi - C1 - C2)
        MAGIC = float(1.5 * 2 ** 23)
        PI = 3.1415925

        @block.vector
        def _(dve):
            v = nc.vector
            step = Link(dve, s_dve)

            def col(c, rows=slice(0, 128)):
                return vec[rows, c:c + 1]

            def low(dst, src, high, signal):
                v.tensor_tensor(dst, src, high.bitcast(F32), ALU.subtract).then_inc(signal, 1)

            def rms(name, n):
                dve.wait_ge(s_nmm, N0[name] + 1)
                v.tensor_scalar(rstd[:, 0:n], PS[:, 6, 0:n], 1 / D, EPS, ALU.mult, ALU.add).then_inc(s_var, 1)
                dve.wait_ge(s_std, N0[name] + 1)
                step(v.reciprocal(rstd[:, 0:n], rstd[:, 0:n]))

            def start_sum():
                step(v.memset(ss[:, :], 0.0))

            def add_squares(name, tile, src, n, i=None):
                v.tensor_tensor(ss[:, 0:n], ss[:, 0:n], src, ALU.add).then_inc(s_ssa, 1)
                dve.wait_ge(s_ssa, val(8 * N0[name] + tile + 1, i, 4))

            def swiglu(f):
                n, name, hb = tok[f], f + "_in", HB[f]

                def first(u, i):
                    U, G = U0[name] + u, G0[name] + u
                    dve.wait_ge(s_unit, val(2 * U + 1, i, 8))
                    v.tensor_tensor(gate[:, u % 2, 0:n], PS[:, bank(G), 0:n], rstd[:, 0:n], ALU.mult).then_inc(s_gate, 1)
                    dve.wait_ge(s_unit, val(2 * U + 2, i, 8))
                    v.tensor_tensor(upg[:, u % 2, 0:n], PS[:, bank(G) + 1, 0:n], rstd[:, 0:n], ALU.mult).then_inc(s_free, 1)
                    dve.wait_ge(s_free, val(G + 1, i, 4))
                    step(v.tensor_tensor(upg[:, u % 2, 0:n], upg[:, u % 2, 0:n], gate[:, u % 2, 0:n], ALU.mult))

                def second(u, i):
                    if u >= 2:
                        dve.wait_ge(s_hlo, val(hb + u - 1, i, 4))
                    dve.wait_ge(s_sig, val(hb + u + 1, i, 4))
                    v.tensor_tensor(hidf[:, u % 2, 0:n], upg[:, u % 2, 0:n], sig[:, u % 2, 0:n], ALU.mult).then_inc(s_hid, 1)
                    dve.wait_ge(s_hid, val(hb + u + 1, i, 4))

                def third(u, i):
                    dve.wait_ge(s_hhi, val(hb + u + 1, i, 4))
                    o = slice(u * T, u * T + n) if i is None else bass.ds(i * (4 * T) + u * T, n)
                    low(hid_l[:, o], hidf[:, u % 2, 0:n], hid_h[:, o], s_hlo)

                def body(us, i):
                    us = list(us)
                    for k, u in enumerate(us):
                        if u == 0:
                            rms(f, n)
                        first(u, i)
                        if k >= 1:
                            second(u - 1, i)
                        if k >= 2:
                            third(u - 2, i)
                    second(us[-1], i)
                    if len(us) > 1:
                        third(us[-2], i)
                    third(us[-1], i)
                turns(step, FC, 4, 4, body)

            def residual(name, n, w, units, factor, norm, g, split):
                groups = 8 // w

                def add(j, i):
                    U, G = U0[name] + units * (j + 1) - 1, G0[name] + j
                    dve.wait_ge(s_unit, val(2 * (U + 1), i, 8 * units))
                    if i is None:
                        x = hv(n, j * w, j * w + w)
                    else:
                        x = h[:, bass.ds(i * 4 + j, 1), T - n:T]
                    v.scalar_tensor_tensor(x, PS[:, bank(G):bank(G) + w, 0:n], factor, x,
                                           ALU.mult, ALU.add).then_inc(s_free, 1)
                    if g is None:
                        return
                    dve.wait_ge(s_free, val(G + 1, i, 4))
                    for q in range(w):
                        m = j * w + q
                        if i is None:
                            v.tensor_scalar(xg[:, j % 2, q, 0:n], hv(n, m)[:, 0, :], col(g + m), None, ALU.mult).then_inc(s_xm, 1)
                        else:
                            v.tensor_scalar(xg[:, j % 2, q, 0:n], h[:, bass.ds(i * 4 + m, 1), T - n:T].rearrange("p o n -> p (o n)"),
                                            vec[:, bass.ds(i * 4 + (g + m), 1)], None, ALU.mult).then_inc(s_xm, 1)

                def after_act(j, i):
                    dve.wait_ge(s_sq, val(Q0[norm] + j + 1, i, 4))
                    for q in range(w):
                        add_squares(norm, j * w + q, sq[:, j % 2, q, 0:n], n, i)
                    if g is None:
                        return
                    for q in range(w):
                        m = j * w + q
                        dve.wait_ge(s_xh, val(X0[split] + m + 1, i, 4))
                        o = slice(m, m + 1) if i is None else bass.ds(i * 4 + m, 1)
                        low(xl[0][:, o, 0:n].rearrange("p o n -> p (o n)"), xg[:, j % 2, q, 0:n],
                            xh[0][:, o, 0:n].rearrange("p o n -> p (o n)"), s_x)

                def body(js, i):
                    js = list(js)
                    for k, j in enumerate(js):
                        add(j, i)
                        if k >= 1:
                            after_act(j - 1, i)
                    after_act(js[-1], i)
                start_sum()
                turns(step, groups, 4, 0, body)

            def split_input(name, b, made, n, chunks=range(KC), at0=0):
                for k in chunks:
                    dve.wait_ge(s_xh, X0[name] + k - at0 + 1)
                    low(xl[b][:, k, 0:n], made(k), xh[b][:, k, 0:n], s_x)

            def head_norms(which):
                tiles = TILES[which]
                for g in groups(which):
                    c, _r = counts(which, g[1] - 1)
                    n, o = tiles[g[0]]["n"], hinv[g[3] % 2]
                    dve.wait_ge(s_hsum, c)
                    v.tensor_scalar(o[0:g[2], 0:n], PS[0:g[2], 6 + g[3] % 2, 0:n], tiles[g[0]]["inv"], EPS,
                                    ALU.mult, ALU.add).then_inc(s_hvar, 1)
                for g in groups(which):
                    n, o = tiles[g[0]]["n"], hinv[g[3] % 2]
                    dve.wait_ge(s_hroot, g[3] + 1)
                    v.reciprocal(o[0:g[2], 0:n], o[0:g[2], 0:n]).then_inc(s_hi_, 1)
                for j in range(len(tiles) + 2):
                    if j < len(tiles) and tiles[j]["norm"]:
                        x = tiles[j]
                        r, n = slice(0, x["rows"]), x["n"]
                        c, _r = counts(which, j)
                        dve.wait_ge(s_hb, c)
                        v.scalar_tensor_tensor(x["x"], x["x"], col(x["g"], r), PS[r, 2 * (c % 2):2 * (c % 2) + 2, 0:n],
                                               ALU.mult, ALU.mult).then_inc(s_hsc, 1)
                    if j >= 2 and tiles[j - 2]["rot"] is not None:
                        x = tiles[j - 2]
                        r, n, m = slice(0, x["rows"]), x["n"], x["m"]
                        c, cr = counts(which, j - 2)
                        dve.wait_ge(s_hrot, cr)
                        b0 = 4 + 2 * (cr % 2)
                        step(v.tensor_tensor(rtt[r, 0:m, 0:n], PS[r, b0:b0 + m, 0:n],
                                             x["sin"].unsqueeze(1).broadcast_to([x["rows"], m, n]), ALU.mult))
                        step(v.tensor_tensor(x["x"], x["x"],
                                             x["cos"].unsqueeze(1).broadcast_to([x["rows"], m, n]), ALU.mult))
                        v.tensor_tensor(x["x"], x["x"], rtt[r, 0:m, 0:n], ALU.add).then_inc(s_hout, 1)
                        dve.wait_ge(s_hout, cr)

            def attention(which):
                jobs, j0 = JOBS[which]
                for j in range(len(jobs) + 4):
                    if j < len(jobs):
                        x, c = jobs[j], j0 + j
                        nk = x["nk"]
                        dve.wait_ge(s_lgm, c + 1)
                        if j >= 2:
                            dve.wait_ge(s_ex, c - 1)
                        step(v.tensor_tensor_reduce(lg[:, c % 2, 0:nk], PS[:, j % 2, 0:nk], x["add"], x["scale"],
                                                    NEG * 100, ALU.add, ALU.max, amx[:, c:c + 1]))
                        v.tensor_scalar(nmx[:, c:c + 1], amx[:, c:c + 1], -1.0, None, ALU.mult).then_inc(s_lg, 1)
                    if 0 <= j - 1 < len(jobs):
                        x, c = jobs[j - 1], j0 + j - 1
                        nk = x["nk"]
                        dve.wait_ge(s_ex, c + 1)
                        step(v.reciprocal(ainv[:, c:c + 1], asum[:, c:c + 1]))
                        if j - 1 >= 2:
                            dve.wait_ge(s_ptm, c - 1)
                        v.tensor_scalar(prn[:, c % 2, 0:nk], pr[:, c % 2, 0:nk], ainv[:, c:c + 1], None,
                                        ALU.mult).then_inc(s_prn, 1)
                    if 0 <= j - 4 < len(jobs):
                        x, c = jobs[j - 4], j0 + j - 4
                        r = slice(64 * (x["head"] % 2), 64 * (x["head"] % 2) + 64)
                        o = slice(128 * x["b"], 128 * x["b"] + 128)
                        dve.wait_ge(s_oh, c + 1)
                        low(xl[1][r, x["head"] // 2, o], PS[r, 4 + c % 2, 0:128], xh[1][r, x["head"] // 2, o], s_ol)

            def drain2(name, u, dst, rows=slice(0, 128), n=T):
                U, G = U0[name] + u, G0[name] + u
                dve.wait_ge(s_unit, 2 * (U + 1))
                v.tensor_copy(dst, PS[rows, bank(G):bank(G) + 2, 0:n]).then_inc(s_free, 1)

            def drain_normed(name, u, dst, n):
                U, G = U0[name] + u, G0[name] + u
                dve.wait_ge(s_unit, 2 * (U + 1))
                v.tensor_tensor(dst, PS[:, bank(G):bank(G) + 2, 0:n],
                                rstd[:, 0:n].unsqueeze(1).broadcast_to([128, 2, n]), ALU.mult).then_inc(s_free, 1)

            step(v.memset(epsc[:, :], 0.0))
            start_sum()
            dve.wait_ge(s_const, 80)
            dve.wait_ge(s_h0, 16)
            for j in range(4):
                for q in range(2):
                    m = 2 * j + q
                    if j >= 2:
                        dve.wait_ge(s_xh, m - 3)
                    v.tensor_scalar(xg[:, j % 2, q, :], h[:, m, :], col(gain["f0"] + m), None, ALU.mult).then_inc(s_xm, 1)
                    dve.wait_ge(s_sq, m + 1)
                    add_squares("f0", m, sq[:, m % 2, 0, :], T)
                    dve.wait_ge(s_xh, m + 1)
                    low(xl[0][:, m, :], xg[:, j % 2, q, :], xh[0][:, m, :], s_x)
            swiglu("f0")
            residual("f0_dn", T, 1, 2, 0.5, "rk", None, None)

            dve.wait_ge(s_ssa, 8 * N0["rk"] + 8)
            rms("rk", T)
            for c in range(KC):
                step.do(v.scalar_tensor_tensor(hn[:, c, :], h[:, c, :], col(norm_col(0, 1) + c), rstd[:, :],
                                               ALU.mult, ALU.mult))
            step.sync()
            step.do(v.tensor_tensor(xx[:, :, 1:T], hn[:, :, 0:T - 1], hn[:, :, 1:T], ALU.subtract))
            step(v.tensor_scalar(xx[:, :, 0:1], hn[:, :, 0:1], -1.0, None, ALU.mult))

            def mix(s, which):
                if s:
                    dve.wait_ge(s_x, X0[f"m{s}"])
                for c in range(KC):
                    v.scalar_tensor_tensor(xmf[:, c, :], xx[:, c, :], col(VEC["rk_mix"] + 8 * which + c), hn[:, c, :],
                                           ALU.mult, ALU.add).then_inc(s_xm, 1)
                if s >= 2:
                    dve.wait_ge(s_unit, 2 * U0[("rk_k", "rk_v", "lora_wa", "lora_g")[s - 2]])
                split_input(f"m{s}", s % 2, lambda k: xmf[:, k, :], T)

            for x in (R_, K_, V_, A_, B_):
                step.do(v.memset(x[:, :, T:TP], 0.0))
            step.sync()
            mix(0, 0)
            mix(1, 2)
            for u in range(4):
                drain2("rk_r", u, R_[:, 2 * u:2 * u + 2, 0:T])
            mix(2, 3)
            for u in range(4):
                drain2("rk_k", u, K_[:, 2 * u:2 * u + 2, 0:T])
            mix(3, 1)
            for u in range(4):
                drain2("rk_v", u, V_[:, 2 * u:2 * u + 2, 0:T])
            mix(4, 4)
            U, G = U0["lora_wa"], G0["lora_wa"]
            dve.wait_ge(s_unit, 2 * (U + 1))
            v.tensor_copy(lh[0:64, :], PS[0:64, bank(G), 0:T]).then_inc(s_lhd, 1)
            v.tensor_copy(lh[64:128, :], PS[64:128, bank(G) + 1, 0:T]).then_inc(s_free, 1)
            mix(5, 5)
            dve.wait_ge(s_lhh, 1)
            low(lh_l[:, :], lh[:, :], lh_h[:, :], s_lhl)
            U, G = U0["lora_g"], G0["lora_g"]
            dve.wait_ge(s_unit, 2 * (U + 1))
            v.tensor_copy(gh[:, :, :], PS[0:80, bank(G):bank(G) + 2, 0:T]).then_inc(s_free, 1)
            dve.wait_ge(s_ghh, 1)
            low(gh_l[:, :, :], gh[:, :, :], gh_h[:, :, :], s_ghl)
            step.do(v.memset(W_[:, :, T:TP], 0.0))
            step(v.memset(wst[:, :, :], 1.0))
            step(v.memset(wst[:, :, 0:TP:CH], 0.0))
            for m in range(KC):
                G = G0["wa2"] + m
                if m < KC - 1:
                    dve.wait_ge(s_part, m + 1)
                else:
                    dve.wait_ge(s_unit, 2 * (U0["wa2"] + 1))
                v.tensor_scalar(W_[:, m, 0:T], PS[:, bank(G), 0:T], col(VEC["w0"] + m), None, ALU.add).then_inc(s_wa, 1)
                v.tensor_scalar(a_g[:, m, :], PS[:, bank(G) + 1, 0:T], col(VEC["a0"] + m), None, ALU.add).then_inc(s_free, 1)
            for c in range(KC):
                v.tensor_scalar(A_[:, c, 0:T], K_[:, c, 0:T], col(VEC["k_k"] + c), None, ALU.mult).then_inc(s_kk, 1)
            dve.wait_ge(s_dec, 1)
            v.tensor_tensor_scan(Wc[:, :, :].rearrange("p c t -> p (c t)"), wst[:, :, :].rearrange("p c t -> p (c t)"),
                                 W_[:, :, :].rearrange("p c t -> p (c t)"), 0.0, ALU.mult, ALU.add).then_inc(s_cum, 1)
            dve.wait_ge(s_kkr, 1)
            step(v.tensor_scalar(kden[:, :], kden[:, :], 1e-12, None, ALU.max))
            v.reciprocal(kden[:, :], kden[:, :]).then_inc(s_kki, 1)
            for m in range(4):
                dve.wait_ge(s_kkb, m + 1)
                v.tensor_tensor(A_[:, 2 * m:2 * m + 2, 0:T], A_[:, 2 * m:2 * m + 2, 0:T],
                                PS[:, 4 + 2 * (m % 2):6 + 2 * (m % 2), 0:T], ALU.mult).then_inc(s_kkd, 1)
            dve.wait_ge(s_kkd, 4)
            dve.wait_ge(s_dk, 2)
            step(v.tensor_tensor(B_[:, :, 0:T], A_[:, :, 0:T], a_g[:, :, :], ALU.mult))
            step(v.tensor_copy(wend[:, :, :], Wc[:, :, CH - 1:TP:CH]))
            for c in range(KC):
                step.do(v.tensor_scalar(a_g[:, c, :], a_g[:, c, :], 1.0, col(VEC["k_a"] + c), ALU.subtract, ALU.mult))
            step.sync()
            step(v.scalar_tensor_tensor(K_[:, :, 0:T], a_g[:, :, :], 1.0, K_[:, :, 0:T], ALU.add, ALU.mult))
            for c in range(KC):
                v.scalar_tensor_tensor(ktmp[:, c, 0:T], R_[:, c, 0:T], col(VEC["r_k"] + c), K_[:, c, 0:T],
                                       ALU.mult, ALU.mult).then_inc(s_rkr, 1)
            step(v.tensor_scalar(first[:, :, :], A_[:, :, 0:TP:CH], -1.0, None, ALU.mult))
            step(v.scalar_tensor_tensor(A_[:, :, 1:TP], A_[:, :, 1:TP], -1.0, Wc[:, :, 0:TP - 1], ALU.mult, ALU.mult))
            step(v.tensor_copy(A_[:, :, 0:TP:CH], first[:, :, :]))
            step(v.tensor_tensor(R_[:, :, :], R_[:, :, :], Wc[:, :, :], ALU.mult))
            step(v.tensor_tensor(B_[:, :, :], B_[:, :, :], W_[:, :, :], ALU.mult))
            step(v.tensor_tensor(K_[:, :, :], K_[:, :, :], W_[:, :, :], ALU.mult))
            for c in range(KC):
                dve.wait_ge(s_bonm, c + 1)
                v.tensor_tensor(bonus[:, c, :], PS[:, 4 + c % 2, 0:T], V_[:, c, 0:T], ALU.mult).then_inc(s_bon, 1)
            dve.wait_ge(s_bon, KC)

            dve.wait_ge(s_rkc, 16)

            dve.wait_ge(s_lo, 2 * (U0["g2"] + 1))
            for half in range(2):
                for q in (2 * half, 2 * half + 1):
                    c0 = 2 * q
                    for pp in range(2):
                        for n, dst in enumerate((ktok[pp], vtok[pp])):
                            dve.wait_ge(s_tr, 4 * (c0 + pp) + 3 + n)
                            v.tensor_copy(dst[:, :, :], PS[0:BLK, 4 * pp + 2 + n, 0:384].rearrange("p (b f) -> p b f", b=NB)
                                          ).then_inc(s_tkd, 1)
                    for n in range(20):
                        e, ty = n // 5, n % 5
                        dst = (LT[e][:, :], L_[e][:, :], lak[e][:, :], mrb[:, 4 * (q % 2) + e, :], mrk[e][:, :])[ty]
                        dve.wait_ge(s_gm, 20 * q + n + 1)
                        v.tensor_tensor(blocks(dst), blocks(PS[0:BLK, n % 8, 0:TP]), mask((0, 1, 0, 2, 2)[ty]),
                                        ALU.mult).then_inc(s_gr, 1)
                        if ty == 1:
                            dve.wait_ge(s_gr, 20 * q + n + 1)
                            step.do(v.tensor_tensor(blocks(XX[e][:, :]), blocks(L_[e][:, :]), mask(3), ALU.mult))
                            step(v.tensor_tensor(blocks(XT[e][:, :]), blocks(LT[e][:, :]), mask(4), ALU.mult))
                            step.do(v.tensor_tensor(blocks(XX[e][:, :]), blocks(XX[e][:, :]), mask(9), ALU.add))
                            v.tensor_tensor(blocks(XT[e][:, :]), blocks(XT[e][:, :]), mask(9), ALU.add).then_inc(s_xi, 1)
                    for lv in range(4):
                        for e in range(4):
                            dve.wait_ge(s_xt, 16 * q + 4 * lv + e + 1)
                            if lv < 3:
                                step.do(v.tensor_tensor(XX[e][:, :], XX[e][:, :], PS[0:BLK, 4 + e, 0:TP], ALU.add))
                            v.tensor_tensor(XT[e][:, :], XT[e][:, :], PS[0:BLK, e, 0:TP], ALU.add).then_inc(s_xd, 1)
                    for pp in range(2):
                        dve.wait_ge(s_yvm, c0 + pp + 1)
                        v.tensor_copy(K_[:, c0 + pp, :], PS[:, 4 + pp, 0:TP]).then_inc(s_yv, 1)
                    for pp in range(2):
                        dve.wait_ge(s_um, c0 + pp + 1)
                        p = 2 * (q % 2) + pp
                        v.tensor_copy(U_[:, :, p * 128:p * 128 + 128],
                                      PS[0:BLK, 6 + pp, 0:384].rearrange("p (b f) -> p b f", b=NB)).then_inc(s_ue, 1)

                q4 = slice(4 * half, 4 * half + 4)
                dve.wait_ge(s_gv, 4 * half + 4)
                dve.wait_ge(s_ue, 4 * half + 4)
                dve.wait_ge(s_yv, 4 * half + 4)
                for ch in range(NCH):
                    b, r = ch // 3, slice(CH * (ch % 3), CH * (ch % 3) + CH)
                    if ch:
                        dve.wait_ge(s_sam, 8 * half + ch)
                        us = U_[r, b, :].rearrange("s (p e i) -> s e p i", e=2, i=64)
                        v.tensor_tensor(us, us, PS[r, 3:5, 0:256].rearrange("s e (p i) -> s e p i", i=64),
                                        ALU.add).then_inc(s_sau, 1)
                    if ch < NCH - 1:
                        new = S_[(ch + 1) % 2]
                        add = GV[:, ch, :]
                        if ch:
                            step(v.tensor_tensor(St[:, :].rearrange("p (q i) -> p q i", q=4),
                                                 S_[ch % 2][:, :].rearrange("p (q i) -> p q i", q=4),
                                                 wend[:, q4, ch:ch + 1].broadcast_to([128, 4, 64]), ALU.mult))
                            step(v.tensor_tensor(St[:, :], St[:, :], GV[:, ch, :], ALU.add))
                            add = St[:, :]
                        dve.wait_ge(s_dsm, 8 * half + ch + 1)
                        v.tensor_tensor(new[:, :], add, PS[:, 5, 0:256], ALU.add).then_inc(s_s, 1)
                        dve.wait_ge(s_s, 8 * half + ch + 1)
                    if ch:
                        dve.wait_ge(s_ysm, 8 * half + ch)
                        ks = K_[:, q4, ch * CH:ch * CH + CH]
                        v.tensor_tensor(ks, ks, PS[:, 6 + ch % 2, 0:4 * CH].rearrange("p (q t) -> p q t", q=4),
                                        ALU.add).then_inc(s_yse, 1)
                dve.wait_ge(s_yse, 8 * half + 8)
                for p in range(4):
                    dve.wait_ge(s_ym, 4 * half + p + 1)
                    c = 4 * half + p
                    v.tensor_tensor(K_[:, c, :], K_[:, c, :], PS[:, p % 2, 0:TP], ALU.add).then_inc(s_yc, 1)

            dve.wait_ge(s_yc, KC)
            for c in range(KC):
                dve.wait_ge(s_mum, c + 1)
                v.scalar_tensor_tensor(R_[:, c, 0:T], PS[:, 4 + c % 2, 0:T], -1 / HD, K_[:, c, 0:T],
                                       ALU.mult, ALU.add).then_inc(s_yc2, 1)
            dve.wait_ge(s_vm, 1)
            v.tensor_scalar(kden[:, :], PS[0:16, 6, 0:T], 1 / HD, LN_EPS, ALU.mult, ALU.add).then_inc(s_bv, 1)
            dve.wait_ge(s_bvr, 1)
            v.reciprocal(kden[:, :], kden[:, :]).then_inc(s_gni, 1)
            for m in range(4):
                dve.wait_ge(s_gnb, m + 1)
                for n in range(2):
                    c = 2 * m + n
                    ins = v.scalar_tensor_tensor(R_[:, c, 0:T], R_[:, c, 0:T], col(VEC["lnx_g"] + c),
                                                 PS[:, 4 + 2 * (m % 2) + n, 0:T], ALU.mult, ALU.mult)
                    if n:
                        ins.then_inc(s_gnd, 1)
            dve.wait_ge(s_gnd, 4)
            for c in range(KC):
                step.do(v.scalar_tensor_tensor(R_[:, c, 0:T], R_[:, c, 0:T], col(VEC["lnx_b"] + c), bonus[:, c, :],
                                               ALU.add, ALU.add))
            step.sync()
            for g in range(4):
                G = G0["g2"] + g
                if g < 3:
                    dve.wait_ge(s_part, 7 + g + 1)
                else:
                    dve.wait_ge(s_unit, 2 * (U0["g2"] + 1))
                v.tensor_tensor(V_[:, 2 * g:2 * g + 2, 0:T], PS[:, bank(G):bank(G) + 2, 0:T],
                                R_[:, 2 * g:2 * g + 2, 0:T], ALU.mult).then_inc(s_free, 1)
            dve.wait_ge(s_free, G0["g2"] + 4)
            split_input("ro", 1, lambda k: V_[:, k, 0:T], T)
            residual("rk_o", T, 2, 1, 1.0, "f1", gain["f1"], "f1")
            swiglu("f1")

            residual("f1_dn", T, 1, 2, 0.5, "f2", gain["f2"], "f2")
            swiglu("f2")
            residual("f2_dn", T, 1, 2, 0.5, "at", norm_col(1, 1), "at")
            rms("at", T)
            for name, c0 in (("at_q", 0), ("at_k", 8), ("at_qi", 12), ("at_tail", 16)):
                for u in range(UN[name]):
                    drain_normed(name, u, rawq[:, c0 + 2 * u:c0 + 2 * u + 2, :], T)
            dve.wait_ge(s_rcm, 1)
            step(v.tensor_copy(rcol_a[0:BLK, :, :], PS[0:BLK, 6, 0:12].rearrange("p (j c) -> p j c", c=4)))
            U, G = U0["at_v"], G0["at_v"]
            dve.wait_ge(s_unit, 2 * (U + 1))
            for j in range(NB):
                kn = min(BLK, T - BLK * j)
                ins = v.tensor_scalar(vt[0:kn, j, :], PS[0:kn, bank(G) + j // 2, (j % 2) * 256:(j % 2) * 256 + 256],
                                      rcol_a[0:kn, j, 0:1], None, ALU.mult)
                ins.then_inc(s_free if j == 2 else s_dve, 1)
            step.n += 2
            dve.wait_ge(s_free, G + 1)
            dve.wait_ge(s_dsc, 48)
            head_norms("at")
            dve.wait_ge(s_wtm, 1)
            v.tensor_scalar(wit[:, :, :], PS[:, 0, 0:16].rearrange("p (b f) -> p b f", b=2),
                            float(8 ** -0.5 * 64 ** -0.5), None, ALU.mult).then_inc(s_wt, 1)
            dve.wait_ge(s_wt, 1)
            for b in range(2):
                nk = META + 128 * (b + 1)
                for hd in range(8):
                    n = b * 8 + hd
                    dve.wait_ge(s_rl, n + 1)
                    if hd == 0:
                        ins = v.tensor_scalar(score[:, b, 0:nk], rel[:, n % 2, 0:nk], wit[:, b, 0:1], None, ALU.mult)
                    else:
                        ins = v.scalar_tensor_tensor(score[:, b, 0:nk], rel[:, n % 2, 0:nk], wit[:, b, hd:hd + 1],
                                                     score[:, b, 0:nk], ALU.mult, ALU.add)
                    ins.then_inc(s_ra, 1)
                    dve.wait_ge(s_ra, n + 1)
            for b in range(2):
                nk = META + 128 * (b + 1)
                step(v.tensor_tensor(taken[0][:, b, 0:nk], score[:, b, 0:nk], cap[:, b, 0:nk], ALU.min))
                for rnd in range(TOPK // 8):
                    src, dst = taken[rnd % 2][:, b, 0:nk], taken[(rnd + 1) % 2][:, b, 0:nk]
                    step(v.max(m8[:, :], src))
                    step(v.match_replace(dst, m8[:, :], src, TAKEN))
                step(v.tensor_scalar(taken[0][:, b, 0:nk], taken[0][:, b, 0:nk], TAKEN, 1.0, ALU.is_equal, ALU.subtract))
                step(v.scalar_tensor_tensor(taken[0][:, b, 0:nk], taken[0][:, b, 0:nk], -NEG, cap[:, b, 0:nk],
                                            ALU.mult, ALU.min))
            attention("at")
            dve.wait_ge(s_ol, 32)
            residual("at_o", SEQ, 2, 1, 1.0, "f3", gain["f3"], "f3")
            swiglu("f3")

            residual("f3_dn", SEQ, 1, 2, 0.5, "b", VEC["norm_mix"], "b")
            rms("b", SEQ)
            for u in range(2):
                drain_normed("b_qa", u, qka[:, 2 * u:2 * u + 2, :], SEQ)
            dve.wait_ge(s_bc, 96)
            step(v.tensor_copy(posf[:, :], posi[:, :]))
            step(v.tensor_scalar(ang[:, :], posf[:, :], freq[:, 0:1], None, ALU.mult))
            for n, (turn, shift) in enumerate(((0.25, math.pi / 2), (0.0, 0.0))):
                step(v.tensor_scalar(posf[:, :], ang[:, :], 1 / (2 * math.pi), turn, ALU.mult, ALU.add))
                step(v.tensor_scalar(posf[:, :], posf[:, :], MAGIC, None, ALU.add))
                step(v.tensor_scalar(posf[:, :], posf[:, :], MAGIC, None, ALU.subtract))
                step(v.scalar_tensor_tensor(red[:, :], posf[:, :], -C1, ang[:, :], ALU.mult, ALU.add))
                for part in (C2, C3):
                    step(v.scalar_tensor_tensor(red[:, :], posf[:, :], -part, red[:, :], ALU.mult, ALU.add))
                step(v.tensor_scalar(red[:, :], red[:, :], shift, PI, ALU.add, ALU.min))
                v.tensor_scalar(cs_b[:, n, :], red[:, :], -PI, None, ALU.max).then_inc(s_ang, 1)
            for u in range(2):
                drain_normed("b_ka", u, qka[:, 4 + 2 * u:6 + 2 * u, :], SEQ)
            dve.wait_ge(s_rcm, 2)
            step(v.tensor_copy(rcol_b[:, :, :], PS[:, 6, 0:8].rearrange("p (j c) -> p j c", c=4)))
            for u in range(2):
                U, G = U0["b_va"] + u, G0["b_va"] + u
                dve.wait_ge(s_unit, 2 * (U + 1))
                for j in range(2):
                    ins = v.tensor_scalar(vat[:, j, u * 256:u * 256 + 256], PS[:, bank(G) + j, 0:256],
                                          rcol_b[:, j, 0:1], None, ALU.mult)
                    ins.then_inc(s_free if j else s_dve, 1)
                step.n += 1
            for u in range(3):
                drain_normed("b_cq", u, craw[:, 2 * u:2 * u + 2, :], SEQ)
            drain_normed("b_ckv", 0, craw[:, 6:8, :], SEQ)
            U, G = U0["b_tail"], G0["b_tail"]
            dve.wait_ge(s_unit, 2 * (U + 1))
            v.tensor_tensor(krope[64:96, :], PS[64:96, bank(G), 0:SEQ], rstd[64:96, 0:SEQ], ALU.mult).then_inc(s_free, 1)
            dve.wait_ge(s_free, G + 1)
            for hd in range(8):
                dve.wait_ge(s_bwm, hd + 1)
                v.tensor_copy(biasw[:, hd, :], PS[:, 4 + hd % 2, 0:384]).then_inc(s_bw, 1)
            dve.wait_ge(s_sin, 2)
            step(v.tensor_scalar(cs_b[:, 1, :], cs_b[:, 1, :], freq[:, 1:2], None, ALU.mult))
            for k in range(8):
                dve.wait_ge(s_csq, k + 1)
                n = 0 if k < 6 else 1
                if k in (0, 6):
                    ins = v.tensor_copy(bt[:, n, :], csq[:, k, :])
                else:
                    ins = v.tensor_tensor(bt[:, n, :], bt[:, n, :], csq[:, k, :], ALU.add)
                ins.then_inc(s_css, 1)
                dve.wait_ge(s_css, k + 1)
            for n, width in enumerate((768, 256)):
                dve.wait_ge(s_cnm, n + 1)
                v.tensor_scalar(cvr[:, n, :], PS[:, 6 + n, 0:SEQ], 1 / width, EPS, ALU.mult, ALU.add).then_inc(s_cv, 1)
            dve.wait_ge(s_cst, 2)
            step(v.reciprocal(cvr[:, :, :], cvr[:, :, :]))
            for k in range(8):
                g = VEC["cq_g"] + k if k < 6 else VEC["ckv_g"] + k - 6
                v.scalar_tensor_tensor(cxf[:, k, :], craw[:, k, :], col(g), cvr[:, 0 if k < 6 else 1, :],
                                       ALU.mult, ALU.mult).then_inc(s_xm, 1)
            split_input("cq", 1, lambda k: cxf[:, k, :], SEQ, range(8))
            for u in range(4):
                drain2("b_uq", u, qkb[:, 2 * u:2 * u + 2, :], slice(0, 96), SEQ)
            for hd in range(8):
                step.do(v.tensor_copy(qkb[64:96, 8 + hd, :], krope[64:96, :]))
            for g in range(2):
                G = G0["b_ukv"] + g
                dve.wait_ge(s_part, 10 + g + 1)
                pair = qkb[0:64, 8 + 4 * g:12 + 4 * g, :].rearrange("p (a e) t -> p a e t", e=2)
                step.do(v.tensor_copy(pair[:, :, 0, :], PS[0:64, bank(G):bank(G) + 2, 0:SEQ]))
                v.tensor_copy(pair[:, :, 1, :], PS[64:128, bank(G):bank(G) + 2, 0:SEQ]).then_inc(s_free, 1)
            U, G = U0["b_ukv"], G0["b_ukv"] + 2
            dve.wait_ge(s_unit, 2 * (U + 1))
            v.tensor_copy(vbt[:, :, :], PS[:, bank(G):bank(G) + 2, 0:512]).then_inc(s_free, 1)
            dve.wait_ge(s_free, G + 1)
            head_norms("b")
            dve.wait_ge(s_hsc, NT0["b"] + 12)
            dve.wait_ge(s_bld, 128)
            attention("b")
            dve.wait_ge(s_ol, 64)
            residual("b_o", SEQ, 2, 1, 1.0, "ff", VEC["norm_ffn"], "ff")

            def ff1(us, i):
                us = list(us)

                def tail(u):
                    dve.wait_ge(s_hf2, val(u + 1, i, 4))
                    o = slice(2 * u * SEQ, 2 * u * SEQ + 2 * SEQ) if i is None else bass.ds(i * (8 * SEQ) + 2 * u * SEQ, 2 * SEQ)
                    low(hid2_l[:, o], hidf2[:, u % 2, :, :].rearrange("p m n -> p (m n)"), hid2_h[:, o], s_hlo2)
                for k, u in enumerate(us):
                    U, G = U0["b_ff1"] + u, G0["b_ff1"] + u
                    dve.wait_ge(s_unit, val(2 * (U + 1), i, 8))
                    if u == 0:
                        rms("ff", SEQ)
                    v.scalar_tensor_tensor(act2[:, u % 2, :, :], PS[:, bank(G):bank(G) + 2, 0:SEQ], 0.0,
                                           rstd[:, 0:SEQ].unsqueeze(1).broadcast_to([128, 2, SEQ]),
                                           ALU.max, ALU.mult).then_inc(s_free, 1)
                    if k:
                        tail(u - 1)
                tail(us[-1])
            ff1(range(4), None)
            with step.loop(3, 0) as i:
                ff1(range(4, 8), i)
            for m in range(KC):
                U, G = U0["b_ff2"] + 2 * m + 1, G0["b_ff2"] + m
                dve.wait_ge(s_unit, 2 * (U + 1))
                v.tensor_tensor(outt[:, m, :], PS[:, bank(G), 0:SEQ], hv(SEQ, m)[:, 0, :], ALU.add).then_inc(s_free, 1)

        @block.scalar
        def _(act):
            a = nc.scalar
            step = Link(act, s_act)
            widths = [w for _n, n, _m, w in STAGES for _ in range(n)]

            def f(out, in_, func, **kw):
                return a.activation(out, in_, func, **kw)

            def hi(U, i=None, k=4, w=None):
                if U >= UNITS:
                    return
                w = widths[U] if w is None else w
                act.wait_ge(s_raw[U % RAW], val(16 * (U // RAW + 1), i, 4 * k))
                for q, part in enumerate(halves(w)):
                    if U >= SPL:
                        act.wait_ge(s_unit, val(2 * (U - SPL) + q + 1, i, 2 * k))
                    f(whi[U % SPL][:, part], raw[U % RAW][:, part], ACT.Copy).then_inc(s_hi, 1)

            def ahead(name, norm=None, n=T):
                for u in range(UN[name]):
                    hi(U0[name] + u + 1)
                    if u == 0 and norm:
                        root(norm, n)

            def last_width(name, u):
                return max(UW[name], widths[U0[name] + UN[name]])

            def root(name, n):
                act.wait_ge(s_var, N0[name] + 1)
                f(rstd[:, 0:n], rstd[:, 0:n], ACT.Sqrt).then_inc(s_std, 1)

            def swiglu_in(fn):
                n, name, hb = tok[fn], fn + "_in", HB[fn]

                def high(u, i):
                    act.wait_ge(s_hid, val(hb + u + 1, i, 4))
                    o = slice(u * T, u * T + n) if i is None else bass.ds(i * (4 * T) + u * T, n)
                    f(hid_h[:, o], hidf[:, u % 2, 0:n], ACT.Copy).then_inc(s_hhi, 1)

                def body(us, i):
                    us = list(us)
                    for k, u in enumerate(us):
                        w = last_width(name, u) if u == us[-1] else UW[name]
                        hi(U0[name] + u + 1, i, 4, w)
                        if u == 0:
                            root(fn, n)
                        act.wait_ge(s_gate, val(hb + u + 1, i, 4))
                        f(sig[:, u % 2, 0:n], gate[:, u % 2, 0:n], ACT.Sigmoid).then_inc(s_sig, 1)
                        if k >= 1:
                            high(u - 1, i)
                    high(us[-1], i)
                turns(step, FC, 4, 0, body)

            def residual(name, n, w, units, norm, split):
                def body(js, i):
                    for j in js:
                        for k in range(units):
                            u = units * j + k + 1
                            ww = UW[name]
                            if i is not None and j == list(js)[-1] and k == units - 1:
                                ww = last_width(name, u)
                            hi(U0[name] + u, i, 4 * units, ww if i is not None else None)
                        G = G0[name] + j
                        act.wait_ge(s_free, val(G + 1, i, 4))
                        if j >= 2 or norm != "f0":
                            pass
                        x = hv(n, j * w, j * w + w) if i is None else h[:, bass.ds(i * 4 + j, 1), T - n:T]
                        f(sq[:, j % 2, 0:w, 0:n], x, ACT.Square).then_inc(s_sq, 1)
                        for q in range(w if split else 0):
                            m = j * w + q
                            act.wait_ge(s_xm, val(XM0[split] + m + 1, i, 4))
                            o = slice(m, m + 1) if i is None else bass.ds(i * 4 + m, 1)
                            f(xh[0][:, o, 0:n].rearrange("p o n -> p (o n)"), xg[:, j % 2, q, 0:n], ACT.Copy).then_inc(s_xh, 1)
                turns(step, 8 // w, 4, 0, body)

            def split_input(name, b, made, n, chunks=range(KC)):
                for k in chunks:
                    act.wait_ge(s_xm, XM0[name] + k + 1)
                    f(xh[b][:, k, 0:n], made(k), ACT.Copy).then_inc(s_xh, 1)

            def head_norms(which):
                tiles = TILES[which]
                for g in groups(which):
                    for j in range(g[0], g[1]):
                        x = tiles[j]
                        c, _r = counts(which, j)
                        if c > 2:
                            act.wait_ge(s_hsum, c - 2)
                        f(sqp[c % 2][0:x["rows"], :, 0:x["n"]], x["x"], ACT.Square).then_inc(s_hsq, 1)
                for g in groups(which):
                    n, o = tiles[g[0]]["n"], hinv[g[3] % 2]
                    act.wait_ge(s_hvar, g[3] + 1)
                    f(o[0:g[2], 0:n], o[0:g[2], 0:n], ACT.Sqrt).then_inc(s_hroot, 1)

            def attention(which):
                jobs, j0 = JOBS[which]
                for j in range(len(jobs) + 4):
                    if j < len(jobs):
                        x, c = jobs[j], j0 + j
                        nk = x["nk"]
                        act.wait_ge(s_lg, c + 1)
                        if j >= 2:
                            act.wait_ge(s_prn, c - 1)
                        f(pr[:, c % 2, 0:nk], lg[:, c % 2, 0:nk], ACT.Exp, bias=nmx[:, c:c + 1],
                          accum_out=asum[:, c:c + 1]).then_inc(s_ex, 1)
                    if 0 <= j - 2 < len(jobs):
                        x, c = jobs[j - 2], j0 + j - 2
                        act.wait_ge(s_ptm, c + 1)
                        if j - 2 >= 2:
                            act.wait_ge(s_om, c - 1)
                        nv = len(x["v"])
                        if which == "at":
                            short = x["v"][-1][2]
                            f(pts[0:BLK, c % 2, 0:nv - 1, :], PS[0:BLK, 2 + c % 2, 0:(nv - 1) * 128].rearrange(
                                "p (n q) -> p n q", q=128), ACT.Copy).then_inc(s_act, 1)
                            step.n += 1
                            f(pts[0:short, c % 2, nv - 1, :], PS[0:short, 2 + c % 2, (nv - 1) * 128:nv * 128],
                              ACT.Copy).then_inc(s_pte, 1)
                        else:
                            f(pts[:, c % 2, 0:nv, :], PS[:, 2 + c % 2, 0:nv * 128].rearrange("p (n q) -> p n q", q=128),
                              ACT.Copy).then_inc(s_pte, 1)
                    if 0 <= j - 3 < len(jobs):
                        x, c = jobs[j - 3], j0 + j - 3
                        r = slice(64 * (x["head"] % 2), 64 * (x["head"] % 2) + 64)
                        act.wait_ge(s_om, c + 1)
                        f(xh[1][r, x["head"] // 2, 128 * x["b"]:128 * x["b"] + 128], PS[r, 4 + c % 2, 0:128],
                          ACT.Copy).then_inc(s_oh, 1)

            act.dma_start(masks[:, :, :], t["scan"].rearrange("p (k s) -> p k s", s=BLK)).then_inc(s_rkc, 16)
            hi(0)
            act.wait_ge(s_h0, 16)
            for m in range(KC):
                if m >= 2:
                    act.wait_ge(s_ssa, m - 1)
                f(sq[:, m % 2, 0, :], h[:, m, :], ACT.Square).then_inc(s_sq, 1)
                act.wait_ge(s_xm, m + 1)
                f(xh[0][:, m, :], xg[:, (m // 2) % 2, m % 2, :], ACT.Copy).then_inc(s_xh, 1)
            swiglu_in("f0")
            residual("f0_dn", T, 1, 2, "rk", None)

            root("rk", T)

            def mixed(s):
                if s >= 2:
                    act.wait_ge(s_unit, 2 * U0[("rk_k", "rk_v", "lora_wa", "lora_g")[s - 2]])
                split_input(f"m{s}", s % 2, lambda k: xmf[:, k, :], T)
            mixed(0)
            mixed(1)
            ahead("rk_r")
            mixed(2)
            ahead("rk_k")
            mixed(3)
            ahead("rk_v")
            mixed(4)
            hi(U0["lora_wa"] + 1)
            act.wait_ge(s_lhd, 1)
            step(f(lh[0:64, :], lh[0:64, :], ACT.Tanh))
            act.wait_ge(s_free, G0["lora_wa"] + 1)
            f(lh_h[:, :], lh[:, :], ACT.Copy).then_inc(s_lhh, 1)
            mixed(5)
            hi(U0["lora_g"] + 1)
            act.wait_ge(s_free, G0["lora_g"] + 1)
            step(f(gh[:, :, :], gh[:, :, :], ACT.Sigmoid))
            f(gh_h[:, :, :], gh[:, :, :], ACT.Copy).then_inc(s_ghh, 1)
            hi(U0["wa2"] + 1)
            act.wait_ge(s_wa, KC)
            f(W_[:, :, 0:T], W_[:, :, 0:T], ACT.Sigmoid).then_inc(s_dec, 1)
            act.wait_ge(s_free, G0["wa2"] + KC)
            step(f(a_g[:, :, :], a_g[:, :, :], ACT.Sigmoid))
            act.wait_ge(s_kk, KC)
            f(ktmp[:, :, 0:T], A_[:, :, 0:T], ACT.Square).then_inc(s_kksq, 1)
            act.wait_ge(s_cum, 1)
            f(W_[:, :, :], Wc[:, :, :], ACT.Exp, scale=math.exp(-0.5)).then_inc(s_dk, 1)
            f(Wc[:, :, :], Wc[:, :, :], ACT.Exp, scale=-math.exp(-0.5)).then_inc(s_dk, 1)
            act.wait_ge(s_kkm, 1)
            f(kden[:, :], PS[0:16, 4, 0:T], ACT.Sqrt).then_inc(s_kkr, 1)
            for q in range(4):
                c0 = 2 * q
                for pp in range(2):
                    p = 2 * (q % 2) + pp
                    for n, dst in enumerate((atok[pp][:, :, :], btok[:, :, p * 128:p * 128 + 128])):
                        act.wait_ge(s_tr, 4 * (c0 + pp) + n + 1)
                        f(dst, PS[0:BLK, 4 * pp + n, 0:384].rearrange("p (b f) -> p b f", b=NB), ACT.Copy).then_inc(s_tka, 1)
                for lv in range(4):
                    for e in range(4):
                        act.wait_ge(s_q, 16 * q + 4 * lv + e + 1)
                        f(QQ[e][:, :], PS[0:BLK, e, 0:TP], ACT.Copy).then_inc(s_qc, 1)
                for pp in range(2):
                    act.wait_ge(s_p1, c0 + pp + 1)
                    f(p1[pp][:, :, :], PS[0:BLK, pp, 0:384].rearrange("p (b f) -> p b f", b=NB), ACT.Copy).then_inc(s_p1c, 1)
                for pp in range(2):
                    act.wait_ge(s_ztm, c0 + pp + 1)
                    f(A_[:, c0 + pp, :], PS[:, 2 + pp, 0:TP], ACT.Copy).then_inc(s_zt, 1)
                for pp in range(2):
                    p = 2 * (q % 2) + pp
                    act.wait_ge(s_gvm, c0 + pp + 1)
                    f(GV[:, :, p * 64:p * 64 + 64].rearrange("q (b j) i -> q j b i", j=3),
                      PS[:, 3 * pp:3 * pp + 3, 0:192].rearrange("q j (b i) -> q j b i", i=64),
                      ACT.Copy).then_inc(s_gv, 1)
            for c in range(KC):
                act.wait_ge(s_yc2, c + 1)
                f(A_[:, c, 0:T], R_[:, c, 0:T], ACT.Square).then_inc(s_ysq, 1)
            act.wait_ge(s_bv, 1)
            f(kden[:, :], kden[:, :], ACT.Sqrt).then_inc(s_bvr, 1)
            hi(U0["g2"] + 1)
            for k in range(KC):
                act.wait_ge(s_free, G0["g2"] + k // 2 + 1)
                f(xh[1][:, k, :], V_[:, k, 0:T], ACT.Copy).then_inc(s_xh, 1)
            residual("rk_o", T, 2, 1, "f1", "f1")
            swiglu_in("f1")

            residual("f1_dn", T, 1, 2, "f2", "f2")
            swiglu_in("f2")
            residual("f2_dn", T, 1, 2, "at", "at")
            for dst, name in ((rot_a[:, :], "rot_a"), (cs_a[:, :, :], "cs_a"), (cap[:, :, :], "cap")):
                src = t[name] if name == "rot_a" else t[name].rearrange("p (c n) -> p c n", c=2)
                act.dma_start(dst, src).then_inc(s_dsc, 16)
            ahead("at_q", "at")
            for name in ("at_k", "at_qi", "at_tail", "at_v"):
                ahead(name)
            act.wait_ge(s_free, G0["at_v"] + 1)
            head_norms("at")
            for n in range(16):
                nk = META + 128 * (n // 8 + 1)
                act.wait_ge(s_rlm, n + 1)
                if n >= 2:
                    act.wait_ge(s_ra, n - 1)
                f(rel[:, n % 2, 0:nk], PS[:, 2 + n % 2, 0:nk], ACT.Relu).then_inc(s_rl, 1)
            attention("at")
            residual("at_o", SEQ, 2, 1, "f3", "f3")
            swiglu_in("f3")

            residual("f3_dn", SEQ, 1, 2, "b", "b")
            for dst, name in ((causal, "causal"), (rot_b, "rot_b"), (freq, "freq"), (distt, "dist")):
                act.dma_start(dst[:, :], t[name]).then_inc(s_bc, 16)
            act.dma_start(relb[:, :, :], t["relb"]).then_inc(s_bc, 16)
            act.dma_start(posi[:, :], t["pos"].broadcast_to([128, SEQ])).then_inc(s_bc, 16)
            ahead("b_qa", "b", SEQ)
            ahead("b_ka")
            for n in range(2):
                act.wait_ge(s_ang, n + 1)
                f(cs_b[:, n, :], cs_b[:, n, :], ACT.Sin).then_inc(s_sin, 1)
            for name in ("b_va", "b_cq", "b_ckv", "b_tail"):
                ahead(name)
            for k in range(8):
                if k == 0:
                    act.wait_ge(s_free, G0["b_tail"] + 1)
                f(csq[:, k, :], craw[:, k, :], ACT.Square).then_inc(s_csq, 1)
            for n in range(2):
                act.wait_ge(s_cv, n + 1)
                f(cvr[:, n, :], cvr[:, n, :], ACT.Sqrt).then_inc(s_cst, 1)
            split_input("cq", 1, lambda k: cxf[:, k, :], SEQ, range(8))
            act.wait_ge(s_bw, 8)
            act.dma_start(t["rows"].rearrange("(p w) -> p w", p=128), biasw[:, :, :].rearrange("p h x -> p (h x)")
                          ).then_inc(s_bst, 16)
            for name in ("b_uq", "b_ukv"):
                ahead(name)
            act.wait_ge(s_bst, 16)
            pitch = 8 * 384 - 1
            skewed = t["rows"][127:127 + 128 * pitch].rearrange("(p w) -> p w", w=pitch)
            for hd in range(8):
                act.dma_start(bias[:, hd, :], skewed[:, hd * 384:hd * 384 + 256]).then_inc(s_bld, 16)
            act.wait_ge(s_free, G0["b_ukv"] + 3)
            head_norms("b")
            attention("b")
            residual("b_o", SEQ, 2, 1, "ff", "ff")

            def ff1(us, i):
                for u in us:
                    hi(U0["b_ff1"] + u + 1, i, 4, 2048)
                    if u == 0:
                        root("ff", SEQ)
                    act.wait_ge(s_free, val(G0["b_ff1"] + u + 1, i, 4))
                    step.do(f(hidf2[:, u % 2, :, :], act2[:, u % 2, :, :], ACT.Square))
                    o = slice(2 * u * SEQ, 2 * u * SEQ + 2 * SEQ) if i is None else bass.ds(i * (8 * SEQ) + 2 * u * SEQ, 2 * SEQ)
                    f(hid2_h[:, o], act2[:, u % 2, :, :].rearrange("p m n -> p (m n)"), ACT.Square).then_inc(s_hf2, 1)
            ff1(range(4), None)
            with step.loop(3, 4) as i:
                ff1(range(4, 8), i)
            for u in range(16):
                hi(U0["b_ff2"] + u + 1)


def tiles(w, cols):
    k, n = w.shape[0] // 128, w.shape[1] // cols
    return np.ascontiguousarray(w.reshape(k, 128, n, cols).transpose(2, 1, 0, 3)).reshape(n, 128, k * cols)


def pairs(w):
    n = w.shape[1] // 256
    x = w.reshape(KC, 128, n, 2, 128).transpose(2, 1, 3, 0, 4)
    return np.ascontiguousarray(x).reshape(n, 128, 2048)


def down_units(w, parts):
    k = w.shape[0] // 128 // parts
    x = w.reshape(parts, k, 128, 8, 128).transpose(3, 0, 2, 1, 4)
    return np.ascontiguousarray(x).reshape(8 * parts, 128, k * 128)


def columns(x):
    return x.reshape(-1, 128).T


def layout(inp):
    f = {k: np.asarray(v) for k, v in inp.items()}
    out = {}
    x = np.concatenate([f["meta"], f["x"][0]], 0)
    out["h0"] = np.ascontiguousarray(x.T.reshape(KC, 128, T).transpose(1, 0, 2))
    for i in range(4):
        w = f["ffn_w_in"][i // 2, i % 2]
        w = w.reshape(D, 2, FC, 128).transpose(0, 2, 1, 3).reshape(D, 2 * FF)
        out[f"w_f{i}_in"] = pairs(w)
        out[f"w_f{i}_dn"] = down_units(f["ffn_w_out"][i // 2, i % 2], 2)
    for name in "rkvo":
        out["w_rk_" + name] = pairs(f["rk_w_" + name][0])
    out["w_lora_wa"] = tiles(np.concatenate([f["rk_w1"][0], f["rk_a1"][0]], 1), 128)
    out["w_lora_g"] = tiles(f["rk_g1"][0], 160)
    out["w_wa2"] = np.concatenate([f["rk_w2"][0], f["rk_a2"][0]], 0)[None]
    g2 = np.zeros((1, 128, 2, D), np.float32)
    g2[0, 0:80] = f["rk_g2"][0].reshape(2, 80, D).transpose(1, 0, 2)
    out["w_g2"] = g2.reshape(1, 128, 2 * D)
    w = f["at_w_in"][0]
    out["w_at_q"] = pairs(w[:, 0:1024])
    k = w[:, 1024:1280].reshape(D, 4, 1, 64)
    out["w_at_k"] = pairs(np.concatenate([k, k], 2).reshape(D, 512))
    out["w_at_v"] = tiles(w[:, 1280:1536], 256)
    out["w_at_qi"] = pairs(w[:, 1536:2048])
    ki, wi = w[:, 2048:2112], w[:, 2112:2120]
    out["w_at_tail"] = pairs(np.concatenate([ki, ki, wi, np.zeros((D, 120), np.float32)], 1))
    out["w_at_o"] = pairs(f["at_w_o"][0])
    w = f["w_in_2"]
    out["w_b_qa"], out["w_b_ka"] = pairs(w[:, 0:512]), pairs(w[:, 512:1024])
    out["w_b_va"], out["w_b_cq"] = tiles(w[:, 1024:1536], 256), pairs(w[:, 1536:2304])
    out["w_b_ckv"] = pairs(w[:, 2304:2560])
    z = np.zeros((D, 64), np.float32)
    out["w_b_tail"] = tiles(np.concatenate([z, w[:, 2560:2592], z[:, 0:32]], 1), 128)
    out["w_b_uq"] = tiles(f["w_uq_2"], 192)
    kv = f["w_ukv_2"].reshape(256, 8, 128)
    out["w_b_ukv"] = tiles(np.concatenate([kv[:, :, 0:64].reshape(256, 512), kv[:, :, 64:].reshape(256, 512)], 1), 1024)
    out["w_b_o"] = pairs(f["w_o_2"])
    out["w_b_ff1"] = pairs(f["w_ff1_2"])
    out["w_b_ff2"] = down_units(f["w_ff2_2"], 2)
    vecs = [f["norm_g"], f["rk_mix"], f["rk_w0"], f["rk_a0"], f["rk_k_k"], f["rk_k_a"], f["rk_r_k"],
            f["rk_lnx_g"], f["rk_lnx_b"], f["norm_mix_g_2"], f["norm_ffn_g_2"], f["cq_norm_g_2"], f["ckv_norm_g_2"]]
    vecs += [np.concatenate([f[n].reshape(-1)] * 2) for n in ("at_q_g", "at_k_g", "qnorm_a_g_2", "knorm_a_g_2")]
    vecs += [np.concatenate([f[n], np.zeros(32, np.float32)]) for n in ("qnorm_b_g_2", "knorm_b_g_2")]
    out["vec"] = np.ascontiguousarray(np.concatenate([columns(x) for x in vecs], 1))
    rb = np.concatenate([f["rel_bias_2"], np.ones((1, 8), np.float32)], 0)
    out["relb"] = np.ascontiguousarray(np.repeat(rb[:, :, None], 128, 2))
    out["pos"] = f["positions_2"].reshape(1, SEQ)
    out.update(shape_constants())
    return {k: np.ascontiguousarray(x) for k, x in out.items()}


def kernel(**inputs):
    import concourse.bacc as bacc
    from concourse.bass_utils import run_bass_kernel_spmd

    nc = bacc.Bacc("TRN2", target_bir_lowering=False, num_devices=1)
    arrays = layout(inputs)
    t = {}
    for name, x in arrays.items():
        t[name] = nc.dram_tensor(name + "_in", x.shape, mybir.dt.from_np(x.dtype), kind="ExternalInput").ap()
    t["out"] = nc.dram_tensor("result", [128, KC, SEQ], F32, kind="ExternalOutput").ap()
    t["rows"] = nc.dram_tensor("bias_rows_scratch", [128 * 8 * 384], F32, kind="Internal").ap()
    build(nc, t)
    r = run_bass_kernel_spmd(nc, [{n + "_in": x for n, x in arrays.items()}], core_ids=[0])
    y = r.results[0]["result"]
    return y.transpose(2, 1, 0).reshape(1, SEQ, D)
```

```python
import math
from contextlib import ExitStack, contextmanager

import numpy as np

import concourse.bass as bass
from concourse import mybir

F32 = mybir.dt.float32
F32R = mybir.dt.float32r
I32 = mybir.dt.int32
ALU = mybir.AluOpType
ACT = mybir.ActivationFunctionType
AX = mybir.AxisListType

D = 1024
KC = D // 128
META = 16
SEQ = 256
T = META + SEQ
FF = 2816
FC = FF // 128
FF2 = 4096
HD = 64
EPS = 1e-6
LN_EPS = 64e-5
H_A = 16
TOPK = 64
BLK = 96
CH = 32
NCH = 9
NB = 3
TP = NB * BLK
NEG = -1.0e30
CAP = 3.0e38
TAKEN = -3.4e38

STAGES = [
    ("f0_in", 22, 22, 2048), ("f0_dn", 16, 8, 1408),
    ("rk_r", 4, 4, 2048), ("rk_k", 4, 4, 2048), ("rk_v", 4, 4, 2048),
    ("lora_wa", 1, 1, 1024), ("lora_g", 1, 1, 1280), ("wa2", 1, 8, 1024),
    ("g2", 1, 4, 2048), ("rk_o", 4, 4, 2048),
    ("f1_in", 22, 22, 2048), ("f1_dn", 16, 8, 1408),
    ("f2_in", 22, 22, 2048), ("f2_dn", 16, 8, 1408),
    ("at_q", 4, 4, 2048), ("at_k", 2, 2, 2048), ("at_qi", 2, 2, 2048), ("at_tail", 1, 1, 2048),
    ("at_v", 1, 1, 2048), ("at_o", 4, 4, 2048),
    ("f3_in", 22, 22, 2048), ("f3_dn", 16, 8, 1408),
    ("b_qa", 2, 2, 2048), ("b_ka", 2, 2, 2048), ("b_va", 2, 2, 2048), ("b_cq", 3, 3, 2048),
    ("b_ckv", 1, 1, 2048), ("b_tail", 1, 1, 1024), ("b_uq", 4, 4, 1152), ("b_ukv", 1, 3, 2048),
    ("b_o", 4, 4, 2048), ("b_ff1", 16, 16, 2048), ("b_ff2", 16, 8, 2048),
]
U0, G0, UN, GN, UW = {}, {}, {}, {}, {}
_u = _g = 0
for _name, _n, _m, _w in STAGES:
    U0[_name], G0[_name], UN[_name], GN[_name], UW[_name] = _u, _g, _n, _m, _w
    _u += _n
    _g += _m
UNITS = _u

RAW = 4
SPL = 2


def halves(w):
    cut = 1024 if w > 1024 else w // 2
    return (slice(0, cut), slice(cut, w))

VEC = {}
_c = 0
for _name, _n in [("norm_g", 48), ("rk_mix", 48), ("w0", 8), ("a0", 8), ("k_k", 8), ("k_a", 8),
                  ("r_k", 8), ("lnx_g", 8), ("lnx_b", 8), ("norm_mix", 8), ("norm_ffn", 8),
                  ("cq_g", 6), ("ckv_g", 2), ("q_g", 1), ("k_g", 1), ("qa_g", 1), ("ka_g", 1),
                  ("qb_g", 1), ("kb_g", 1)]:
    VEC[_name] = _c
    _c += _n
NVEC = _c

LEVELS = (2, 4, 8, 16)


def norm_col(layer, which):
    return VEC["norm_g"] + (layer * 3 + which) * KC


def shape_constants():
    c = {}
    c["ident"] = np.eye(128, dtype=np.float32)
    c["ones"] = np.ones((128, 128), np.float32)
    half = np.arange(128) // 64
    c["bo64"] = (half[:, None] == half[None, :]).astype(np.float32)
    c["sel"] = np.zeros((128, 88), np.float32)
    c["sel"][np.arange(128), 30 + half] = 1.0
    c["sel"][:96, 56 + 15] = 1.0
    s = np.arange(BLK)
    same = (s[:, None] // CH) == (s[None, :] // CH)
    strict_t = same & (s[:, None] < s[None, :])
    m = [strict_t, strict_t.T, same & (s[:, None] <= s[None, :])]
    lvl = []
    for size in (1,) + LEVELS:
        lo = (s[:, None] // (2 * size) == s[None, :] // (2 * size)) & \
             (s[:, None] // size % 2 == 1) & (s[None, :] // size % 2 == 0)
        lvl.append(lo)
    m += [lvl[0], lvl[0].T] + [x.T for x in lvl[1:]] + [np.eye(BLK, dtype=bool)]
    scan = np.stack([x.astype(np.float32) for x in m], 1)
    c["scan"] = np.zeros((128, 10 * BLK), np.float32)
    c["scan"][:BLK] = scan.reshape(BLK, -1)
    rot = np.zeros((128, 128), np.float32)
    for b in (0, 64):
        for i in range(8):
            rot[b + i + 8, b + i] = 1.0
            rot[b + i, b + i + 8] = 1.0
    c["rot_a"] = rot
    inv = (np.float32(500000.0) ** (-np.arange(0, 16, 2, dtype=np.float32) / np.float32(16))).astype(np.float32)
    ang = np.arange(T, dtype=np.float32)[:, None] * inv[None, :]
    cs, sn = np.cos(ang).astype(np.float32).T, np.sin(ang).astype(np.float32).T
    ct, st = np.ones((128, T), np.float32), np.zeros((128, T), np.float32)
    for b in (0, 64):
        ct[b:b + 8] = cs
        ct[b + 8:b + 16] = cs
        st[b:b + 8] = -sn
        st[b + 8:b + 16] = sn
    c["cs_a"] = np.concatenate([ct, st], 1)
    cap = np.full((128, 2, T), CAP, np.float32)
    for b in range(2):
        q = META + 128 * b + np.arange(128)
        cap[:, b][np.arange(T)[None, :] > q[:, None]] = -CAP
    c["cap"] = cap.reshape(128, 2 * T)
    rb = np.zeros((128, 96), np.float32)
    for i in range(16):
        rb[64 + i + 16, 64 + i] = 1.0
        rb[64 + i, 64 + i + 16] = 1.0
    c["rot_b"] = rb
    invb = (np.float32(1.0) / (np.float32(10000.0) ** (np.arange(0, 32, 2, dtype=np.float32) / np.float32(32)))).astype(np.float32)
    fr = np.zeros((128, 2), np.float32)
    fr[64:80, 0] = invb
    fr[80:96, 0] = invb
    fr[64:80, 1] = -1.0
    fr[80:96, 1] = 1.0
    c["freq"] = fr
    k = np.arange(256)[None, :] - 128 - np.arange(128)[:, None]
    c["causal"] = np.where(k > 0, np.float32(NEG), np.float32(0)).astype(np.float32)
    dist = 255 - np.arange(384)
    safe = np.maximum(np.maximum(dist, 0), 1).astype(np.float32)
    large = 16 + (np.log(safe / 16) / math.log(2048 / 16) * 16).astype(np.int64)
    large = np.minimum(large, 31)
    bucket = np.where(np.maximum(dist, 0) < 16, np.maximum(dist, 0), large)
    oh = np.zeros((33, 384), np.float32)
    oh[bucket, np.arange(384)] = 8.0
    times = (dist <= 128).astype(int) + (dist % 4 == 0) + (dist % 16 == 0)
    oh[32] = np.where((dist >= 0) & (times > 0), 8.0 * np.log(np.maximum(times, 1)), NEG)
    c["dist"] = oh
    return c


class Link:

    def __init__(self, eng, sem):
        self.eng, self.sem, self.n, self.i, self.per = eng, sem, 0, None, 0

    def value(self):
        return self.n if self.i is None else self.i * self.per + self.n

    def do(self, ins):
        ins.then_inc(self.sem, 1)
        self.n += 1

    def sync(self):
        self.eng.wait_ge(self.sem, self.value())

    def __call__(self, ins):
        self.do(ins)
        self.sync()

    @contextmanager
    def loop(self, times, per):
        first = self.n
        with self.eng.Fori(0, times) as i:
            self.i, self.per = i, per
            yield i
            assert self.n - first == per, f"steps {self.n - first}, not {per}"
        self.i = None
        self.n = first + per * times


def val(c, i, k):
    return c if i is None else i * k + c


def turns(link, n, per, steps, body, at_least=0):
    peel = n % per
    while peel < at_least:
        peel += per
    if peel:
        body(range(peel), None)
    if n - peel == per:
        body(range(peel, n), None)
    elif n > peel:
        with link.loop((n - peel) // per, steps) as i:
            body(range(peel, peel + per), i)



SPLITS = [("f0", 8), ("m0", 8), ("m1", 8), ("m2", 8), ("m3", 8), ("m4", 8), ("m5", 8), ("ro", 8),
          ("f1", 8), ("f2", 8), ("at", 8), ("f3", 8), ("b", 8), ("cq", 6), ("ckv", 2), ("ff", 8)]
X0, XM0 = {}, {}
_x = _m = 0
for _name, _n in SPLITS:
    X0[_name], XM0[_name] = _x, _m
    _x += _n
    _m += 0 if _name == "ro" else _n
NORMS = [("f0", 8), ("rk", 8), ("f1", 4), ("f2", 8), ("at", 8), ("f3", 4), ("b", 8), ("ff", 4)]
Q0, N0 = {}, {}
_q = 0
for _i, (_name, _n) in enumerate(NORMS):
    Q0[_name], N0[_name] = _q, _i
    _q += _n


def build(nc, t):
    ctx = ExitStack()
    with ctx:
        used = [0]

        class Region:

            def __init__(self, start):
                self.here = start

            def __call__(self, name, shape, dtype=F32):
                size = 4 * int(np.prod(shape[1:]))
                x = nc.alloc_sbuf_tensor_at(name, shape, dtype, offset=self.here)
                self.here += (size + 31) // 32 * 32
                used[0] = max(used[0], self.here)
                return x

        def sem(name):
            return ctx.enter_context(nc.semaphore(name))

        keep = Region((nc.sbuf_base + 63) // 32 * 32)
        keep_at = keep.here
        raw = [keep(f"raw{i}", [128, 2048]) for i in range(RAW)]
        whi = [keep(f"whi{i}", [128, 2048], F32R) for i in range(SPL)]
        wlo = [keep(f"wlo{i}", [128, 2048], F32R) for i in range(SPL)]
        h = keep("h", [128, KC, T])
        ident = keep("ident", [128, 128])
        ones = keep("ones", [128, 128])
        bo64 = keep("bo64", [128, 128])
        sel = keep("sel", [128, 88])
        vec = keep("vec", [128, NVEC])
        ss = keep("ss", [128, T])
        rstd = keep("rstd", [128, T])
        epsc = keep("epsc", [128, 2])

        arena = keep.here
        xr = Region(arena)
        xh, xl = [None, None], [None, None]
        xh[0] = xr("xh0", [128, KC, T], F32R)
        xl[0] = xr("xl0", [128, KC, T], F32R)
        after_x0 = xr.here
        xh[1] = xr("xh1", [128, KC, T], F32R)
        xl[1] = xr("xl1", [128, KC, T], F32R)
        after_x1 = xr.here

        ff = Region(after_x0)
        hid_h = ff("hid_h", [128, FC * T], F32R)
        hid_l = ff("hid_l", [128, FC * T], F32R)
        gate = ff("gate", [128, 2, T])
        upg = ff("upg", [128, 2, T])
        sig = ff("sig", [128, 2, T])
        hidf = ff("hidf", [128, 2, T])
        sq = ff("sq", [128, 2, 2, T])
        xg = ff("xg", [128, 2, 2, T])
        ff = Region(after_x0)
        hid2_h = ff("hid2_h", [128, 32 * SEQ], F32R)
        hid2_l = ff("hid2_l", [128, 32 * SEQ], F32R)
        act2 = ff("act2", [128, 2, 2, SEQ])
        hidf2 = ff("hidf2", [128, 2, 2, SEQ])
        outt = ff("outt", [128, KC, SEQ])

        rk = Region(after_x1)
        hn = rk("hn", [128, KC, T])
        xx = rk("xx", [128, KC, T])
        rk.here = after_x1 + 2 * 4 * KC * TP
        a_g = rk("a_g", [128, KC, T])
        head_end = rk.here
        lh_at = rk.here
        lh = rk("lh", [128, T])
        lh_h = rk("lh_h", [128, T], F32R)
        lh_l = rk("lh_l", [128, T], F32R)
        gh = rk("gh", [80, 2, T])
        gh_h = rk("gh_h", [80, 2, T], F32R)
        gh_l = rk("gh_l", [80, 2, T], F32R)
        wend = rk("wend", [128, KC, NCH])
        first = rk("first", [128, KC, NCH])
        R_ = rk("R_", [128, KC, TP])
        K_ = rk("K_", [128, KC, TP])
        V_ = rk("V_", [128, KC, TP])
        A_ = rk("A_", [128, KC, TP])
        B_ = rk("B_", [128, KC, TP])
        w_at = rk.here
        W_ = rk("W_", [128, KC, TP])
        masks = rk("masks", [128, 10, BLK])
        r2 = Region(w_at)
        xmf = r2("xmf", [128, KC, T])
        bonus = Region(w_at)("bonus", [128, KC, T])
        r2 = Region(after_x1)
        wst = r2("wst", [128, KC, TP])
        Wc = r2("Wc", [128, KC, TP])
        ktmp = Region(after_x0)("ktmp", [128, KC, TP])
        kden = Region(arena)("kden", [16, T])
        sc = Region(arena)
        U_ = sc("U_", [96, NB, 512])
        mrb = sc("mrb", [96, 8, TP])
        btok = sc("btok", [96, NB, 512])
        GV = sc("GV", [128, NCH, 256])
        L_ = QQ = [sc(f"L{e}", [96, TP]) for e in range(4)]
        LT = [sc(f"LT{e}", [96, TP]) for e in range(4)]
        xx_at = sc.here
        XX = [sc(f"XX{e}", [96, TP]) for e in range(4)]
        lm_at = sc.here
        LM = [sc(f"LM{e}", [96, TP]) for e in range(4)]
        XT = [sc(f"XT{e}", [96, TP]) for e in range(4)]
        lak = [sc(f"lak{e}", [96, TP]) for e in range(2)]
        in_raw = Region(keep_at + (U0["rk_o"] + 3) % RAW * 8192)
        mrk_at = in_raw.here
        mrk = [in_raw(f"mrk{e}", [96, TP]) for e in range(4)]
        lak += [in_raw(f"lak{e}", [96, TP]) for e in range(2, 4)]
        atok = [sc(f"atok{e}", [96, NB, 128]) for e in range(2)]
        ktok = [sc("ktok0", [96, NB, 128]), Region(rk.here)("ktok1", [96, NB, 128])]
        in_lh = Region(lh_at)
        vtok = [in_lh(f"vtok{e}", [96, NB, 128]) for e in range(2)]
        in_lm, in_mrk, in_xx = Region(lm_at), Region(mrk_at), Region(xx_at)
        p1 = [in_lm(f"p1{e}", [96, NB, 128]) for e in range(2)]
        bh = [in_mrk(f"bh{e}", [128, TP]) for e in range(2)]
        kh = [in_mrk(f"kh{e}", [128, TP]) for e in range(2)]
        S_ = [in_xx(f"S{e}", [128, 256]) for e in range(2)]
        St = in_xx("St", [128, 256])
        assert sc.here <= head_end, (sc.here, head_end)

        ds_ = Region(after_x1)
        rawq = ds_("rawq", [128, 18, T])
        vt = ds_("vt", [96, NB, 256])
        rot_a = ds_("rot_a", [128, 128])
        cs_a = ds_("cs_a", [128, 2, T])
        cap = ds_("cap", [128, 2, T])
        wit = ds_("wit", [128, 2, 8])
        rel = ds_("rel", [128, 2, T])
        score = ds_("score", [128, 2, T])
        taken = [ds_(f"taken{i}", [128, 2, T]) for i in range(2)]
        m8 = ds_("m8", [128, 8])
        rcol_a = ds_("rcol_a", [128, NB, 4])
        b2 = Region(after_x1)
        qka = b2("qka", [128, 8, SEQ])
        vat = b2("vat", [128, 2, 512])
        craw = b2("craw", [128, 8, SEQ])
        krope = b2("krope", [128, SEQ])
        cxf_at = b2.here
        qkb = b2("qkb", [96, 16, SEQ])
        vbt = b2("vbt", [128, 2, 512])
        bias = b2("bias", [128, 8, 256])
        causal = b2("causal", [128, 256])
        rot_b = b2("rot_b", [128, 96])
        cs_b = b2("cs_b", [128, 2, SEQ])
        rcol_c = b2("rcol_c", [128, 2, 4])
        rcol_b = b2("rcol_b", [128, 2, 4])
        posi = b2("posi", [128, SEQ], I32)
        posf = b2("posf", [128, SEQ])
        ang = b2("ang", [128, SEQ])
        red = b2("red", [128, SEQ])
        freq = b2("freq", [128, 2])
        distt = b2("distt", [33, 384])
        relb = b2("relb", [33, 8, 128])
        bt = b2("bt", [128, 2, SEQ])
        cvr = b2("cvr", [128, 2, SEQ])
        csq = Region(cxf_at + 4 * 8 * SEQ)("csq", [128, 8, SEQ])
        cxf = Region(cxf_at)("cxf", [128, 8, SEQ])
        attn_at = max(ds_.here, b2.here)
        an = Region(attn_at)
        biasw = Region(attn_at)("biasw", [128, 8, 384])
        lg = an("lg", [128, 2, T])
        pr = an("pr", [128, 3, T])
        prn = an("prn", [128, 3, T])
        pts = an("pts", [128, 2, 3, 128])
        amx = an("amx", [128, 64])
        nmx = an("nmx", [128, 64])
        asum = an("asum", [128, 64])
        ainv = an("ainv", [128, 64])

        sqp = [an(f"sqp{i}", [128, 2, T]) for i in range(2)]
        hinv = [an(f"hinv{i}", [32, T]) for i in range(2)]
        rtt = an("rtt", [128, 2, T])
        assert used[0] <= nc.sbuf_usable_end, (used[0], nc.sbuf_usable_end)

        PS = ctx.enter_context(nc.psum_tensor("PS", [128, 8, 512], F32))


        def by_head(tile, rows=16):
            return sel[:, 30 - 2 * tile:30 - 2 * tile + rows]

        def row(r, rows, m):
            return ident[0:rows, r:r + 1].broadcast_to([rows, m])

        s_raw = [sem(f"raw_arrived{i}") for i in range(RAW)]
        s_hi = sem("hi_split")
        s_lo = sem("lo_split")
        s_unit = sem("unit_used")
        s_free = sem("group_drained")
        s_xm = sem("x_made")
        s_xh = sem("x_high")
        s_x = sem("x_low")
        s_sq = sem("squared")
        s_ssa = sem("squares_added")
        s_nmm = sem("norm_summed")
        s_var = sem("mean_square")
        s_std = sem("root")
        s_gate = sem("gate_scaled")
        s_sig = sem("gate_sigmoid")
        s_hid = sem("hidden_made")
        s_hhi = sem("hidden_high")
        s_hlo = sem("hidden_low")
        s_cinv = sem("latent_inverse")
        s_rcm = sem("token_rms_in_rows")
        s_dve, s_act, s_pool = sem("dve_step"), sem("act_step"), sem("pool_step")
        s_h = [sem(f"h_arrived{i}") for i in range(2)]
        s_vec, s_const = sem("vectors_arrived"), sem("constants_arrived")
        s_rkc = sem("scan_masks_arrived")
        s_dsc = sem("dsa_tables_arrived")
        s_bc = sem("last_block_tables_arrived")

        s_lhd, s_lhh, s_lhl = sem("lora_drained"), sem("lora_high"), sem("lora_low")
        s_ghh, s_ghl = sem("gate_lora_high"), sem("gate_lora_low")
        s_part = sem("part_of_unit")
        s_wa, s_dec = sem("decay_and_a_drained"), sem("decay_sigmoid")
        s_cum, s_dk = sem("decays_added"), sem("decays_multiplied")
        s_kk, s_kksq, s_kkm, s_kkr = sem("kk_made"), sem("kk_squared"), sem("kk_summed"), sem("kk_root")
        s_rkr, s_bonm, s_bon = sem("bonus_products"), sem("bonus_summed"), sem("bonus_made")
        s_rks, s_wst = sem("r_and_k_scaled"), sem("chunk_starts_marked")
        s_kki, s_kkb, s_kkd = sem("kk_inverse"), sem("kk_spread"), sem("kk_divided")
        s_gni, s_gnb, s_gnd = sem("y_inverse"), sem("y_spread"), sem("y_divided")
        s_hinv, s_hb = sem("head_inverse"), sem("head_spread")
        s_bk, s_tr = sem("pair_ready"), sem("transposed")
        s_tka, s_tkd = sem("tokens_major_act"), sem("tokens_major_dve")
        s_gm, s_gr = sem("gram_product"), sem("gram_masked")
        s_lm, s_q, s_qc, s_xt = sem("level_mask"), sem("level_q"), sem("level_q_copied"), sem("level_update")
        s_xd, s_xi = sem("level_added"), sem("inverse_begun")
        s_p1, s_p1c, s_um, s_ue = sem("lak_v"), sem("lak_v_copied"), sem("u_product"), sem("u_copied")
        s_ztm, s_zt, s_yvm, s_yv = sem("z_product"), sem("z_copied"), sem("yv_product"), sem("yv_copied")
        s_gvm, s_gv = sem("gamma_product"), sem("gamma_copied")
        s_sam, s_sau, s_dsm, s_s = sem("sa_product"), sem("sa_made"), sem("state_product"), sem("state_made")
        s_ysm, s_yse, s_ym, s_yc = sem("ys_product"), sem("ys_added"), sem("intra_product"), sem("y_added")
        s_mum, s_yc2, s_ysq, s_vm = sem("y_mean"), sem("y_centred"), sem("y_squared"), sem("y_var_sum")
        s_bv, s_bvr = sem("y_var"), sem("y_root")
        s_hsq, s_hsum, s_hvar, s_hroot = sem("head_squared"), sem("head_summed"), sem("head_var"), sem("head_root")
        s_hsc, s_hrot, s_hout = sem("head_scaled"), sem("head_rotated"), sem("head_ready")
        s_wtm, s_wt = sem("wi_transposed"), sem("wi_ready")
        s_rlm, s_rl, s_ra = sem("index_product"), sem("index_relu"), sem("index_added")
        s_lgm, s_lg, s_ex, s_prn = sem("logits"), sem("logits_max"), sem("exponentials"), sem("probabilities")
        s_ptm, s_pte, s_om, s_oh, s_ol = (sem("p_transposed"), sem("p_copied"), sem("head_product"),
                                          sem("head_high"), sem("head_low"))
        s_csq, s_css, s_cnm, s_cv, s_cst = (sem("latent_squared"), sem("latent_squares_added"),
                                            sem("latent_summed"), sem("latent_var"), sem("latent_root"))
        s_ang, s_sin = sem("angles"), sem("sines")
        s_bwm, s_bw, s_bst, s_bld = (sem("bias_rows_product"), sem("bias_rows"), sem("bias_stored"),
                                     sem("bias_loaded"))
        s_hf2, s_hlo2 = sem("relu_squared"), sem("hidden2_low")
        s_out = sem("result_stored")

        tok = {"f0": T, "f1": T, "f2": T, "f3": SEQ}
        gain = {"f0": norm_col(0, 0), "f1": norm_col(0, 2), "f2": norm_col(1, 0), "f3": norm_col(1, 2)}

        def hv(n, a, b=None):
            b = a + 1 if b is None else b
            return h[:, a:b, T - n:T]

        def bank(G):
            return 2 * (G % 2)

        def mask(k):
            return masks[0:BLK, k, :].unsqueeze(1).broadcast_to([BLK, NB, BLK])

        def blocks(x):
            return x.rearrange("p (b t) -> p b t", b=NB)

        block = ctx.enter_context(nc.Block())

        @block.sync
        def _(sp):
            link = Link(sp, None)
            r_arrived, r_split = sp.alloc_register("arrived"), sp.alloc_register("split")
            for m in (0, 4):
                sp.dma_start(h[:, m:m + 4, :], t["h0"][:, m:m + 4, :]).then_inc(s_h[m // 4], 16)
                if m == 0:
                    sp.dma_start(vec[:, :], t["vec"]).then_inc(s_vec, 16)

            def load(name):
                src, w, u0 = t["w_" + name], UW[name], U0[name]

                def body(us, i):
                    for u in us:
                        U = u0 + u
                        arrived, split = val(16 * (U // RAW), i, 16), val(2 * (U - RAW + 1), i, 8)
                        s = src[u] if i is None else src[bass.ds(i * 4 + u, 1)].rearrange("o p w -> (o p) w")
                        if i is not None:
                            sp.reg_mov(r_arrived, arrived)
                            sp.reg_mov(r_split, split)
                            arrived, split = r_arrived, r_split
                        if name == "rk_o" and u == 3:
                            sp.wait_ge(s_yc, KC)
                        if U >= RAW:
                            sp.wait_ge(s_raw[U % RAW], arrived)
                            sp.wait_ge(s_lo, split)
                        sp.dma_start(raw[U % RAW][:, 0:w], s).then_inc(s_raw[U % RAW], 16)
                turns(link, UN[name], 4, 0, body, RAW - u0 if u0 < RAW else 0)

            for name, *_ in STAGES:
                load(name)
            sp.wait_ge(s_free, G0["b_ff2"] + 8)
            sp.dma_start(t["out"], outt[:, :, :]).then_inc(s_out, 16)
            sp.wait_ge(s_out, 16)

        @block.gpsimd
        def _(pool):
            link = Link(pool, None)

            def scan_part():
                step = Link(pool, s_pool)
                tt = nc.gpsimd.tensor_tensor
                pool.wait_ge(s_lo, 2 * (U0["g2"] + 1))
                pool.wait_ge(s_rkr, KC)
                tt(K_[:, :, :], K_[:, :, :], W_[:, :, :], ALU.mult).then_inc(s_rks, 1)
                tt(R_[:, :, :], R_[:, :, :], Wc[:, :, :], ALU.mult).then_inc(s_rks, 1)
                pool.wait_ge(s_rks, 2)
                pool.wait_ge(s_rkc, 16)
                pool.wait_ge(s_bon, KC)
                for q in range(4):
                    for pp in range(2):
                        if q and pp == 0:
                            pool.wait_ge(s_yvm, 2 * q)
                        for n, (dst, src) in enumerate(((bh[pp], B_), (kh[pp], K_))):
                            ins = tt(dst[:, :].rearrange("p (n t) -> p n t", t=CH),
                                     src[:, 2 * q + pp, :].rearrange("p (n t) -> p n t", t=CH),
                                     wend[:, 2 * q + pp, :].unsqueeze(2).broadcast_to([128, NCH, CH]), ALU.mult)
                            ins.then_inc(s_bk, 1)
                    for e in range(4):
                        pool.wait_ge(s_gr, 20 * q + 5 * e + 2)
                        step(tt(blocks(XX[e][:, :]), blocks(L_[e][:, :]), mask(3), ALU.mult))
                        step.do(tt(blocks(XX[e][:, :]), blocks(XX[e][:, :]), mask(9), ALU.add))
                        tt(blocks(LM[e][:, :]), blocks(LT[e][:, :]), mask(5), ALU.mult).then_inc(s_lm, 1)
                    for lv in range(1, 4):
                        for e in range(4):
                            pool.wait_ge(s_q, 16 * q + 4 * (lv - 1) + e + 1)
                            tt(blocks(LM[e][:, :]), blocks(LT[e][:, :]), mask(5 + lv), ALU.mult).then_inc(s_lm, 1)

            for name, n, _m, w in STAGES:
                u0 = U0[name]

                def body(us, i):
                    for u in us:
                        U = u0 + u
                        for q, part in enumerate(halves(w)):
                            pool.wait_ge(s_hi, val(2 * U + q + 1, i, 8))
                            if U >= SPL:
                                pool.wait_ge(s_unit, val(2 * (U - SPL) + q + 1, i, 8))
                            nc.gpsimd.tensor_tensor(wlo[U % SPL][:, part], raw[U % RAW][:, part],
                                                    whi[U % SPL][:, part].bitcast(F32), ALU.subtract
                                                    ).then_inc(s_lo, 1)
                turns(link, n, 4, 0, body)
                if name == "wa2":
                    pool.wait_ge(s_x, X0["m5"] + 8)
                    nc.gpsimd.memset(wst[:, :, :], 1.0).then_inc(s_wst, 1)
                    pool.wait_ge(s_wst, 1)
                    nc.gpsimd.memset(wst[:, :, 0:TP:CH], 0.0).then_inc(s_wst, 1)
                if name == "g2":
                    scan_part()
        HB = {f"f{i}": FC * i for i in range(4)}

        def dsa_jobs():
            out = []
            for hd in range(16):
                e, g = hd % 2, hd // 4
                for b in range(2):
                    nk = META + 128 * (b + 1)
                    rows = slice(64 * e, 64 * e + 64)
                    vb = [(vt[0:min(BLK, nk - BLK * j), j, g * 64:g * 64 + 64], BLK * j, min(BLK, nk - BLK * j))
                          for j in range(-(-nk // BLK))]
                    out.append(dict(q=rawq[rows, hd // 2, META + 128 * b:META + 128 * b + 128],
                                    k=rawq[rows, 8 + g, 0:nk], nk=nk, add=taken[0][:, b, 0:nk],
                                    scale=0.125, v=vb, head=hd, b=b))
            return out

        def last_jobs():
            out = []
            for hd in range(16):
                for b in range(2):
                    nk = 128 * (b + 1)
                    if hd < 8:
                        e = hd % 2
                        rows = slice(64 * e, 64 * e + 64)
                        q, k = qka[rows, hd // 2, 128 * b:128 * b + 128], qka[rows, 4 + hd // 2, 0:nk]
                        add, scale, val_ = bias[:, hd, 256 - nk:256], 0.125, vat
                    else:
                        q, k = qkb[0:96, hd - 8, 128 * b:128 * b + 128], qkb[0:96, hd, 0:nk]
                        add, scale, val_ = causal[:, 256 - nk:256], float(96 ** -0.5), vbt
                    vb = [(val_[:, j, (hd % 8) * 64:(hd % 8) * 64 + 64], 128 * j, 128) for j in range(b + 1)]
                    out.append(dict(q=q, k=k, nk=nk, add=add, scale=scale, v=vb, head=hd, b=b))
            return out

        JOBS = {"at": (dsa_jobs(), 0), "b": (last_jobs(), 32)}

        def head_tiles_at():
            out = []
            for j in (12, 14, 16, 0, 2, 4, 6, 8, 10):
                gain_ = VEC["q_g"] if j < 8 else VEC["k_g"]
                if j == 16:
                    out.append(dict(x=rawq[:, 16:17, :], rows=128, m=1, n=T, norm=False, rot=rot_a[:, :],
                                    cos=cs_a[:, 0, :], sin=cs_a[:, 1, :]))
                    continue
                out.append(dict(x=rawq[:, j:j + 2, :], rows=128, m=2, n=T, norm=j < 12, one=bo64[:, :],
                                inv=1 / 64, g=gain_, rot=rot_a[:, :], cos=cs_a[:, 0, :], sin=cs_a[:, 1, :]))
            return out

        def head_tiles_b():
            out = []
            for j in range(0, 8, 2):
                out.append(dict(x=qka[:, j:j + 2, :], rows=128, m=2, n=SEQ, norm=True, one=bo64[:, :],
                                inv=1 / 64, g=VEC["qa_g"] if j < 4 else VEC["ka_g"], rot=None))
            for j in range(0, 16, 2):
                out.append(dict(x=qkb[:, j:j + 2, :], rows=96, m=2, n=SEQ, norm=True,
                                one=ones[0:96, 0:96], inv=1 / 96, g=VEC["qb_g"] if j < 8 else VEC["kb_g"],
                                rot=rot_b[0:96, :], cos=cs_b[0:96, 0, :], sin=cs_b[0:96, 1, :]))
            return out

        TILES = {"at": head_tiles_at(), "b": head_tiles_b()}
        NT0 = {"at": 0, "b": sum(x["norm"] for x in TILES["at"])}
        RT0 = {"at": 0, "b": len(TILES["at"])}

        def counts(which, j):
            ts = TILES[which][:j + 1]
            return (NT0[which] + sum(x["norm"] for x in ts),
                    RT0[which] + sum(x["rot"] is not None for x in ts))

        GROUPS = [("at", 3, 9, 24, 0), ("b", 0, 4, 16, 1), ("b", 4, 12, 16, 2)]

        def groups(which):
            return [g[1:] for g in GROUPS if g[0] == which]

        def head_sum(x, j, q, g):
            a, _b, rows, _n = g
            t_ = 2 * (j - a) + q
            return by_head(t_, rows) if x["rows"] == 128 else sel[0:96, 71 - t_:71 - t_ + rows]

        @block.tensor
        def _(pe):
            link = Link(pe, None)
            mm = nc.tensor.matmul

            def products(out, w, x, start, stop, tokens=False):
                for n, (a, b) in enumerate(((w[0], x[0]), (w[0], x[1]), (w[1], x[0]))):
                    last = mm(out, b, a, start=start and n == 0, stop=stop and n == 2) if tokens else \
                        mm(out, a, b, start=start and n == 0, stop=stop and n == 2)
                return last

            def weights(U, rows, cols):
                return whi[U % SPL][rows, cols], wlo[U % SPL][rows, cols]

            ALLR = slice(0, 128)

            def norm_sum(name, n):
                pe.wait_ge(s_ssa, 8 * (N0[name] + 1))
                mm(PS[:, 6, 0:n], ones[:, :], ss[:, 0:n], start=True, stop=True).then_inc(s_nmm, 1)

            def project(name, n, b, x, norm=None, straight=0):
                def body(us, i):
                    for u in us:
                        U, G = U0[name] + u, G0[name] + u
                        for mi in range(2):
                            pe.wait_ge(s_lo, val(2 * U + mi + 1, i, 8))
                            if G >= 2 and mi == 0:
                                pe.wait_ge(s_free, val(G - 1, i, 4))
                            for k in range(KC):
                                if x and u == 0 and mi == 0:
                                    pe.wait_ge(s_x, X0[x] + k + 1)
                                c = mi * 1024 + k * 128
                                last = products(PS[:, bank(G) + mi, 0:n], weights(U, ALLR, slice(c, c + 128)),
                                                (xh[b][:, k, 0:n], xl[b][:, k, 0:n]), k == 0, k == KC - 1)
                            last.then_inc(s_unit, 1)
                            if u == 0 and mi == 0 and norm:
                                norm_sum(norm, n)
                if straight:
                    body(range(straight), None)
                    with link.loop((UN[name] - straight) // 4, 0) as i:
                        body(range(straight, straight + 4), i)
                else:
                    turns(link, UN[name], 4, 0, body)

            def project_down(name, n, hh, hl, stride, nk, ready):
                half = nk // 2

                def body(ms, i):
                    for m in ms:
                        G = G0[name] + m
                        for part in range(2):
                            U = U0[name] + 2 * m + part
                            if part == 0:
                                pe.wait_ge(s_free, val(G - 1, i, 2))
                            for k in range(half):
                                kk = part * half + k
                                if k in (0, 8):
                                    pe.wait_ge(s_lo, val(2 * U + k // 8 + 1, i, 8))
                                if m == 0:
                                    ready(kk)
                                last = products(PS[:, bank(G), 0:n], weights(U, ALLR, slice(k * 128, k * 128 + 128)),
                                                (hh[:, kk * stride:kk * stride + n], hl[:, kk * stride:kk * stride + n]),
                                                kk == 0, kk == nk - 1)
                                if k in (7, half - 1):
                                    last.then_inc(s_unit, 1)
                turns(link, 8, 2, 0, body, 2)

            def swiglu(f):
                project(f + "_in", tok[f], 0, f, norm=f)
                project_down(f + "_dn", tok[f], hid_h, hid_l, T, FC,
                             lambda kk: pe.wait_ge(s_hlo, HB[f] + kk + 1))

            def head_sums(which):
                tiles = TILES[which]
                for g in groups(which):
                    for j in range(g[0], g[1]):
                        x = tiles[j]
                        c, _r = counts(which, j)
                        pe.wait_ge(s_hsq, c)
                        for q in range(2):
                            last = mm(PS[0:g[2], 6 + g[3] % 2, 0:x["n"]], head_sum(x, j, q, g),
                                      sqp[c % 2][0:x["rows"], q, 0:x["n"]], start=j == g[0] and q == 0,
                                      stop=j == g[1] - 1 and q == 1)
                        last.then_inc(s_hsum, 1)
            def head_norms(which, j0, j1):
                tiles = TILES[which]
                for j in range(j0, j1 + 2):
                    if j < j1 and tiles[j]["norm"]:
                        x = tiles[j]
                        g = [g for g in groups(which) if g[0] <= j < g[1]][0]
                        c, _r = counts(which, j)
                        if j == g[0]:
                            pe.wait_ge(s_hinv, g[3] + 1)
                        if c - NT0[which] > 2:
                            pe.wait_ge(s_hsc, c - 2)
                        for q in range(2):
                            o, t_, inv = 2 * (c % 2) + q, 2 * (j - g[0]) + q, hinv[g[3] % 2][0:g[2], 0:x["n"]]
                            if x["rows"] == 96:
                                last = mm(PS[0:96, o, 0:x["n"]], row(t_, g[2], 96), inv, start=True, stop=True)
                            for e in range(2 if x["rows"] == 128 else 0):
                                last = mm(PS[64 * e:64 * e + 64, o, 0:x["n"]], row(2 * t_ + e, g[2], 64), inv,
                                          start=True, stop=True)
                        last.then_inc(s_hb, 1)
                    if j - 2 >= j0 and tiles[j - 2]["rot"] is not None:
                        x = tiles[j - 2]
                        r, n = slice(0, x["rows"]), x["n"]
                        c, cr = counts(which, j - 2)
                        if x["norm"]:
                            pe.wait_ge(s_hsc, c)
                        if cr - RT0[which] > 2:
                            pe.wait_ge(s_hout, cr - 2)
                        for q in range(x["m"]):
                            last = mm(PS[r, 4 + 2 * (cr % 2) + q, 0:n], x["rot"], x["x"][r, q, :],
                                      start=True, stop=True)
                        last.then_inc(s_hrot, 1)

            def attention(which):
                jobs, j0 = JOBS[which]
                for j in range(len(jobs) + 4):
                    if 0 <= j - 3 < len(jobs):
                        x, c = jobs[j - 3], j0 + j - 3
                        pe.wait_ge(s_prn, c + 1)
                        if j - 3 >= 2:
                            pe.wait_ge(s_pte, c - 1)
                        for n, (_v, k0, kn) in enumerate(x["v"]):
                            last = nc.tensor.transpose(PS[0:kn, 2 + c % 2, n * 128:n * 128 + 128],
                                                       prn[:, c % 3, k0:k0 + kn], ident[:, :])
                        last.then_inc(s_ptm, 1)
                    if j < len(jobs):
                        x, c = jobs[j], j0 + j
                        if j >= 2:
                            pe.wait_ge(s_lg, c - 1)
                        mm(PS[:, j % 2, 0:x["nk"]], x["q"], x["k"], start=True, stop=True).then_inc(s_lgm, 1)
                    if 0 <= j - 4 < len(jobs):
                        x, c = jobs[j - 4], j0 + j - 4
                        pe.wait_ge(s_pte, c + 1)
                        if j - 4 >= 2:
                            pe.wait_ge(s_ol, c - 1)
                        r = 64 * (x["head"] % 2)
                        for n, (v, k0, kn) in enumerate(x["v"]):
                            last = mm(PS[r:r + 64, 4 + c % 2, 0:128], v, pts[0:kn, c % 2, n, :],
                                      start=n == 0, stop=n == len(x["v"]) - 1)
                        last.then_inc(s_om, 1)

            pe.wait_ge(s_const, 64)
            swiglu("f0")
            norm_sum("rk", T)
            project("rk_r", T, 0, "m0")
            project("rk_k", T, 1, "m1")
            project("rk_v", T, 0, "m2")
            U, G = U0["lora_wa"], G0["lora_wa"]
            pe.wait_ge(s_lo, 2 * U + 2)
            pe.wait_ge(s_free, G - 1)
            for mi in range(2):
                for k in range(KC):
                    pe.wait_ge(s_x, X0[f"m{3 + mi}"] + k + 1)
                    last = products(PS[:, bank(G) + mi, 0:T], weights(U, ALLR, slice(k * 128, k * 128 + 128)),
                                    (xh[1 - mi][:, k, :], xl[1 - mi][:, k, :]), k == 0, k == KC - 1)
            last.then_inc(s_unit, 2)
            U, G = U0["lora_g"], G0["lora_g"]
            pe.wait_ge(s_lo, 2 * U + 2)
            pe.wait_ge(s_free, G - 1)
            for mi in range(2):
                for k in range(KC):
                    pe.wait_ge(s_x, X0["m5"] + k + 1)
                    c = k * 160 + mi * 80
                    last = products(PS[0:80, bank(G) + mi, 0:T], weights(U, ALLR, slice(c, c + 80)),
                                    (xh[1][:, k, :], xl[1][:, k, :]), k == 0, k == KC - 1)
            last.then_inc(s_unit, 2)
            U = U0["wa2"]
            pe.wait_ge(s_lo, 2 * U + 2)
            pe.wait_ge(s_lhl, 1)
            for m in range(KC):
                G = G0["wa2"] + m
                pe.wait_ge(s_free, G - 1)
                for mi in range(2):
                    r = slice(64 * mi, 64 * mi + 64)
                    last = products(PS[:, bank(G) + mi, 0:T], weights(U, r, slice(m * 128, m * 128 + 128)),
                                    (lh_h[r, :], lh_l[r, :]), True, True)
                last.then_inc(*((s_part, 1) if m < KC - 1 else (s_unit, 2)))
            pe.wait_ge(s_kksq, 1)
            for c in range(KC):
                last = mm(PS[0:16, 4, 0:T], by_head(c), ktmp[:, c, 0:T], start=c == 0, stop=c == KC - 1)
            last.then_inc(s_kkm, 1)
            pe.wait_ge(s_kki, 1)
            pe.wait_ge(s_free, G0["wa2"] + KC)
            for m in range(4):
                for n in range(2):
                    for e in range(2):
                        last = mm(PS[64 * e:64 * e + 64, (5 + 2 * m + n) % 8, 0:T], row(4 * m + 2 * n + e, 16, 64),
                                  kden[:, :], start=True, stop=True)
                last.then_inc(s_kkb, 1)
            pe.wait_ge(s_rkr, KC)
            pe.wait_ge(s_kkd, 4)
            for c in range(KC):
                last = mm(PS[:, c, 0:T], bo64[:, :], ktmp[:, c, 0:T], start=True, stop=True)
            last.then_inc(s_bonm, 1)

            def bl(b):
                return slice(b * BLK, b * BLK + BLK)

            def tk(e):
                return slice(64 * e, 64 * e + 64)

            def per_block(out, left, right):
                for e in range(2):
                    for b in range(NB):
                        last = mm(out(e, b), left(e, b), right(e, b), start=True, stop=True)
                return last

            for half in range(2):
                for q in (2 * half, 2 * half + 1):
                    c0 = 2 * q
                    if q:
                        for s in (s_zt, s_gv, s_yv, s_ue):
                            pe.wait_ge(s, c0)
                        if q == 2:
                            pe.wait_ge(s_yc, 4)
                    for pp in range(2):
                        c = c0 + pp
                        pe.wait_ge(s_bk, 2 * c + 2)
                        for n, src in enumerate((A_[:, c, :], bh[pp][:, :], kh[pp][:, :], V_[:, c, :])):
                            for b in range(NB):
                                last = nc.tensor.transpose(PS[0:BLK, 4 * pp + n, b * 128:b * 128 + 128],
                                                           src[:, bl(b)], ident[:, :])
                            last.then_inc(s_tr, 1)
                    for n in range(20):
                        c, e, ty = c0 + n // 10, n // 5 % 2, n % 5
                        if n in (0, 4):
                            pe.wait_ge(s_tka, 2 * (c0 + n // 4) + 2)
                            pe.wait_ge(s_tkd, 2 * (c0 + n // 4) + 2)
                        if n >= 8:
                            pe.wait_ge(s_gr, 20 * q + n - 7)
                        left = (B_, A_, K_, B_, K_)[ty]
                        right = (A_, B_, A_, R_, R_)[ty]
                        for b in range(NB):
                            last = mm(PS[0:BLK, n % 8, bl(b)], left[tk(e), c, bl(b)], right[tk(e), c, bl(b)],
                                      start=True, stop=True)
                        last.then_inc(s_gm, 1)
                    pe.wait_ge(s_gr, 20 * q + 20)
                    pe.wait_ge(s_xi, 4 * q + 4)
                    for lv in range(4):
                        for e in range(4):
                            pe.wait_ge(s_lm, 16 * q + 4 * lv + e + 1)
                            if lv:
                                pe.wait_ge(s_xd, 16 * q + 4 * (lv - 1) + e + 1)
                            for b in range(NB):
                                last = mm(PS[0:BLK, e, bl(b)], LM[e][:, bl(b)], XX[e][:, bl(b)], start=True, stop=True)
                            last.then_inc(s_q, 1)
                        for e in range(4):
                            pe.wait_ge(s_qc, 16 * q + 4 * lv + e + 1)
                            if lv < 3:
                                for b in range(NB):
                                    mm(PS[0:BLK, 4 + e, bl(b)], XT[e][:, bl(b)], QQ[e][:, bl(b)], start=True, stop=True)
                            for b in range(NB):
                                last = mm(PS[0:BLK, e, bl(b)], QQ[e][:, bl(b)], XT[e][:, bl(b)], start=True, stop=True)
                            last.then_inc(s_xt, 1)
                    pe.wait_ge(s_xd, 16 * q + 16)
                    for pp in range(2):
                        per_block(lambda e, b: PS[0:BLK, pp, b * 128 + 64 * e:b * 128 + 64 * e + 64],
                                  lambda e, b: lak[2 * pp + e][:, bl(b)], lambda e, b: vtok[pp][:, b, tk(e)]).then_inc(s_p1, 1)
                    for pp in range(2):
                        per_block(lambda e, b: PS[tk(e), 2 + pp, bl(b)],
                                  lambda e, b: atok[pp][:, b, tk(e)], lambda e, b: XT[2 * pp + e][:, bl(b)]).then_inc(s_ztm, 1)
                    for pp in range(2):
                        per_block(lambda e, b: PS[tk(e), 4 + pp, bl(b)],
                                  lambda e, b: vtok[pp][:, b, tk(e)], lambda e, b: mrk[2 * pp + e][:, bl(b)]).then_inc(s_yvm, 1)
                    for pp in range(2):
                        pe.wait_ge(s_p1c, c0 + pp + 1)
                        per_block(lambda e, b: PS[0:BLK, 6 + pp, b * 128 + 64 * e:b * 128 + 64 * e + 64],
                                  lambda e, b: XT[2 * pp + e][:, bl(b)], lambda e, b: p1[pp][:, b, tk(e)]).then_inc(s_um, 1)
                    for pp in range(2):
                        pe.wait_ge(s_zt, c0 + pp + 1)
                        if pp:
                            pe.wait_ge(s_yv, c0 + 2)
                        for ch in range(NCH):
                            b, r = ch // 3, slice(CH * (ch % 3), CH * (ch % 3) + CH)
                            for e in range(2):
                                last = mm(PS[tk(e), 3 * pp + ch % 3, b * 64:b * 64 + 64], ktok[pp][r, b, tk(e)],
                                          vtok[pp][r, b, tk(e)], start=True, stop=True)
                        last.then_inc(s_gvm, 1)

                heads = [(p, e) for p in range(4) for e in range(2)]
                pe.wait_ge(s_ue, 4 * half + 4)
                pe.wait_ge(s_zt, 4 * half + 4)
                pe.wait_ge(s_gv, 4 * half + 4)
                for ch in range(NCH):
                    b, r0 = ch // 3, CH * (ch % 3)
                    r = slice(r0, r0 + CH)
                    if ch:
                        for m in range(2):
                            pe.wait_ge(s_s, 16 * half + 2 * ch - 1 + m)
                            for p, e in heads[4 * m:4 * m + 4]:
                                last = mm(PS[r, 3 * (1 - m) + e, (p % 2) * 64:(p % 2) * 64 + 64],
                                          A_[64 * e:64 * e + 64, 4 * half + p, ch * CH:ch * CH + CH],
                                          S_[ch % 2][64 * e:64 * e + 64, p * 64:p * 64 + 64], start=True, stop=True)
                            last.then_inc(s_sam, 1)
                    if ch:
                        if ch > 2:
                            pe.wait_ge(s_yse, 8 * half + ch - 2)
                        for p, e in heads:
                            last = mm(PS[64 * e:64 * e + 64, 6 + ch % 2, p * CH:p * CH + CH],
                                      S_[ch % 2][64 * e:64 * e + 64, p * 64:p * 64 + 64],
                                      R_[64 * e:64 * e + 64, 4 * half + p, ch * CH:ch * CH + CH],
                                      start=True, stop=True)
                        last.then_inc(s_ysm, 1)
                    if ch < NCH - 1:
                        for m in range(2):
                            if ch:
                                pe.wait_ge(s_sau, 16 * half + 2 * ch - 1 + m)
                            for p, e in heads[4 * m:4 * m + 4]:
                                last = mm(PS[64 * e:64 * e + 64, (5, 2)[m], (p % 2) * 64:(p % 2) * 64 + 64],
                                          btok[r, b, p * 128 + 64 * e:p * 128 + 64 * e + 64],
                                          U_[r, b, (2 * p + e) * 64:(2 * p + e) * 64 + 64], start=True, stop=True)
                            last.then_inc(s_dsm, 1)
                pe.wait_ge(s_sau, 16 * half + 16)
                for p in range(4):
                    if p >= 2:
                        pe.wait_ge(s_yc, 4 * half + p - 1)
                    for e in range(2):
                        for b in range(NB):
                            last = mm(PS[64 * e:64 * e + 64, p % 2, b * BLK:b * BLK + BLK],
                                      U_[:, b, (2 * p + e) * 64:(2 * p + e) * 64 + 64],
                                      mrb[:, 2 * p + e, b * BLK:b * BLK + BLK], start=True, stop=True)
                    last.then_inc(s_ym, 1)

            for c in range(KC):
                if c == 0:
                    pe.wait_ge(s_yc, KC)
                if c >= 2:
                    pe.wait_ge(s_yc2, c - 1)
                mm(PS[:, 4 + c % 2, 0:T], bo64[:, :], K_[:, c, 0:T], start=True, stop=True).then_inc(s_mum, 1)
            for c in range(KC):
                pe.wait_ge(s_ysq, c + 1)
                last = mm(PS[0:16, 6, 0:T], by_head(c), A_[:, c, 0:T], start=c == 0, stop=c == KC - 1)
            last.then_inc(s_vm, 1)
            pe.wait_ge(s_gni, 1)
            for m in range(4):
                for n in range(2):
                    for e in range(2):
                        last = mm(PS[64 * e:64 * e + 64, 2 * m + n, 0:T], row(4 * m + 2 * n + e, 16, 64),
                                  kden[:, :], start=True, stop=True)
                last.then_inc(s_gnb, 1)
            pe.wait_ge(s_gnd, 2)
            U = U0["g2"]
            pe.wait_ge(s_lo, 2 * U + 2)
            pe.wait_ge(s_ghl, 1)
            for g in range(4):
                G = G0["g2"] + g
                pe.wait_ge(s_free, G - 1)
                for mi in range(2):
                    for k in range(2):
                        c = k * D + (2 * g + mi) * 128
                        last = products(PS[:, bank(G) + mi, 0:T], weights(U, slice(0, 80), slice(c, c + 128)),
                                        (gh_h[:, k, :], gh_l[:, k, :]), k == 0, k == 1)
                last.then_inc(*((s_part, 1) if g < 3 else (s_unit, 2)))
            project("rk_o", T, 1, "ro")
            swiglu("f1")

            swiglu("f2")
            project("at_q", T, 0, "at", norm="at")
            project("at_k", T, 0, "at")
            project("at_qi", T, 0, "at")
            project("at_tail", T, 0, "at")
            pe.wait_ge(s_free, G0["at_q"] + 1)
            for j in range(NB):
                kn = min(BLK, T - BLK * j)
                last = mm(PS[0:kn, 6, 4 * j:4 * j + 4], rstd[:, j * BLK:j * BLK + kn], ident[:, 0:4],
                          start=True, stop=True)
            last.then_inc(s_rcm, 1)
            U, G = U0["at_v"], G0["at_v"]
            pe.wait_ge(s_lo, 2 * U + 2)
            pe.wait_ge(s_free, G - 1)
            for j in range(NB):
                kn = min(BLK, T - BLK * j)
                for k in range(KC):
                    last = products(PS[0:kn, bank(G) + j // 2, (j % 2) * 256:(j % 2) * 256 + 256],
                                    weights(U, ALLR, slice(k * 256, k * 256 + 256)),
                                    (xh[0][:, k, j * BLK:j * BLK + kn], xl[0][:, k, j * BLK:j * BLK + kn]),
                                    k == 0, k == KC - 1, tokens=True)
            last.then_inc(s_unit, 2)
            pe.wait_ge(s_free, G + 1)
            pe.wait_ge(s_dsc, 48)
            head_sums("at")
            pe.wait_ge(s_hvar, 1)
            head_norms("at", 0, 3)
            pe.wait_ge(s_hout, 3)
            for b in range(2):
                last = nc.tensor.transpose(PS[:, 0, b * 8:b * 8 + 8], rawq[0:8, 17, META + 128 * b:META + 128 * b + 128],
                                           ident[0:8, 0:8])
            last.then_inc(s_wtm, 1)
            pe.wait_ge(s_wt, 1)
            for b in range(2):
                nk = META + 128 * (b + 1)
                for hd in range(8):
                    n = b * 8 + hd
                    r = slice(64 * (hd % 2), 64 * (hd % 2) + 64)
                    if n >= 2:
                        pe.wait_ge(s_rl, n - 1)
                    mm(PS[:, 2 + n % 2, 0:nk], rawq[r, 12 + hd // 2, META + 128 * b:META + 128 * b + 128],
                       rawq[r, 16, 0:nk], start=True, stop=True).then_inc(s_rlm, 1)
            pe.wait_ge(s_rl, 16)
            head_norms("at", 3, 9)
            pe.wait_ge(s_hout, RT0["b"])
            attention("at")
            pe.wait_ge(s_ol, 32)
            project("at_o", SEQ, 1, None)
            swiglu("f3")

            project("b_qa", SEQ, 0, "b", norm="b")
            project("b_ka", SEQ, 0, "b")
            pe.wait_ge(s_free, G0["b_qa"] + 1)
            for j in range(2):
                last = mm(PS[:, 6, 4 * j:4 * j + 4], rstd[:, j * 128:j * 128 + 128], ident[:, 0:4],
                          start=True, stop=True)
            last.then_inc(s_rcm, 1)
            pe.wait_ge(s_bc, 96)
            for hd in range(8):
                if hd >= 2:
                    pe.wait_ge(s_bw, hd - 1)
                mm(PS[:, 4 + hd % 2, 0:384], relb[:, hd, :], distt[:, :], start=True, stop=True).then_inc(s_bwm, 1)
            for u in range(2):
                U, G = U0["b_va"] + u, G0["b_va"] + u
                pe.wait_ge(s_lo, 2 * U + 2)
                pe.wait_ge(s_free, G - 1)
                for j in range(2):
                    for k in range(KC):
                        last = products(PS[:, bank(G) + j, 0:256], weights(U, ALLR, slice(k * 256, k * 256 + 256)),
                                        (xh[0][:, k, j * 128:j * 128 + 128], xl[0][:, k, j * 128:j * 128 + 128]),
                                        k == 0, k == KC - 1, tokens=True)
                last.then_inc(s_unit, 2)
            project("b_cq", SEQ, 0, "b")
            project("b_ckv", SEQ, 0, "b")
            U, G = U0["b_tail"], G0["b_tail"]
            pe.wait_ge(s_lo, 2 * U + 2)
            pe.wait_ge(s_free, G - 1)
            for k in range(KC):
                last = products(PS[:, bank(G), 0:SEQ], weights(U, ALLR, slice(k * 128, k * 128 + 128)),
                                (xh[0][:, k, 0:SEQ], xl[0][:, k, 0:SEQ]), k == 0, k == KC - 1)
            last.then_inc(s_unit, 2)
            def latent_sum(n):
                pe.wait_ge(s_css, (6, 8)[n])
                mm(PS[:, 6 + n, 0:SEQ], ones[:, :], bt[:, n, :], start=True, stop=True).then_inc(s_cnm, 1)
            latent_sum(0)
            for u in range(4):
                U, G = U0["b_uq"] + u, G0["b_uq"] + u
                pe.wait_ge(s_lo, 2 * U + 2)
                pe.wait_ge(s_free, G - 1)
                for mi in range(2):
                    for k in range(6):
                        if u == 0:
                            pe.wait_ge(s_x, X0["cq"] + k + 1)
                        c = k * 192 + mi * 96
                        last = products(PS[0:96, bank(G) + mi, 0:SEQ], weights(U, ALLR, slice(c, c + 96)),
                                        (xh[1][:, k, 0:SEQ], xl[1][:, k, 0:SEQ]), k == 0, k == 5)
                last.then_inc(s_unit, 2)
                if u == 0:
                    latent_sum(1)
            pe.wait_ge(s_cinv, 2)
            for j in range(2):
                last = mm(PS[:, 6, 4 * j:4 * j + 4], cvr[:, 1, j * 128:j * 128 + 128], ident[:, 0:4],
                          start=True, stop=True)
            last.then_inc(s_rcm, 1)
            U = U0["b_ukv"]
            pe.wait_ge(s_lo, 2 * U + 2)
            pe.wait_ge(s_x, X0["ckv"] + 2)
            for g in range(3):
                G = G0["b_ukv"] + g
                pe.wait_ge(s_free, G - 1)
                for mi in range(2):
                    for k in range(2):
                        if g < 2:
                            c = k * 1024 + (2 * g + mi) * 128
                            last = products(PS[:, bank(G) + mi, 0:SEQ], weights(U, ALLR, slice(c, c + 128)),
                                            (xh[1][:, 6 + k, 0:SEQ], xl[1][:, 6 + k, 0:SEQ]), k == 0, k == 1)
                        else:
                            c = k * 1024 + 512
                            tb = slice(mi * 128, mi * 128 + 128)
                            last = products(PS[:, bank(G) + mi, 0:512], weights(U, ALLR, slice(c, c + 512)),
                                            (xh[1][:, 6 + k, tb], xl[1][:, 6 + k, tb]), k == 0, k == 1, tokens=True)
                last.then_inc(*((s_part, 1) if g < 2 else (s_unit, 2)))
            pe.wait_ge(s_free, G0["b_ukv"] + 3)
            head_sums("b")
            head_norms("b", 0, 12)
            pe.wait_ge(s_hout, RT0["b"] + 8)
            pe.wait_ge(s_hsc, NT0["b"] + 12)
            attention("b")
            pe.wait_ge(s_ol, 64)
            project("b_o", SEQ, 1, None)
            project("b_ff1", SEQ, 0, "ff", norm="ff", straight=4)
            project_down("b_ff2", SEQ, hid2_h, hid2_l, SEQ, 32,
                         lambda kk: pe.wait_ge(s_hlo2, kk // 2 + 1))

        C1 = 6.28125
        C2 = float(np.float32(np.float16(2 * math.pi - C1)))
        C3 = float(2 * math.pi - C1 - C2)
        MAGIC = float(1.5 * 2 ** 23)
        PI = 3.1415925

        @block.vector
        def _(dve):
            v = nc.vector
            step = Link(dve, s_dve)

            def col(c, rows=slice(0, 128)):
                return vec[rows, c:c + 1]

            def low(dst, src, high, signal):
                v.tensor_tensor(dst, src, high.bitcast(F32), ALU.subtract).then_inc(signal, 1)

            def rms(name, n):
                dve.wait_ge(s_nmm, N0[name] + 1)
                v.tensor_scalar(rstd[:, 0:n], PS[:, 6, 0:n], 1 / D, EPS, ALU.mult, ALU.add).then_inc(s_var, 1)
                dve.wait_ge(s_std, N0[name] + 1)
                step(v.reciprocal(rstd[:, 0:n], rstd[:, 0:n]))

            def start_sum():
                step(v.memset(ss[:, :], 0.0))

            def add_squares(name, tile, src, n, i=None, per=2):
                v.tensor_tensor(ss[:, 0:n], ss[:, 0:n], src, ALU.add).then_inc(s_ssa, 1)
                dve.wait_ge(s_ssa, val(8 * N0[name] + tile + 1, i, per))

            def swiglu(f):
                n, name, hb = tok[f], f + "_in", HB[f]

                def first(u, i):
                    U, G = U0[name] + u, G0[name] + u
                    dve.wait_ge(s_unit, val(2 * U + 1, i, 8))
                    v.tensor_tensor(gate[:, u % 2, 0:n], PS[:, bank(G), 0:n], rstd[:, 0:n], ALU.mult).then_inc(s_gate, 1)
                    dve.wait_ge(s_unit, val(2 * U + 2, i, 8))
                    v.tensor_tensor(upg[:, u % 2, 0:n], PS[:, bank(G) + 1, 0:n], rstd[:, 0:n], ALU.mult).then_inc(s_free, 1)
                    dve.wait_ge(s_free, val(G + 1, i, 4))
                    step(v.tensor_tensor(upg[:, u % 2, 0:n], upg[:, u % 2, 0:n], gate[:, u % 2, 0:n], ALU.mult))

                def second(u, i):
                    if u >= 2:
                        dve.wait_ge(s_hlo, val(hb + u - 1, i, 4))
                    dve.wait_ge(s_sig, val(hb + u + 1, i, 4))
                    v.tensor_tensor(hidf[:, u % 2, 0:n], upg[:, u % 2, 0:n], sig[:, u % 2, 0:n], ALU.mult).then_inc(s_hid, 1)
                    dve.wait_ge(s_hid, val(hb + u + 1, i, 4))

                def third(u, i):
                    dve.wait_ge(s_hhi, val(hb + u + 1, i, 4))
                    o = slice(u * T, u * T + n) if i is None else bass.ds(i * (4 * T) + u * T, n)
                    low(hid_l[:, o], hidf[:, u % 2, 0:n], hid_h[:, o], s_hlo)

                def body(us, i):
                    for u in us:
                        if u == 0:
                            rms(f, n)
                        first(u, i)
                        if u >= 1:
                            second(u - 1, i)
                        if u >= 2:
                            third(u - 2, i)
                turns(step, FC, 4, 4, body, 2)
                second(FC - 1, None)
                third(FC - 2, None)
                third(FC - 1, None)

            def residual(name, n, w, units, factor, norm, g, split):
                groups, per = 8 // w, 4 if w == 2 else 2

                def add(j, i):
                    U, G = U0[name] + units * (j + 1) - 1, G0[name] + j
                    dve.wait_ge(s_unit, val(2 * (U + 1), i, 2 * per * units))
                    if i is None:
                        x = hv(n, j * w, j * w + w)
                    else:
                        x = h[:, bass.ds(i * per + j, 1), T - n:T]
                    v.scalar_tensor_tensor(x, PS[:, bank(G):bank(G) + w, 0:n], factor, x,
                                           ALU.mult, ALU.add).then_inc(s_free, 1)
                    if g is None:
                        return
                    dve.wait_ge(s_free, val(G + 1, i, per))
                    for q in range(w):
                        m = j * w + q
                        if i is None:
                            v.tensor_scalar(xg[:, j % 2, q, 0:n], hv(n, m)[:, 0, :], col(g + m), None, ALU.mult).then_inc(s_xm, 1)
                        else:
                            v.tensor_scalar(xg[:, j % 2, q, 0:n], h[:, bass.ds(i * per + m, 1), T - n:T].rearrange("p o n -> p (o n)"),
                                            vec[:, bass.ds(i * per + (g + m), 1)], None, ALU.mult).then_inc(s_xm, 1)

                def after_act(j, i):
                    dve.wait_ge(s_sq, val(Q0[norm] + j + 1, i, per))
                    for q in range(w):
                        add_squares(norm, j * w + q, sq[:, j % 2, q, 0:n], n, i)
                    if g is None:
                        return
                    for q in range(w):
                        m = j * w + q
                        dve.wait_ge(s_xh, val(X0[split] + m + 1, i, per))
                        o = slice(m, m + 1) if i is None else bass.ds(i * per + m, 1)
                        low(xl[0][:, o, 0:n].rearrange("p o n -> p (o n)"), xg[:, j % 2, q, 0:n],
                            xh[0][:, o, 0:n].rearrange("p o n -> p (o n)"), s_x)

                def body(js, i):
                    for j in js:
                        add(j, i)
                        if j >= 1:
                            after_act(j - 1, i)
                start_sum()
                turns(step, groups, per, 0, body, 1)
                after_act(groups - 1, None)

            def split_input(name, b, made, n, chunks=range(KC), at0=0):
                for k in chunks:
                    dve.wait_ge(s_xh, X0[name] + k - at0 + 1)
                    low(xl[b][:, k, 0:n], made(k), xh[b][:, k, 0:n], s_x)

            def top_scores(part):
                b, nk = part // 4, META + 128 * (part // 4 + 1)
                x = taken[0][:, b, 0:nk]
                if part % 4 == 0:
                    step(v.tensor_tensor(x, score[:, b, 0:nk], cap[:, b, 0:nk], ALU.min))
                for rnd in range(2):
                    src, dst = taken[rnd][:, b, 0:nk], taken[1 - rnd][:, b, 0:nk]
                    step(v.max(m8[:, :], src))
                    step(v.match_replace(dst, m8[:, :], src, TAKEN))
                if part % 4 == 3:
                    step(v.tensor_scalar(x, x, TAKEN, 1.0, ALU.is_equal, ALU.subtract))
                    step(v.scalar_tensor_tensor(x, x, -NEG, cap[:, b, 0:nk], ALU.mult, ALU.min))

            def head_inverses(which):
                tiles = TILES[which]
                for g in groups(which):
                    c, _r = counts(which, g[1] - 1)
                    n, o = tiles[g[0]]["n"], hinv[g[3] % 2]
                    dve.wait_ge(s_hsum, c)
                    v.tensor_scalar(o[0:g[2], 0:n], PS[0:g[2], 6 + g[3] % 2, 0:n], tiles[g[0]]["inv"], EPS,
                                    ALU.mult, ALU.add).then_inc(s_hvar, 1)
                for g in groups(which):
                    n, o = tiles[g[0]]["n"], hinv[g[3] % 2]
                    dve.wait_ge(s_hroot, g[3] + 1)
                    v.reciprocal(o[0:g[2], 0:n], o[0:g[2], 0:n]).then_inc(s_hinv, 1)
            def head_norms(which, j0, j1):
                tiles = TILES[which]
                for j in range(j0, j1 + 2):
                    if j0 == 3:
                        top_scores(j - j0)
                    if j < j1 and tiles[j]["norm"]:
                        x = tiles[j]
                        r, n = slice(0, x["rows"]), x["n"]
                        c, _r = counts(which, j)
                        dve.wait_ge(s_hb, c)
                        v.scalar_tensor_tensor(x["x"], x["x"], col(x["g"], r), PS[r, 2 * (c % 2):2 * (c % 2) + 2, 0:n],
                                               ALU.mult, ALU.mult).then_inc(s_hsc, 1)
                    if j - 2 >= j0 and tiles[j - 2]["rot"] is not None:
                        x = tiles[j - 2]
                        r, n, m = slice(0, x["rows"]), x["n"], x["m"]
                        c, cr = counts(which, j - 2)
                        dve.wait_ge(s_hrot, cr)
                        b0 = 4 + 2 * (cr % 2)
                        step(v.tensor_tensor(rtt[r, 0:m, 0:n], PS[r, b0:b0 + m, 0:n],
                                             x["sin"].unsqueeze(1).broadcast_to([x["rows"], m, n]), ALU.mult))
                        step(v.tensor_tensor(x["x"], x["x"],
                                             x["cos"].unsqueeze(1).broadcast_to([x["rows"], m, n]), ALU.mult))
                        v.tensor_tensor(x["x"], x["x"], rtt[r, 0:m, 0:n], ALU.add).then_inc(s_hout, 1)
                        dve.wait_ge(s_hout, cr)

            def attention(which):
                jobs, j0 = JOBS[which]
                for j in range(len(jobs) + 5):
                    if j < len(jobs):
                        x, c = jobs[j], j0 + j
                        nk = x["nk"]
                        dve.wait_ge(s_lgm, c + 1)
                        if j >= 2:
                            dve.wait_ge(s_ex, c - 1)
                        step(v.tensor_tensor_reduce(lg[:, c % 2, 0:nk], PS[:, j % 2, 0:nk], x["add"], x["scale"],
                                                    NEG * 100, ALU.add, ALU.max, amx[:, c:c + 1]))
                        v.tensor_scalar(nmx[:, c:c + 1], amx[:, c:c + 1], -1.0, None, ALU.mult).then_inc(s_lg, 1)
                    if 0 <= j - 1 < len(jobs):
                        x, c = jobs[j - 1], j0 + j - 1
                        nk = x["nk"]
                        dve.wait_ge(s_ex, c + 1)
                        step(v.reciprocal(ainv[:, c:c + 1], asum[:, c:c + 1]))
                        if j - 1 >= 3:
                            dve.wait_ge(s_ptm, c - 2)
                        v.tensor_scalar(prn[:, c % 3, 0:nk], pr[:, c % 2, 0:nk], ainv[:, c:c + 1], None,
                                        ALU.mult).then_inc(s_prn, 1)
                    if 0 <= j - 5 < len(jobs):
                        x, c = jobs[j - 5], j0 + j - 5
                        r = slice(64 * (x["head"] % 2), 64 * (x["head"] % 2) + 64)
                        o = slice(128 * x["b"], 128 * x["b"] + 128)
                        dve.wait_ge(s_oh, c + 1)
                        low(xl[1][r, x["head"] // 2, o], PS[r, 4 + c % 2, 0:128], xh[1][r, x["head"] // 2, o], s_ol)

            def drain2(name, u, dst, rows=slice(0, 128), n=T):
                U, G = U0[name] + u, G0[name] + u
                dve.wait_ge(s_unit, 2 * (U + 1))
                v.tensor_copy(dst, PS[rows, bank(G):bank(G) + 2, 0:n]).then_inc(s_free, 1)

            def drain_normed(name, u, dst, n):
                U, G = U0[name] + u, G0[name] + u
                dve.wait_ge(s_unit, 2 * (U + 1))
                v.tensor_tensor(dst, PS[:, bank(G):bank(G) + 2, 0:n],
                                rstd[:, 0:n].unsqueeze(1).broadcast_to([128, 2, n]), ALU.mult).then_inc(s_free, 1)

            step(v.memset(epsc[:, :], 0.0))
            start_sum()
            dve.wait_ge(s_vec, 16)
            for m in range(KC + 1):
                if m in (0, 4):
                    dve.wait_ge(s_h[m // 4], 16)
                if m < KC:
                    if m >= 4:
                        dve.wait_ge(s_x, m - 3)
                    v.tensor_scalar(xg[:, (m // 2) % 2, m % 2, :], h[:, m, :], col(gain["f0"] + m), None, ALU.mult).then_inc(s_xm, 1)
                if m:
                    dve.wait_ge(s_sq, m)
                    add_squares("f0", m - 1, sq[:, (m - 1) % 2, 0, :], T)
                    dve.wait_ge(s_xh, m)
                    low(xl[0][:, m - 1, :], xg[:, ((m - 1) // 2) % 2, (m - 1) % 2, :], xh[0][:, m - 1, :], s_x)
            swiglu("f0")
            residual("f0_dn", T, 1, 2, 0.5, "rk", None, None)

            dve.wait_ge(s_ssa, 8 * N0["rk"] + 8)
            rms("rk", T)
            def shift(c0):
                for c in range(c0, c0 + 4):
                    step.do(v.scalar_tensor_tensor(hn[:, c, :], h[:, c, :], col(norm_col(0, 1) + c), rstd[:, :],
                                                   ALU.mult, ALU.mult))
                step.sync()
                q = slice(c0, c0 + 4)
                step.do(v.tensor_tensor(xx[:, q, 1:T], hn[:, q, 0:T - 1], hn[:, q, 1:T], ALU.subtract))
                step(v.tensor_scalar(xx[:, q, 0:1], hn[:, q, 0:1], -1.0, None, ALU.mult))

            def mix_chunk(c, which):
                v.scalar_tensor_tensor(xmf[:, c, :], xx[:, c, :], col(VEC["rk_mix"] + 8 * which + c), hn[:, c, :],
                                       ALU.mult, ALU.add).then_inc(s_xm, 1)

            def mix(s, which):
                if s:
                    dve.wait_ge(s_x, X0[f"m{s}"])
                for c in range(KC):
                    mix_chunk(c, which)
                if s >= 2:
                    dve.wait_ge(s_unit, 2 * U0[("rk_k", "rk_v", "lora_wa", "lora_g")[s - 2]])
                split_input(f"m{s}", s % 2, lambda k: xmf[:, k, :], T)

            for c0 in (0, 4):
                shift(c0)
                for c in range(c0, c0 + 4):
                    mix_chunk(c, 0)
                for c in range(c0, c0 + 4):
                    dve.wait_ge(s_xh, X0["m0"] + c + 1)
                    low(xl[0][:, c, :], xmf[:, c, :], xh[0][:, c, :], s_x)
            for x in (R_, K_, V_, A_, B_):
                step.do(v.memset(x[:, :, T:TP], 0.0))
            step.sync()
            mix(1, 2)
            for u in range(4):
                drain2("rk_r", u, R_[:, 2 * u:2 * u + 2, 0:T])
            mix(2, 3)
            for u in range(4):
                drain2("rk_k", u, K_[:, 2 * u:2 * u + 2, 0:T])
            mix(3, 1)
            for u in range(4):
                drain2("rk_v", u, V_[:, 2 * u:2 * u + 2, 0:T])
            mix(4, 4)
            U, G = U0["lora_wa"], G0["lora_wa"]
            dve.wait_ge(s_unit, 2 * (U + 1))
            v.tensor_copy(lh[0:64, :], PS[0:64, bank(G), 0:T]).then_inc(s_lhd, 1)
            v.tensor_copy(lh[64:128, :], PS[64:128, bank(G) + 1, 0:T]).then_inc(s_free, 1)
            mix(5, 5)
            dve.wait_ge(s_lhh, 1)
            low(lh_l[:, :], lh[:, :], lh_h[:, :], s_lhl)
            U, G = U0["lora_g"], G0["lora_g"]
            dve.wait_ge(s_unit, 2 * (U + 1))
            v.tensor_copy(gh[:, :, :], PS[0:80, bank(G):bank(G) + 2, 0:T]).then_inc(s_free, 1)
            dve.wait_ge(s_ghh, 1)
            low(gh_l[:, :, :], gh[:, :, :], gh_h[:, :, :], s_ghl)
            step(v.memset(W_[:, :, T:TP], 0.0))
            for m in range(KC):
                G = G0["wa2"] + m
                if m < KC - 1:
                    dve.wait_ge(s_part, m + 1)
                else:
                    dve.wait_ge(s_unit, 2 * (U0["wa2"] + 1))
                v.tensor_scalar(W_[:, m, 0:T], PS[:, bank(G), 0:T], col(VEC["w0"] + m), None, ALU.add).then_inc(s_wa, 1)
                v.tensor_scalar(a_g[:, m, :], PS[:, bank(G) + 1, 0:T], col(VEC["a0"] + m), None, ALU.add).then_inc(s_free, 1)
            for c in range(KC):
                v.tensor_scalar(A_[:, c, 0:T], K_[:, c, 0:T], col(VEC["k_k"] + c), None, ALU.mult).then_inc(s_kk, 1)
            dve.wait_ge(s_wst, 2)
            dve.wait_ge(s_dec, 1)
            v.tensor_tensor_scan(Wc[:, :, :].rearrange("p c t -> p (c t)"), wst[:, :, :].rearrange("p c t -> p (c t)"),
                                 W_[:, :, :].rearrange("p c t -> p (c t)"), 0.0, ALU.mult, ALU.add).then_inc(s_cum, 1)
            dve.wait_ge(s_kkr, 1)
            step(v.tensor_scalar(kden[:, :], kden[:, :], 1e-12, None, ALU.max))
            v.reciprocal(kden[:, :], kden[:, :]).then_inc(s_kki, 1)
            dve.wait_ge(s_dk, 2)
            step.do(v.tensor_copy(wend[:, :, :], Wc[:, :, CH - 1:TP:CH]))
            for c in range(KC):
                step.do(v.tensor_scalar(B_[:, c, 0:T], a_g[:, c, :], 1.0, col(VEC["k_a"] + c), ALU.subtract, ALU.mult))
            step.sync()
            step(v.scalar_tensor_tensor(K_[:, :, 0:T], B_[:, :, 0:T], 1.0, K_[:, :, 0:T], ALU.add, ALU.mult))
            for c in range(KC):
                v.scalar_tensor_tensor(ktmp[:, c, 0:T], R_[:, c, 0:T], col(VEC["r_k"] + c), K_[:, c, 0:T],
                                       ALU.mult, ALU.mult).then_inc(s_rkr, 1)
            for m in range(4):
                dve.wait_ge(s_kkb, m + 1)
                for n in range(2):
                    ins = v.tensor_tensor(A_[:, 2 * m + n, 0:T], A_[:, 2 * m + n, 0:T],
                                          PS[:, (5 + 2 * m + n) % 8, 0:T], ALU.mult)
                    ins.then_inc(s_kkd if n else s_dve, 1)
                step.n += 1
            dve.wait_ge(s_kkd, 4)
            step(v.tensor_tensor(B_[:, :, 0:T], A_[:, :, 0:T], a_g[:, :, :], ALU.mult))
            step(v.tensor_scalar(first[:, :, :], A_[:, :, 0:TP:CH], -1.0, None, ALU.mult))
            step(v.scalar_tensor_tensor(A_[:, :, 1:TP], A_[:, :, 1:TP], -1.0, Wc[:, :, 0:TP - 1], ALU.mult, ALU.mult))
            step(v.tensor_copy(A_[:, :, 0:TP:CH], first[:, :, :]))
            step(v.tensor_tensor(B_[:, :, :], B_[:, :, :], W_[:, :, :], ALU.mult))
            dve.wait_ge(s_rks, 2)
            dve.wait_ge(s_bonm, 1)
            for c in range(KC):
                v.tensor_tensor(bonus[:, c, :], PS[:, c, 0:T], V_[:, c, 0:T], ALU.mult).then_inc(s_bon, 1)
            dve.wait_ge(s_bon, KC)

            dve.wait_ge(s_rkc, 16)

            dve.wait_ge(s_lo, 2 * (U0["g2"] + 1))
            for half in range(2):
                for q in (2 * half, 2 * half + 1):
                    c0 = 2 * q
                    for pp in range(2):
                        for n, dst in enumerate((ktok[pp], vtok[pp])):
                            dve.wait_ge(s_tr, 4 * (c0 + pp) + 3 + n)
                            v.tensor_copy(dst[:, :, :], PS[0:BLK, 4 * pp + 2 + n, 0:384].rearrange("p (b f) -> p b f", b=NB)
                                          ).then_inc(s_tkd, 1)
                    for n in range(20):
                        e, ty = n // 5, n % 5
                        dst = (LT[e][:, :], L_[e][:, :], lak[e][:, :], mrb[:, 4 * (q % 2) + e, :], mrk[e][:, :])[ty]
                        dve.wait_ge(s_gm, 20 * q + n + 1)
                        v.tensor_tensor(blocks(dst), blocks(PS[0:BLK, n % 8, 0:TP]), mask((0, 1, 0, 2, 2)[ty]),
                                        ALU.mult).then_inc(s_gr, 1)
                        if ty == 1:
                            dve.wait_ge(s_gr, 20 * q + n + 1)
                            step(v.tensor_tensor(blocks(XT[e][:, :]), blocks(LT[e][:, :]), mask(4), ALU.mult))
                            v.tensor_tensor(blocks(XT[e][:, :]), blocks(XT[e][:, :]), mask(9), ALU.add).then_inc(s_xi, 1)
                    for lv in range(4):
                        for e in range(4):
                            dve.wait_ge(s_xt, 16 * q + 4 * lv + e + 1)
                            if lv < 3:
                                step.do(v.tensor_tensor(XX[e][:, :], XX[e][:, :], PS[0:BLK, 4 + e, 0:TP], ALU.add))
                            v.tensor_tensor(XT[e][:, :], XT[e][:, :], PS[0:BLK, e, 0:TP], ALU.add).then_inc(s_xd, 1)
                    for pp in range(2):
                        dve.wait_ge(s_yvm, c0 + pp + 1)
                        v.tensor_copy(K_[:, c0 + pp, :], PS[:, 4 + pp, 0:TP]).then_inc(s_yv, 1)
                    for pp in range(2):
                        dve.wait_ge(s_um, c0 + pp + 1)
                        p = 2 * (q % 2) + pp
                        v.tensor_copy(U_[:, :, p * 128:p * 128 + 128],
                                      PS[0:BLK, 6 + pp, 0:384].rearrange("p (b f) -> p b f", b=NB)).then_inc(s_ue, 1)

                q4 = slice(4 * half, 4 * half + 4)
                dve.wait_ge(s_gv, 4 * half + 4)
                dve.wait_ge(s_ue, 4 * half + 4)
                dve.wait_ge(s_yv, 4 * half + 4)
                for ch in range(NCH):
                    b, r = ch // 3, slice(CH * (ch % 3), CH * (ch % 3) + CH)
                    add = GV[:, ch, :]
                    if 0 < ch < NCH - 1:
                        dve.wait_ge(s_s, 16 * half + 2 * ch)
                        step(v.tensor_tensor(St[:, :].rearrange("p (q i) -> p q i", q=4),
                                             S_[ch % 2][:, :].rearrange("p (q i) -> p q i", q=4),
                                             wend[:, q4, ch:ch + 1].broadcast_to([128, 4, 64]), ALU.mult))
                        step(v.tensor_tensor(St[:, :], St[:, :], GV[:, ch, :], ALU.add))
                        add = St[:, :]
                    for m in range(2 if ch else 0):
                        dve.wait_ge(s_sam, 16 * half + 2 * ch - 1 + m)
                        us = U_[r, b, m * 256:m * 256 + 256].rearrange("s (p e i) -> s e p i", e=2, i=64)
                        v.tensor_tensor(us, us, PS[r, 3 * (1 - m):3 * (1 - m) + 2, 0:128].rearrange(
                            "s e (p i) -> s e p i", i=64), ALU.add).then_inc(s_sau, 1)
                    for m in range(2 if ch < NCH - 1 else 0):
                        dve.wait_ge(s_dsm, 16 * half + 2 * ch + 1 + m)
                        part = slice(128 * m, 128 * m + 128)
                        v.tensor_tensor(S_[(ch + 1) % 2][:, part], add[:, part], PS[:, (5, 2)[m], 0:128],
                                        ALU.add).then_inc(s_s, 1)
                    if ch:
                        dve.wait_ge(s_ysm, 8 * half + ch)
                        ks = K_[:, q4, ch * CH:ch * CH + CH]
                        v.tensor_tensor(ks, ks, PS[:, 6 + ch % 2, 0:4 * CH].rearrange("p (q t) -> p q t", q=4),
                                        ALU.add).then_inc(s_yse, 1)
                dve.wait_ge(s_yse, 8 * half + 8)
                for p in range(4):
                    dve.wait_ge(s_ym, 4 * half + p + 1)
                    c = 4 * half + p
                    v.tensor_tensor(K_[:, c, :], K_[:, c, :], PS[:, p % 2, 0:TP], ALU.add).then_inc(s_yc, 1)

            dve.wait_ge(s_yc, KC)
            for c in range(KC):
                dve.wait_ge(s_mum, c + 1)
                v.scalar_tensor_tensor(R_[:, c, 0:T], PS[:, 4 + c % 2, 0:T], -1 / HD, K_[:, c, 0:T],
                                       ALU.mult, ALU.add).then_inc(s_yc2, 1)
            dve.wait_ge(s_vm, 1)
            v.tensor_scalar(kden[:, :], PS[0:16, 6, 0:T], 1 / HD, LN_EPS, ALU.mult, ALU.add).then_inc(s_bv, 1)
            dve.wait_ge(s_bvr, 1)
            v.reciprocal(kden[:, :], kden[:, :]).then_inc(s_gni, 1)
            for m in range(4):
                dve.wait_ge(s_gnb, m + 1)
                for n in range(2):
                    c = 2 * m + n
                    ins = v.scalar_tensor_tensor(R_[:, c, 0:T], R_[:, c, 0:T], col(VEC["lnx_g"] + c),
                                                 PS[:, 2 * m + n, 0:T], ALU.mult, ALU.mult)
                    if n:
                        ins.then_inc(s_gnd, 1)
            dve.wait_ge(s_gnd, 4)
            for c in range(KC):
                step.do(v.scalar_tensor_tensor(R_[:, c, 0:T], R_[:, c, 0:T], col(VEC["lnx_b"] + c), bonus[:, c, :],
                                               ALU.add, ALU.add))
            step.sync()
            for g in range(4):
                G = G0["g2"] + g
                if g < 3:
                    dve.wait_ge(s_part, 7 + g + 1)
                else:
                    dve.wait_ge(s_unit, 2 * (U0["g2"] + 1))
                v.tensor_tensor(V_[:, 2 * g:2 * g + 2, 0:T], PS[:, bank(G):bank(G) + 2, 0:T],
                                R_[:, 2 * g:2 * g + 2, 0:T], ALU.mult).then_inc(s_free, 1)
            dve.wait_ge(s_free, G0["g2"] + 4)
            split_input("ro", 1, lambda k: V_[:, k, 0:T], T)
            residual("rk_o", T, 2, 1, 1.0, "f1", gain["f1"], "f1")
            swiglu("f1")

            residual("f1_dn", T, 1, 2, 0.5, "f2", gain["f2"], "f2")
            swiglu("f2")
            residual("f2_dn", T, 1, 2, 0.5, "at", norm_col(1, 1), "at")
            rms("at", T)
            for name, c0 in (("at_q", 0), ("at_k", 8), ("at_qi", 12), ("at_tail", 16)):
                for u in range(UN[name]):
                    drain_normed(name, u, rawq[:, c0 + 2 * u:c0 + 2 * u + 2, :], T)
            dve.wait_ge(s_rcm, 1)
            step(v.tensor_copy(rcol_a[0:BLK, :, :], PS[0:BLK, 6, 0:12].rearrange("p (j c) -> p j c", c=4)))
            U, G = U0["at_v"], G0["at_v"]
            dve.wait_ge(s_unit, 2 * (U + 1))
            for j in range(NB):
                kn = min(BLK, T - BLK * j)
                ins = v.tensor_scalar(vt[0:kn, j, :], PS[0:kn, bank(G) + j // 2, (j % 2) * 256:(j % 2) * 256 + 256],
                                      rcol_a[0:kn, j, 0:1], None, ALU.mult)
                ins.then_inc(s_free if j == 2 else s_dve, 1)
            step.n += 2
            dve.wait_ge(s_free, G + 1)
            dve.wait_ge(s_dsc, 48)
            head_inverses("at")
            head_norms("at", 0, 3)
            dve.wait_ge(s_wtm, 1)
            v.tensor_scalar(wit[:, :, :], PS[:, 0, 0:16].rearrange("p (b f) -> p b f", b=2),
                            float(8 ** -0.5 * 64 ** -0.5), None, ALU.mult).then_inc(s_wt, 1)
            dve.wait_ge(s_wt, 1)
            for b in range(2):
                nk = META + 128 * (b + 1)
                for hd in range(8):
                    n = b * 8 + hd
                    dve.wait_ge(s_rl, n + 1)
                    if hd == 0:
                        ins = v.tensor_scalar(score[:, b, 0:nk], rel[:, n % 2, 0:nk], wit[:, b, 0:1], None, ALU.mult)
                    else:
                        ins = v.scalar_tensor_tensor(score[:, b, 0:nk], rel[:, n % 2, 0:nk], wit[:, b, hd:hd + 1],
                                                     score[:, b, 0:nk], ALU.mult, ALU.add)
                    ins.then_inc(s_ra, 1)
                    dve.wait_ge(s_ra, n + 1)
            head_norms("at", 3, 9)
            attention("at")
            dve.wait_ge(s_ol, 32)
            residual("at_o", SEQ, 2, 1, 1.0, "f3", gain["f3"], "f3")
            swiglu("f3")

            residual("f3_dn", SEQ, 1, 2, 0.5, "b", VEC["norm_mix"], "b")
            rms("b", SEQ)
            for u in range(2):
                drain_normed("b_qa", u, qka[:, 2 * u:2 * u + 2, :], SEQ)
            dve.wait_ge(s_bc, 96)
            step(v.tensor_copy(posf[:, :], posi[:, :]))
            step(v.tensor_scalar(ang[:, :], posf[:, :], freq[:, 0:1], None, ALU.mult))
            for n, (turn, shift) in enumerate(((0.25, math.pi / 2), (0.0, 0.0))):
                step(v.tensor_scalar(posf[:, :], ang[:, :], 1 / (2 * math.pi), turn, ALU.mult, ALU.add))
                step(v.tensor_scalar(posf[:, :], posf[:, :], MAGIC, None, ALU.add))
                step(v.tensor_scalar(posf[:, :], posf[:, :], MAGIC, None, ALU.subtract))
                step(v.scalar_tensor_tensor(red[:, :], posf[:, :], -C1, ang[:, :], ALU.mult, ALU.add))
                for part in (C2, C3):
                    step(v.scalar_tensor_tensor(red[:, :], posf[:, :], -part, red[:, :], ALU.mult, ALU.add))
                step(v.tensor_scalar(red[:, :], red[:, :], shift, PI, ALU.add, ALU.min))
                v.tensor_scalar(cs_b[:, n, :], red[:, :], -PI, None, ALU.max).then_inc(s_ang, 1)
            for u in range(2):
                drain_normed("b_ka", u, qka[:, 4 + 2 * u:6 + 2 * u, :], SEQ)
            for hd in range(8):
                dve.wait_ge(s_bwm, hd + 1)
                v.tensor_copy(biasw[:, hd, :], PS[:, 4 + hd % 2, 0:384]).then_inc(s_bw, 1)
            dve.wait_ge(s_rcm, 2)
            step(v.tensor_copy(rcol_b[:, :, :], PS[:, 6, 0:8].rearrange("p (j c) -> p j c", c=4)))
            for u in range(2):
                U, G = U0["b_va"] + u, G0["b_va"] + u
                dve.wait_ge(s_unit, 2 * (U + 1))
                for j in range(2):
                    ins = v.tensor_scalar(vat[:, j, u * 256:u * 256 + 256], PS[:, bank(G) + j, 0:256],
                                          rcol_b[:, j, 0:1], None, ALU.mult)
                    ins.then_inc(s_free if j else s_dve, 1)
                step.n += 1
            def latent_in(k):
                g = VEC["cq_g"] + k if k < 6 else VEC["ckv_g"] + k - 6
                v.tensor_scalar(cxf[:, k, :], craw[:, k, :], col(g), None, ALU.mult).then_inc(s_xm, 1)

            def latent_add(k):
                dve.wait_ge(s_csq, k + 1)
                n = 0 if k < 6 else 1
                if k in (0, 6):
                    ins = v.tensor_copy(bt[:, n, :], csq[:, k, :])
                else:
                    ins = v.tensor_tensor(bt[:, n, :], bt[:, n, :], csq[:, k, :], ALU.add)
                ins.then_inc(s_css, 1)
                dve.wait_ge(s_css, k + 1)

            def latent_low(k):
                dve.wait_ge(s_xh, X0["cq"] + k + 1)
                low(xl[1][:, k, 0:SEQ], cxf[:, k, :], xh[1][:, k, 0:SEQ], s_x)

            def latent_root(n, width):
                dve.wait_ge(s_cnm, n + 1)
                v.tensor_scalar(cvr[:, n, :], PS[:, 6 + n, 0:SEQ], 1 / width, EPS, ALU.mult, ALU.add).then_inc(s_cv, 1)
                dve.wait_ge(s_cst, n + 1)
                v.reciprocal(cvr[:, n, :], cvr[:, n, :]).then_inc(s_cinv, 1)
                dve.wait_ge(s_cinv, n + 1)

            for u in range(4):
                name, w = ("b_cq", u) if u < 3 else ("b_ckv", 0)
                drain_normed(name, w, craw[:, 2 * u:2 * u + 2, :], SEQ)
                dve.wait_ge(s_free, G0["b_cq"] + u + 1)
                latent_in(2 * u)
                latent_in(2 * u + 1)
                if u:
                    for k in (2 * u - 2, 2 * u - 1):
                        latent_low(k)
                        latent_add(k)
            latent_low(6)
            latent_low(7)
            U, G = U0["b_tail"], G0["b_tail"]
            dve.wait_ge(s_unit, 2 * (U + 1))
            v.tensor_tensor(krope[64:96, :], PS[64:96, bank(G), 0:SEQ], rstd[64:96, 0:SEQ], ALU.mult).then_inc(s_free, 1)
            latent_add(6)
            latent_add(7)
            dve.wait_ge(s_sin, 2)
            step(v.tensor_scalar(cs_b[:, 1, :], cs_b[:, 1, :], freq[:, 1:2], None, ALU.mult))
            latent_root(0, 768)
            for u in range(4):
                U, G = U0["b_uq"] + u, G0["b_uq"] + u
                dve.wait_ge(s_unit, 2 * (U + 1))
                v.tensor_tensor(qkb[:, 2 * u:2 * u + 2, :], PS[0:96, bank(G):bank(G) + 2, 0:SEQ],
                                cvr[0:96, 0:1, :].broadcast_to([96, 2, SEQ]), ALU.mult).then_inc(s_free, 1)
                if u == 0:
                    latent_root(1, 256)
            for hd in range(8):
                step.do(v.tensor_copy(qkb[64:96, 8 + hd, :], krope[64:96, :]))
            dve.wait_ge(s_rcm, 3)
            step(v.tensor_copy(rcol_c[:, :, :], PS[:, 6, 0:8].rearrange("p (j c) -> p j c", c=4)))
            for g in range(2):
                G = G0["b_ukv"] + g
                dve.wait_ge(s_part, 10 + g + 1)
                pair = qkb[0:64, 8 + 4 * g:12 + 4 * g, :].rearrange("p (a e) t -> p a e t", e=2)
                for e in range(2):
                    r = slice(64 * e, 64 * e + 64)
                    ins = v.tensor_tensor(pair[:, :, e, :], PS[r, bank(G):bank(G) + 2, 0:SEQ],
                                          cvr[r, 1:2, :].broadcast_to([64, 2, SEQ]), ALU.mult)
                    ins.then_inc(s_free if e else s_dve, 1)
                step.n += 1
            U, G = U0["b_ukv"], G0["b_ukv"] + 2
            dve.wait_ge(s_unit, 2 * (U + 1))
            for j in range(2):
                ins = v.tensor_scalar(vbt[:, j, :], PS[:, bank(G) + j, 0:512], rcol_c[:, j, 0:1], None, ALU.mult)
                ins.then_inc(s_free if j else s_dve, 1)
            step.n += 1
            dve.wait_ge(s_free, G + 1)
            head_inverses("b")
            head_norms("b", 0, 12)
            dve.wait_ge(s_hsc, NT0["b"] + 12)
            dve.wait_ge(s_bld, 128)
            attention("b")
            dve.wait_ge(s_ol, 64)
            residual("b_o", SEQ, 2, 1, 1.0, "ff", VEC["norm_ffn"], "ff")

            def ff1(us, i):
                us = list(us)

                def tail(u):
                    dve.wait_ge(s_hf2, val(u + 1, i, 4))
                    o = slice(2 * u * SEQ, 2 * u * SEQ + 2 * SEQ) if i is None else bass.ds(i * (8 * SEQ) + 2 * u * SEQ, 2 * SEQ)
                    low(hid2_l[:, o], hidf2[:, u % 2, :, :].rearrange("p m n -> p (m n)"), hid2_h[:, o], s_hlo2)
                for k, u in enumerate(us):
                    U, G = U0["b_ff1"] + u, G0["b_ff1"] + u
                    dve.wait_ge(s_unit, val(2 * (U + 1), i, 8))
                    if u == 0:
                        rms("ff", SEQ)
                    v.scalar_tensor_tensor(act2[:, u % 2, :, :], PS[:, bank(G):bank(G) + 2, 0:SEQ], 0.0,
                                           rstd[:, 0:SEQ].unsqueeze(1).broadcast_to([128, 2, SEQ]),
                                           ALU.max, ALU.mult).then_inc(s_free, 1)
                    if k:
                        tail(u - 1)
                tail(us[-1])
            ff1(range(4), None)
            with step.loop(3, 0) as i:
                ff1(range(4, 8), i)
            for m in range(KC):
                U, G = U0["b_ff2"] + 2 * m + 1, G0["b_ff2"] + m
                dve.wait_ge(s_unit, 2 * (U + 1))
                v.tensor_tensor(outt[:, m, :], PS[:, bank(G), 0:SEQ], hv(SEQ, m)[:, 0, :], ALU.add).then_inc(s_free, 1)

        @block.scalar
        def _(act):
            a = nc.scalar
            step = Link(act, s_act)
            widths = [w for _n, n, _m, w in STAGES for _ in range(n)]

            def f(out, in_, func, **kw):
                return a.activation(out, in_, func, **kw)

            def hi(U, i=None, k=4, w=None):
                if U >= UNITS:
                    return
                w = widths[U] if w is None else w
                act.wait_ge(s_raw[U % RAW], val(16 * (U // RAW + 1), i, 4 * k))
                for q, part in enumerate(halves(w)):
                    if U >= SPL:
                        act.wait_ge(s_unit, val(2 * (U - SPL) + q + 1, i, 2 * k))
                    f(whi[U % SPL][:, part], raw[U % RAW][:, part], ACT.Copy).then_inc(s_hi, 1)

            def ahead(name, norm=None, n=T):
                for u in range(UN[name]):
                    hi(U0[name] + u + 1)
                    if u == 0 and norm:
                        root(norm, n)

            def last_width(name, u):
                return max(UW[name], widths[U0[name] + UN[name]])

            def root(name, n):
                act.wait_ge(s_var, N0[name] + 1)
                f(rstd[:, 0:n], rstd[:, 0:n], ACT.Sqrt).then_inc(s_std, 1)

            def swiglu_in(fn):
                n, name, hb = tok[fn], fn + "_in", HB[fn]

                def high(u, i):
                    act.wait_ge(s_hid, val(hb + u + 1, i, 4))
                    o = slice(u * T, u * T + n) if i is None else bass.ds(i * (4 * T) + u * T, n)
                    f(hid_h[:, o], hidf[:, u % 2, 0:n], ACT.Copy).then_inc(s_hhi, 1)

                def body(us, i):
                    us = list(us)
                    for u in us:
                        w = last_width(name, u) if u == us[-1] else UW[name]
                        hi(U0[name] + u + 1, i, 4, w)
                        if u == 0:
                            root(fn, n)
                        act.wait_ge(s_gate, val(hb + u + 1, i, 4))
                        f(sig[:, u % 2, 0:n], gate[:, u % 2, 0:n], ACT.Sigmoid).then_inc(s_sig, 1)
                        if u >= 1:
                            high(u - 1, i)
                turns(step, FC, 4, 0, body, 2)
                hi(U0[fn + "_dn"] + 1)
                high(FC - 1, None)

            def residual(name, n, w, units, norm, split):
                per = 4 if w == 2 else 2

                def after_add(j, i):
                    act.wait_ge(s_free, val(G0[name] + j + 1, i, per))
                    x = hv(n, j * w, j * w + w) if i is None else h[:, bass.ds(i * per + j, 1), T - n:T]
                    f(sq[:, j % 2, 0:w, 0:n], x, ACT.Square).then_inc(s_sq, 1)
                    for q in range(w if split else 0):
                        m = j * w + q
                        act.wait_ge(s_xm, val(XM0[split] + m + 1, i, per))
                        o = slice(m, m + 1) if i is None else bass.ds(i * per + m, 1)
                        f(xh[0][:, o, 0:n].rearrange("p o n -> p (o n)"), xg[:, j % 2, q, 0:n], ACT.Copy).then_inc(s_xh, 1)

                def body(js, i):
                    js = list(js)
                    for j in js:
                        for k in range(units):
                            u = units * j + k + 1
                            ww = UW[name]
                            if j == js[-1] and k == units - 1:
                                ww = last_width(name, u)
                            if u > 1 or units == 1:
                                hi(U0[name] + u, i, per * units, ww if i is not None else None)
                            if k == 0 and j >= 1:
                                after_add(j - 1, i)
                turns(step, 8 // w, per, 0, body, 1)
                after_add(8 // w - 1, None)

            def split_input(name, b, made, n, chunks=range(KC)):
                for k in chunks:
                    act.wait_ge(s_xm, XM0[name] + k + 1)
                    f(xh[b][:, k, 0:n], made(k), ACT.Copy).then_inc(s_xh, 1)

            def head_norms(which):
                tiles = TILES[which]
                for g in groups(which):
                    for j in range(g[0], g[1]):
                        x = tiles[j]
                        c, _r = counts(which, j)
                        if c > 2:
                            act.wait_ge(s_hsum, c - 2)
                        f(sqp[c % 2][0:x["rows"], :, 0:x["n"]], x["x"], ACT.Square).then_inc(s_hsq, 1)
                for g in groups(which):
                    n, o = tiles[g[0]]["n"], hinv[g[3] % 2]
                    act.wait_ge(s_hvar, g[3] + 1)
                    f(o[0:g[2], 0:n], o[0:g[2], 0:n], ACT.Sqrt).then_inc(s_hroot, 1)

            def attention(which):
                jobs, j0 = JOBS[which]
                for j in range(len(jobs) + 5):
                    if 0 <= j - 3 < len(jobs):
                        x, c = jobs[j - 3], j0 + j - 3
                        act.wait_ge(s_ptm, c + 1)
                        if j - 3 >= 2:
                            act.wait_ge(s_om, c - 1)
                        nv = len(x["v"])
                        if which == "at":
                            short = x["v"][-1][2]
                            f(pts[0:BLK, c % 2, 0:nv - 1, :], PS[0:BLK, 2 + c % 2, 0:(nv - 1) * 128].rearrange(
                                "p (n q) -> p n q", q=128), ACT.Copy).then_inc(s_act, 1)
                            step.n += 1
                            f(pts[0:short, c % 2, nv - 1, :], PS[0:short, 2 + c % 2, (nv - 1) * 128:nv * 128],
                              ACT.Copy).then_inc(s_pte, 1)
                        else:
                            f(pts[:, c % 2, 0:nv, :], PS[:, 2 + c % 2, 0:nv * 128].rearrange("p (n q) -> p n q", q=128),
                              ACT.Copy).then_inc(s_pte, 1)
                    if j < len(jobs):
                        x, c = jobs[j], j0 + j
                        nk = x["nk"]
                        act.wait_ge(s_lg, c + 1)
                        if j >= 2:
                            act.wait_ge(s_prn, c - 1)
                        f(pr[:, c % 2, 0:nk], lg[:, c % 2, 0:nk], ACT.Exp, bias=nmx[:, c:c + 1],
                          accum_out=asum[:, c:c + 1]).then_inc(s_ex, 1)
                    if 0 <= j - 4 < len(jobs):
                        x, c = jobs[j - 4], j0 + j - 4
                        r = slice(64 * (x["head"] % 2), 64 * (x["head"] % 2) + 64)
                        act.wait_ge(s_om, c + 1)
                        f(xh[1][r, x["head"] // 2, 128 * x["b"]:128 * x["b"] + 128], PS[r, 4 + c % 2, 0:128],
                          ACT.Copy).then_inc(s_oh, 1)

            for dst, name in ((ones, "ones"), (ident, "ident"), (bo64, "bo64"), (sel, "sel")):
                act.dma_start(dst[:, :], t[name]).then_inc(s_const, 16)
            act.dma_start(masks[:, :, :], t["scan"].rearrange("p (k s) -> p k s", s=BLK)).then_inc(s_rkc, 16)
            for m in range(KC):
                if m in (0, 4):
                    act.wait_ge(s_h[m // 4], 16)
                if m >= 2:
                    act.wait_ge(s_ssa, m - 1)
                f(sq[:, m % 2, 0, :], h[:, m, :], ACT.Square).then_inc(s_sq, 1)
                act.wait_ge(s_xm, m + 1)
                f(xh[0][:, m, :], xg[:, (m // 2) % 2, m % 2, :], ACT.Copy).then_inc(s_xh, 1)
                if m == 2:
                    hi(0)
            swiglu_in("f0")
            residual("f0_dn", T, 1, 2, "rk", None)

            root("rk", T)

            def mixed(s):
                if s >= 2:
                    act.wait_ge(s_unit, 2 * U0[("rk_k", "rk_v", "lora_wa", "lora_g")[s - 2]])
                split_input(f"m{s}", s % 2, lambda k: xmf[:, k, :], T)
            mixed(0)
            hi(U0["rk_r"] + 1)
            mixed(1)
            for u in range(1, 4):
                hi(U0["rk_r"] + u + 1)
            hi(U0["rk_k"] + 1)
            mixed(2)
            for u in range(1, 4):
                hi(U0["rk_k"] + u + 1)
            hi(U0["rk_v"] + 1)
            mixed(3)
            for u in range(1, 4):
                hi(U0["rk_v"] + u + 1)
            mixed(4)
            hi(U0["lora_wa"] + 1)
            act.wait_ge(s_lhd, 1)
            step(f(lh[0:64, :], lh[0:64, :], ACT.Tanh))
            act.wait_ge(s_free, G0["lora_wa"] + 1)
            f(lh_h[:, :], lh[:, :], ACT.Copy).then_inc(s_lhh, 1)
            mixed(5)
            hi(U0["lora_g"] + 1)
            act.wait_ge(s_free, G0["lora_g"] + 1)
            step(f(gh[:, :, :], gh[:, :, :], ACT.Sigmoid))
            f(gh_h[:, :, :], gh[:, :, :], ACT.Copy).then_inc(s_ghh, 1)
            hi(U0["wa2"] + 1)
            act.wait_ge(s_wa, KC)
            f(W_[:, :, 0:T], W_[:, :, 0:T], ACT.Sigmoid).then_inc(s_dec, 1)
            act.wait_ge(s_free, G0["wa2"] + KC)
            step(f(a_g[:, :, :], a_g[:, :, :], ACT.Sigmoid))
            act.wait_ge(s_kk, KC)
            f(ktmp[:, :, 0:T], A_[:, :, 0:T], ACT.Square).then_inc(s_kksq, 1)
            act.wait_ge(s_cum, 1)
            f(W_[:, :, :], Wc[:, :, :], ACT.Exp, scale=math.exp(-0.5)).then_inc(s_dk, 1)
            f(Wc[:, :, :], Wc[:, :, :], ACT.Exp, scale=-math.exp(-0.5)).then_inc(s_dk, 1)
            act.wait_ge(s_kkm, 1)
            f(kden[:, :], PS[0:16, 4, 0:T], ACT.Sqrt).then_inc(s_kkr, 1)
            for q in range(4):
                c0 = 2 * q
                for pp in range(2):
                    p = 2 * (q % 2) + pp
                    for n, dst in enumerate((atok[pp][:, :, :], btok[:, :, p * 128:p * 128 + 128])):
                        act.wait_ge(s_tr, 4 * (c0 + pp) + n + 1)
                        f(dst, PS[0:BLK, 4 * pp + n, 0:384].rearrange("p (b f) -> p b f", b=NB), ACT.Copy).then_inc(s_tka, 1)
                for lv in range(4):
                    for e in range(4):
                        act.wait_ge(s_q, 16 * q + 4 * lv + e + 1)
                        f(QQ[e][:, :], PS[0:BLK, e, 0:TP], ACT.Copy).then_inc(s_qc, 1)
                for pp in range(2):
                    act.wait_ge(s_p1, c0 + pp + 1)
                    f(p1[pp][:, :, :], PS[0:BLK, pp, 0:384].rearrange("p (b f) -> p b f", b=NB), ACT.Copy).then_inc(s_p1c, 1)
                for pp in range(2):
                    act.wait_ge(s_ztm, c0 + pp + 1)
                    f(A_[:, c0 + pp, :], PS[:, 2 + pp, 0:TP], ACT.Copy).then_inc(s_zt, 1)
                for pp in range(2):
                    p = 2 * (q % 2) + pp
                    act.wait_ge(s_gvm, c0 + pp + 1)
                    f(GV[:, :, p * 64:p * 64 + 64].rearrange("q (b j) i -> q j b i", j=3),
                      PS[:, 3 * pp:3 * pp + 3, 0:192].rearrange("q j (b i) -> q j b i", i=64),
                      ACT.Copy).then_inc(s_gv, 1)
            for c in range(KC):
                act.wait_ge(s_yc2, c + 1)
                f(A_[:, c, 0:T], R_[:, c, 0:T], ACT.Square).then_inc(s_ysq, 1)
            act.wait_ge(s_bv, 1)
            f(kden[:, :], kden[:, :], ACT.Sqrt).then_inc(s_bvr, 1)
            hi(U0["g2"] + 1)
            for k in range(KC):
                act.wait_ge(s_free, G0["g2"] + k // 2 + 1)
                f(xh[1][:, k, :], V_[:, k, 0:T], ACT.Copy).then_inc(s_xh, 1)
            residual("rk_o", T, 2, 1, "f1", "f1")
            swiglu_in("f1")

            residual("f1_dn", T, 1, 2, "f2", "f2")
            swiglu_in("f2")
            residual("f2_dn", T, 1, 2, "at", "at")
            for dst, name in ((rot_a[:, :], "rot_a"), (cs_a[:, :, :], "cs_a"), (cap[:, :, :], "cap")):
                src = t[name] if name == "rot_a" else t[name].rearrange("p (c n) -> p c n", c=2)
                act.dma_start(dst, src).then_inc(s_dsc, 16)
            ahead("at_q", "at")
            for name in ("at_k", "at_qi", "at_tail", "at_v"):
                ahead(name)
            act.wait_ge(s_free, G0["at_v"] + 1)
            head_norms("at")
            for n in range(16):
                nk = META + 128 * (n // 8 + 1)
                act.wait_ge(s_rlm, n + 1)
                if n >= 2:
                    act.wait_ge(s_ra, n - 1)
                f(rel[:, n % 2, 0:nk], PS[:, 2 + n % 2, 0:nk], ACT.Relu).then_inc(s_rl, 1)
            attention("at")
            residual("at_o", SEQ, 2, 1, "f3", "f3")
            swiglu_in("f3")

            residual("f3_dn", SEQ, 1, 2, "b", "b")
            for dst, name in ((causal, "causal"), (rot_b, "rot_b"), (freq, "freq"), (distt, "dist")):
                act.dma_start(dst[:, :], t[name]).then_inc(s_bc, 16)
            act.dma_start(relb[:, :, :], t["relb"]).then_inc(s_bc, 16)
            act.dma_start(posi[:, :], t["pos"].broadcast_to([128, SEQ])).then_inc(s_bc, 16)
            ahead("b_qa", "b", SEQ)
            ahead("b_ka")
            for n in range(2):
                act.wait_ge(s_ang, n + 1)
                f(cs_b[:, n, :], cs_b[:, n, :], ACT.Sin).then_inc(s_sin, 1)
            ahead("b_va")

            def latent(k):
                if k % 2 == 0:
                    act.wait_ge(s_free, G0["b_cq"] + k // 2 + 1)
                f(csq[:, k, :], craw[:, k, :], ACT.Square).then_inc(s_csq, 1)
                act.wait_ge(s_xm, XM0["cq"] + k + 1)
                f(xh[1][:, k, 0:SEQ], cxf[:, k, :], ACT.Copy).then_inc(s_xh, 1)
            for u, U in enumerate((U0["b_cq"] + 1, U0["b_cq"] + 2, U0["b_ckv"], U0["b_tail"], U0["b_uq"])):
                hi(U)
                if u:
                    latent(2 * u - 2)
                    latent(2 * u - 1)
            for n in range(2):
                act.wait_ge(s_cv, n + 1)
                f(cvr[:, n, :], cvr[:, n, :], ACT.Sqrt).then_inc(s_cst, 1)
                if n == 0:
                    hi(U0["b_uq"] + 1)
            act.wait_ge(s_bw, 8)
            act.dma_start(t["rows"].rearrange("(p w) -> p w", p=128), biasw[:, :, :].rearrange("p h x -> p (h x)")
                          ).then_inc(s_bst, 16)
            for u in range(1, 4):
                hi(U0["b_uq"] + u + 1)
            ahead("b_ukv")
            act.wait_ge(s_bst, 16)
            pitch = 8 * 384 - 1
            skewed = t["rows"][127:127 + 128 * pitch].rearrange("(p w) -> p w", w=pitch)
            for hd in range(8):
                act.dma_start(bias[:, hd, :], skewed[:, hd * 384:hd * 384 + 256]).then_inc(s_bld, 16)
            act.wait_ge(s_free, G0["b_ukv"] + 3)
            head_norms("b")
            attention("b")
            residual("b_o", SEQ, 2, 1, "ff", "ff")

            def ff1(us, i):
                for u in us:
                    hi(U0["b_ff1"] + u + 1, i, 4, 2048)
                    if u == 0:
                        root("ff", SEQ)
                    act.wait_ge(s_free, val(G0["b_ff1"] + u + 1, i, 4))
                    step.do(f(hidf2[:, u % 2, :, :], act2[:, u % 2, :, :], ACT.Square))
                    o = slice(2 * u * SEQ, 2 * u * SEQ + 2 * SEQ) if i is None else bass.ds(i * (8 * SEQ) + 2 * u * SEQ, 2 * SEQ)
                    f(hid2_h[:, o], act2[:, u % 2, :, :].rearrange("p m n -> p (m n)"), ACT.Square).then_inc(s_hf2, 1)
            ff1(range(4), None)
            with step.loop(3, 4) as i:
                ff1(range(4, 8), i)
            for u in range(16):
                hi(U0["b_ff2"] + u + 1)


def tiles(w, cols):
    k, n = w.shape[0] // 128, w.shape[1] // cols
    return np.ascontiguousarray(w.reshape(k, 128, n, cols).transpose(2, 1, 0, 3)).reshape(n, 128, k * cols)


def pairs(w):
    n = w.shape[1] // 256
    x = w.reshape(KC, 128, n, 2, 128).transpose(2, 1, 3, 0, 4)
    return np.ascontiguousarray(x).reshape(n, 128, 2048)


def down_units(w, parts):
    k = w.shape[0] // 128 // parts
    x = w.reshape(parts, k, 128, 8, 128).transpose(3, 0, 2, 1, 4)
    return np.ascontiguousarray(x).reshape(8 * parts, 128, k * 128)


def columns(x):
    return x.reshape(-1, 128).T


def layout(inp):
    f = {k: np.asarray(v) for k, v in inp.items()}
    out = {}
    x = np.concatenate([f["meta"], f["x"][0]], 0)
    out["h0"] = np.ascontiguousarray(x.T.reshape(KC, 128, T).transpose(1, 0, 2))
    for i in range(4):
        w = f["ffn_w_in"][i // 2, i % 2]
        w = w.reshape(D, 2, FC, 128).transpose(0, 2, 1, 3).reshape(D, 2 * FF)
        out[f"w_f{i}_in"] = pairs(w)
        out[f"w_f{i}_dn"] = down_units(f["ffn_w_out"][i // 2, i % 2], 2)
    for name in "rkvo":
        out["w_rk_" + name] = pairs(f["rk_w_" + name][0])
    out["w_lora_wa"] = tiles(np.concatenate([f["rk_w1"][0], f["rk_a1"][0]], 1), 128)
    out["w_lora_g"] = tiles(f["rk_g1"][0], 160)
    out["w_wa2"] = np.concatenate([f["rk_w2"][0], f["rk_a2"][0]], 0)[None]
    g2 = np.zeros((1, 128, 2, D), np.float32)
    g2[0, 0:80] = f["rk_g2"][0].reshape(2, 80, D).transpose(1, 0, 2)
    out["w_g2"] = g2.reshape(1, 128, 2 * D)
    w = f["at_w_in"][0]
    out["w_at_q"] = pairs(w[:, 0:1024])
    k = w[:, 1024:1280].reshape(D, 4, 1, 64)
    out["w_at_k"] = pairs(np.concatenate([k, k], 2).reshape(D, 512))
    out["w_at_v"] = tiles(w[:, 1280:1536], 256)
    out["w_at_qi"] = pairs(w[:, 1536:2048])
    ki, wi = w[:, 2048:2112], w[:, 2112:2120]
    out["w_at_tail"] = pairs(np.concatenate([ki, ki, wi, np.zeros((D, 120), np.float32)], 1))
    out["w_at_o"] = pairs(f["at_w_o"][0])
    w = f["w_in_2"]
    out["w_b_qa"], out["w_b_ka"] = pairs(w[:, 0:512]), pairs(w[:, 512:1024])
    out["w_b_va"], out["w_b_cq"] = tiles(w[:, 1024:1536], 256), pairs(w[:, 1536:2304])
    out["w_b_ckv"] = pairs(w[:, 2304:2560])
    z = np.zeros((D, 64), np.float32)
    out["w_b_tail"] = tiles(np.concatenate([z, w[:, 2560:2592], z[:, 0:32]], 1), 128)
    out["w_b_uq"] = tiles(f["w_uq_2"], 192)
    kv = f["w_ukv_2"].reshape(256, 8, 128)
    out["w_b_ukv"] = tiles(np.concatenate([kv[:, :, 0:64].reshape(256, 512), kv[:, :, 64:].reshape(256, 512)], 1), 1024)
    out["w_b_o"] = pairs(f["w_o_2"])
    out["w_b_ff1"] = pairs(f["w_ff1_2"])
    out["w_b_ff2"] = down_units(f["w_ff2_2"], 2)
    vecs = [f["norm_g"], f["rk_mix"], f["rk_w0"], f["rk_a0"], f["rk_k_k"], f["rk_k_a"], f["rk_r_k"],
            f["rk_lnx_g"], f["rk_lnx_b"], f["norm_mix_g_2"], f["norm_ffn_g_2"], f["cq_norm_g_2"], f["ckv_norm_g_2"]]
    vecs += [np.concatenate([f[n].reshape(-1)] * 2) for n in ("at_q_g", "at_k_g", "qnorm_a_g_2", "knorm_a_g_2")]
    vecs += [np.concatenate([f[n], np.zeros(32, np.float32)]) for n in ("qnorm_b_g_2", "knorm_b_g_2")]
    out["vec"] = np.ascontiguousarray(np.concatenate([columns(x) for x in vecs], 1))
    rb = np.concatenate([f["rel_bias_2"], np.ones((1, 8), np.float32)], 0)
    out["relb"] = np.ascontiguousarray(np.repeat(rb[:, :, None], 128, 2))
    out["pos"] = f["positions_2"].reshape(1, SEQ)
    out.update(shape_constants())
    return {k: np.ascontiguousarray(x) for k, x in out.items()}


def kernel(**inputs):
    import concourse.bacc as bacc
    from concourse.bass_utils import run_bass_kernel_spmd

    nc = bacc.Bacc("TRN2", target_bir_lowering=False, num_devices=1)
    arrays = layout(inputs)
    t = {}
    for name, x in arrays.items():
        t[name] = nc.dram_tensor(name + "_in", x.shape, mybir.dt.from_np(x.dtype), kind="ExternalInput").ap()
    t["out"] = nc.dram_tensor("result", [128, KC, SEQ], F32, kind="ExternalOutput").ap()
    t["rows"] = nc.dram_tensor("bias_rows_scratch", [128 * 8 * 384], F32, kind="Internal").ap()
    build(nc, t)
    r = run_bass_kernel_spmd(nc, [{n + "_in": x for n, x in arrays.items()}], core_ids=[0])
    y = r.results[0]["result"]
    return y.transpose(2, 1, 0).reshape(1, SEQ, D)
```
